# Optimizing a Trainium2 kernel written in Bass

```python
import math
import jax, jax.numpy as jnp
from jax import lax
import numpy as np

D_MODEL = 1024
BATCH = 1
SEQ = 256
DEPTH = 2

CONV_CH = D_MODEL // 2
CONV_WIDTH = 31
DIFF_QK_DIM = 64
DIFF_V_DIM = 2 * DIFF_QK_DIM
DIFF_HEADS = D_MODEL // 256
MOBA_HEAD_DIM = 64
MOBA_HEADS = D_MODEL // 128
MOBA_BLOCK = 256
MOBA_TOPK = 3
MOBA_Q_CHUNK = 32
ATTN_Q_BLOCK = 128
D_FF = 4 * D_MODEL
ROPE_THETA = 10000.0
N_BRANCHES = 3
LN_EPS = 1e-5
NEG = -1e30
DEEPNORM_ALPHA = (2.0 * DEPTH) ** 0.25
DEEPNORM_BETA = (8.0 * DEPTH) ** -0.25

COLS_CONV = 2 * CONV_CH
COLS_DIFF_QK = 2 * DIFF_HEADS * DIFF_QK_DIM
COLS_DIFF_V = DIFF_HEADS * DIFF_V_DIM
COLS_MOBA = MOBA_HEADS * MOBA_HEAD_DIM
COLS_GATE = N_BRANCHES * D_MODEL
IN_COLS = COLS_CONV + 2 * COLS_DIFF_QK + COLS_DIFF_V + 3 * COLS_MOBA + COLS_GATE


def _split_offsets():
    sizes = [COLS_CONV, COLS_DIFF_QK, COLS_DIFF_QK, COLS_DIFF_V, COLS_MOBA, COLS_MOBA, COLS_MOBA]
    offs, acc = [], 0
    for s in sizes:
        acc += s
        offs.append(acc)
    return offs

def layer_norm(x, g, b):
    xf = x.astype(jnp.float32)
    mu = jnp.mean(xf, axis=-1, keepdims=True)
    var = jnp.mean(jnp.square(xf - mu), axis=-1, keepdims=True)
    y = (xf - mu) * lax.rsqrt(var + LN_EPS) * g.astype(jnp.float32) + b.astype(jnp.float32)
    return y.astype(x.dtype)

def rms_norm(x, g):
    xf = x.astype(jnp.float32)
    y = xf * lax.rsqrt(jnp.mean(jnp.square(xf), axis=-1, keepdims=True) + LN_EPS) * g.astype(jnp.float32)
    return y.astype(x.dtype)

def rope_tables(seq, dim):
    pos = jnp.arange(seq, dtype=jnp.float32)
    inv = ROPE_THETA ** (-jnp.arange(0, dim, 2, dtype=jnp.float32) / dim)
    ang = pos[:, None] * inv[None, :]
    ang = jnp.concatenate([ang, ang], axis=-1)
    return jnp.cos(ang), jnp.sin(ang)

def apply_rope(x, cos, sin):
    c = cos[None, :, None, :].astype(x.dtype)
    s = sin[None, :, None, :].astype(x.dtype)
    x1, x2 = jnp.split(x, 2, axis=-1)
    return x * c + jnp.concatenate([-x2, x1], axis=-1) * s

def conv_branch(u, conv_w, conv_b, ln_g, ln_b, w_out):
    a, gt = jnp.split(u, 2, axis=-1)
    h = a * jax.nn.sigmoid(gt)
    h = lax.conv_general_dilated(
        h, conv_w.astype(h.dtype), window_strides=(1,),
        padding=[(CONV_WIDTH - 1, 0)],
        dimension_numbers=("NWC", "WIO", "NWC"),
        feature_group_count=CONV_CH) + conv_b
    h = jax.nn.silu(layer_norm(h, ln_g, ln_b))
    return h @ w_out

def diff_attention(q, k, v, lq1, lk1, lq2, lk2, subln_g, layer_idx, cos, sin, w_out):
    B, S, _ = q.shape
    H, d = DIFF_HEADS, DIFF_QK_DIM
    q = apply_rope(q.reshape(B, S, 2 * H, d), cos, sin)
    k = apply_rope(k.reshape(B, S, 2 * H, d), cos, sin)
    q = q.transpose(0, 2, 1, 3).reshape(B, H, 2, S, d)
    k = k.transpose(0, 2, 1, 3).reshape(B, H, 2, S, d)
    v = v.reshape(B, S, H, DIFF_V_DIM).transpose(0, 2, 1, 3)
    lambda_init = 0.8 - 0.6 * math.exp(-0.3 * layer_idx)
    f32 = jnp.float32
    lam = (jnp.exp(jnp.sum(lq1.astype(f32) * lk1.astype(f32)))
           - jnp.exp(jnp.sum(lq2.astype(f32) * lk2.astype(f32))) + lambda_init)
    scale = d ** -0.5
    nqb = S // ATTN_Q_BLOCK
    qb = q.reshape(B, H, 2, nqb, ATTN_Q_BLOCK, d).transpose(3, 0, 1, 2, 4, 5)
    key_pos = jnp.arange(S)

    def one_block(args):
        qblk, bi = args
        s = jnp.einsum("bhtqd,bhtkd->bhtqk", qblk, k).astype(f32) * scale
        qpos = bi * ATTN_Q_BLOCK + jnp.arange(ATTN_Q_BLOCK)
        s = jnp.where(key_pos[None, :] <= qpos[:, None], s, NEG)
        p = jax.nn.softmax(s, axis=-1)
        a = p[:, :, 0] - lam * p[:, :, 1]
        return jnp.einsum("bhqk,bhkv->bhqv", a.astype(v.dtype), v)

    o = lax.map(one_block, (qb, jnp.arange(nqb)))
    o = o.transpose(1, 0, 3, 2, 4).reshape(B, S, H, DIFF_V_DIM)
    o = rms_norm(o, subln_g) * (1.0 - lambda_init)
    return o.reshape(B, S, H * DIFF_V_DIM) @ w_out

def moba_attention(q, k, v, cos, sin, w_out):
    B, S, _ = q.shape
    H, hd, BL, QC = MOBA_HEADS, MOBA_HEAD_DIM, MOBA_BLOCK, MOBA_Q_CHUNK
    q = apply_rope(q.reshape(B, S, H, hd), cos, sin).transpose(0, 2, 1, 3)
    k = apply_rope(k.reshape(B, S, H, hd), cos, sin).transpose(0, 2, 1, 3)
    v = v.reshape(B, S, H, hd).transpose(0, 2, 1, 3)
    nb = -(-S // BL)
    pad = nb * BL - S
    kb = jnp.pad(k, ((0, 0), (0, 0), (0, pad), (0, 0))).reshape(B, H, nb, BL, hd)
    vb = jnp.pad(v, ((0, 0), (0, 0), (0, pad), (0, 0))).reshape(B, H, nb, BL, hd)
    kmean = jnp.mean(kb, axis=3)
    topk = min(MOBA_TOPK, nb)
    scale = hd ** -0.5
    f32 = jnp.float32
    nch = S // QC
    qc = q.reshape(B, H, nch, QC, hd).transpose(2, 0, 1, 3, 4)
    bidx = jnp.arange(B)[:, None, None, None]
    hidx = jnp.arange(H)[None, :, None, None]
    blk_ids = jnp.arange(nb)

    def one_chunk(args):
        qch, ci = args
        start = ci * QC
        own = start // BL
        qpos = start + jnp.arange(QC)
        gate = jnp.einsum("bhqd,bhnd->bhqn", qch, kmean).astype(f32)
        gate = jnp.where(blk_ids < own, gate, NEG)
        _, idx = lax.top_k(gate, topk)
        valid = idx < own
        k_sel = kb[bidx, hidx, idx]
        v_sel = vb[bidx, hidx, idx]
        s_sel = jnp.einsum("bhqd,bhqnjd->bhqnj", qch, k_sel).astype(f32) * scale
        s_sel = jnp.where(valid[..., None], s_sel, NEG).reshape(B, H, QC, topk * BL)
        k_own = lax.dynamic_index_in_dim(kb, own, axis=2, keepdims=False)
        v_own = lax.dynamic_index_in_dim(vb, own, axis=2, keepdims=False)
        s_own = jnp.einsum("bhqd,bhjd->bhqj", qch, k_own).astype(f32) * scale
        kpos = own * BL + jnp.arange(BL)
        s_own = jnp.where(kpos[None, :] <= qpos[:, None], s_own, NEG)
        p = jax.nn.softmax(jnp.concatenate([s_sel, s_own], axis=-1), axis=-1).astype(v.dtype)
        p_sel = p[..., :topk * BL].reshape(B, H, QC, topk, BL)
        p_own = p[..., topk * BL:]
        return (jnp.einsum("bhqnj,bhqnjd->bhqd", p_sel, v_sel)
                + jnp.einsum("bhqj,bhjd->bhqd", p_own, v_own))

    o = lax.map(one_chunk, (qc, jnp.arange(nch)))
    o = o.transpose(1, 0, 3, 2, 4).reshape(B, S, H * hd)
    return o @ w_out

def first_inputs(seed: int = 0) -> dict:
    key = jax.random.key(seed)
    ks = jax.random.split(key, 26)
    n = jax.random.normal
    L, D = DEPTH, D_MODEL
    beta = DEEPNORM_BETA
    return {
        "x": n(ks[0], (BATCH, SEQ, D), jnp.float32),
        "w_in": n(ks[1], (L, D, IN_COLS), jnp.float32) * D ** -0.5,
        "b_gate": 0.02 * n(ks[2], (L, COLS_GATE), jnp.float32),
        "conv_w": n(ks[3], (L, CONV_WIDTH, 1, CONV_CH), jnp.float32) * CONV_WIDTH ** -0.5,
        "conv_b": 0.02 * n(ks[4], (L, CONV_CH), jnp.float32),
        "conv_ln_g": 1.0 + 0.02 * n(ks[5], (L, CONV_CH), jnp.float32),
        "conv_ln_b": 0.02 * n(ks[6], (L, CONV_CH), jnp.float32),
        "w_conv_out": n(ks[7], (L, CONV_CH, D), jnp.float32) * CONV_CH ** -0.5 * beta,
        "lam_q1": 0.1 * n(ks[8], (L, DIFF_QK_DIM), jnp.float32),
        "lam_k1": 0.1 * n(ks[9], (L, DIFF_QK_DIM), jnp.float32),
        "lam_q2": 0.1 * n(ks[10], (L, DIFF_QK_DIM), jnp.float32),
        "lam_k2": 0.1 * n(ks[11], (L, DIFF_QK_DIM), jnp.float32),
        "diff_subln_g": 1.0 + 0.02 * n(ks[12], (L, DIFF_V_DIM), jnp.float32),
        "w_diff_out": n(ks[13], (L, COLS_DIFF_V, D), jnp.float32) * COLS_DIFF_V ** -0.5 * beta,
        "w_moba_out": n(ks[14], (L, COLS_MOBA, D), jnp.float32) * COLS_MOBA ** -0.5 * beta,
        "w_o": n(ks[15], (L, D, D), jnp.float32) * D ** -0.5 * beta,
        "ln1_g": 1.0 + 0.02 * n(ks[16], (L, D), jnp.float32),
        "ln1_b": 0.02 * n(ks[17], (L, D), jnp.float32),
        "w_ff1": n(ks[18], (L, D, D_FF), jnp.float32) * D ** -0.5 * beta,
        "b_ff1": 0.02 * n(ks[19], (L, D_FF), jnp.float32),
        "w_ff2": n(ks[20], (L, D_FF, D), jnp.float32) * D_FF ** -0.5 * beta,
        "b_ff2": 0.02 * n(ks[21], (L, D), jnp.float32),
        "ln2_g": 1.0 + 0.02 * n(ks[22], (L, D), jnp.float32),
        "ln2_b": 0.02 * n(ks[23], (L, D), jnp.float32),
    }

def first_block(x, w_in, b_gate, conv_w, conv_b, conv_ln_g, conv_ln_b, w_conv_out,
              lam_q1, lam_k1, lam_q2, lam_k2, diff_subln_g, w_diff_out, w_moba_out, w_o,
              ln1_g, ln1_b, w_ff1, b_ff1, w_ff2, b_ff2, ln2_g, ln2_b):
    B, S, D = x.shape
    cos, sin = rope_tables(S, DIFF_QK_DIM)
    offs = _split_offsets()
    for l in range(DEPTH):
        u = x @ w_in[l]
        u_conv, dq, dk, dv, mq, mk, mv, g = jnp.split(u, offs, axis=-1)
        y_a = conv_branch(u_conv, conv_w[l], conv_b[l], conv_ln_g[l], conv_ln_b[l], w_conv_out[l])
        y_b = diff_attention(dq, dk, dv, lam_q1[l], lam_k1[l], lam_q2[l], lam_k2[l],
                             diff_subln_g[l], l, cos, sin, w_diff_out[l])
        y_c = moba_attention(mq, mk, mv, cos, sin, w_moba_out[l])
        gates = jax.nn.sigmoid(g + b_gate[l]).reshape(B, S, N_BRANCHES, D)
        m = gates[:, :, 0] * y_a + gates[:, :, 1] * y_b + gates[:, :, 2] * y_c
        x = layer_norm(DEEPNORM_ALPHA * x + m @ w_o[l], ln1_g[l], ln1_b[l])
        h = jnp.square(jax.nn.relu(x @ w_ff1[l] + b_ff1[l]))
        x = layer_norm(DEEPNORM_ALPHA * x + h @ w_ff2[l] + b_ff2[l], ln2_g[l], ln2_b[l])
    return x


DEPTH_2 = 1

N_HEADS = 8
HEAD_DIM = 64
ATTN_WIDTH = N_HEADS * HEAD_DIM
KV_RANK = 128
IDX_HEADS = 8
IDX_DIM = 64
TOPK_MAX = 256
Q_BLOCK = 128
CHUNK = 128
GMLP_GROUPS = 4
GMLP_GROUP_DIM = 128
GMLP_WIDTH = GMLP_GROUPS * GMLP_GROUP_DIM
NUM_BUCKETS = 32
MAX_DISTANCE = 128
N_GROUPS = 4
EXPERTS_PER_GROUP = 8
N_EXPERTS = N_GROUPS * EXPERTS_PER_GROUP
TOP_K_INNER = 2
D_FF_EXPERT = 256
EPS = 1e-6
IN_SIZES = (ATTN_WIDTH, KV_RANK, IDX_HEADS * IDX_DIM, IDX_DIM, IDX_HEADS, GMLP_WIDTH, GMLP_WIDTH, D_MODEL, D_MODEL)
IN_COLS_2 = ATTN_WIDTH + KV_RANK + IDX_HEADS * IDX_DIM + IDX_DIM + IDX_HEADS + 2 * GMLP_WIDTH + 2 * D_MODEL


def rms_norm_2(x, g):
    xf = x.astype(jnp.float32)
    y = xf * lax.rsqrt(jnp.mean(xf * xf, axis=-1, keepdims=True) + EPS)
    return y.astype(x.dtype) * g

def layer_norm_2(x, g, b):
    xf = x.astype(jnp.float32)
    mu = jnp.mean(xf, axis=-1, keepdims=True)
    var = jnp.mean(jnp.square(xf - mu), axis=-1, keepdims=True)
    return ((xf - mu) * lax.rsqrt(var + EPS)).astype(x.dtype) * g + b

def t5_bucket(n):
    max_exact = NUM_BUCKETS // 2
    nf = jnp.maximum(n, 1).astype(jnp.float32)
    large = max_exact + (jnp.log(nf / max_exact) / np.float32(np.log(MAX_DISTANCE / max_exact)) * (NUM_BUCKETS - max_exact)).astype(jnp.int32)
    large = jnp.minimum(large, NUM_BUCKETS - 1)
    return jnp.where(n < max_exact, n, large)

def sparse_attention(q_lat, q_idx, w_idx, c_kv, k_idx, rel_bias):
    B, T = c_kv.shape[:2]
    nb = T // Q_BLOCK
    topk = min(TOPK_MAX, T // 4)
    scale = HEAD_DIM ** -0.5
    s_pos = jnp.arange(T, dtype=jnp.int32)

    def to_blocks(a):
        return jnp.moveaxis(a.reshape((B, nb, Q_BLOCK) + a.shape[2:]), 1, 0)

    def block(args):
        blk, ql, qi, wi = args
        t_pos = blk * Q_BLOCK + jnp.arange(Q_BLOCK, dtype=jnp.int32)
        rel = jax.nn.relu(jnp.einsum('bqhd,bsd->bqhs', qi, k_idx))
        index = jnp.einsum('bqhs,bqh->bqs', rel, wi)
        causal = s_pos[None, :] <= t_pos[:, None]
        index = jnp.where(causal[None], index, -jnp.inf)
        _, sel = lax.top_k(index, topk)
        c_sel = jax.vmap(lambda c, i: c[i])(c_kv, sel)
        dist = t_pos[None, :, None] - sel
        valid = dist >= 0
        bias = rel_bias[t5_bucket(jnp.maximum(dist, 0))]
        scores = jnp.einsum('bqhr,bqkr->bqhk', ql, c_sel).astype(jnp.float32) * scale
        scores = scores + jnp.transpose(bias, (0, 1, 3, 2)).astype(jnp.float32)
        scores = jnp.where(valid[:, :, None, :], scores, -jnp.inf)
        p = jax.nn.softmax(scores, axis=-1).astype(c_sel.dtype)
        return jnp.einsum('bqhk,bqkr->bqhr', p, c_sel)

    out = lax.map(block, (jnp.arange(nb, dtype=jnp.int32), to_blocks(q_lat), to_blocks(q_idx), to_blocks(w_idx)))
    return jnp.moveaxis(out, 0, 1).reshape(B, T, N_HEADS, KV_RANK)

def chunked_gmlp(u, v, ln_g, ln_b, w_s, b_s):
    B, T = u.shape[:2]
    u = jax.nn.gelu(u)
    v = layer_norm_2(jax.nn.gelu(v), ln_g, ln_b)
    vc = v.reshape(B, T // CHUNK, CHUNK, GMLP_GROUPS, GMLP_GROUP_DIM)
    mask = jnp.tril(jnp.ones((CHUNK, CHUNK), dtype=bool))
    ws = jnp.where(mask[None], w_s, 0.0)
    s = jnp.einsum('gij,bcjge->bcige', ws, vc) + jnp.transpose(b_s)[None, None, :, :, None]
    return u * s.reshape(B, T, GMLP_WIDTH)

def hier_moe(h, rg_w, rg_b, re_w, re_b, w_gate, w_up, w_down):
    N = h.shape[0]
    gp = jax.nn.softmax((h @ rg_w + rg_b).astype(jnp.float32), axis=-1)
    g_w, g_idx = lax.top_k(gp, 1)
    el = (h @ re_w + re_b).reshape(N, N_GROUPS, EXPERTS_PER_GROUP)
    el = jnp.take_along_axis(el, g_idx[:, :, None], axis=1)[:, 0]
    ep = jax.nn.softmax(el.astype(jnp.float32), axis=-1)
    e_w, e_idx = lax.top_k(ep, TOP_K_INNER)
    e_w = g_w * e_w / jnp.sum(e_w, axis=-1, keepdims=True)
    eid = g_idx * EXPERTS_PER_GROUP + e_idx
    comb = jnp.sum(jax.nn.one_hot(eid, N_EXPERTS, dtype=jnp.float32) * e_w[..., None], axis=1).astype(h.dtype)
    y = jnp.zeros_like(h)
    for e in range(N_EXPERTS):
        he = jax.nn.silu(h @ w_gate[e]) * (h @ w_up[e])
        y = y + comb[:, e:e + 1] * (he @ w_down[e])
    return y

def second_inputs(seed: int = 0) -> dict:
    key = jax.random.key(seed)
    ks = jax.random.split(key, 24)

    def nrm(k, shape, s):
        return jax.random.normal(k, shape, jnp.float32) * s

    return {
        "x": nrm(ks[0], (BATCH, SEQ, D_MODEL), 1.0),
        "w_in": nrm(ks[1], (DEPTH_2, D_MODEL, IN_COLS_2), D_MODEL ** -0.5),
        "kv_norm_g": 1.0 + nrm(ks[2], (DEPTH_2, KV_RANK), 0.01),
        "w_uk": nrm(ks[3], (DEPTH_2, KV_RANK, N_HEADS, HEAD_DIM), KV_RANK ** -0.5),
        "w_uv": nrm(ks[4], (DEPTH_2, KV_RANK, N_HEADS, HEAD_DIM), KV_RANK ** -0.5),
        "rel_bias": nrm(ks[5], (NUM_BUCKETS, N_HEADS), 0.5),
        "ln_v_g": 1.0 + nrm(ks[6], (DEPTH_2, GMLP_WIDTH), 0.01),
        "ln_v_b": nrm(ks[7], (DEPTH_2, GMLP_WIDTH), 0.01),
        "w_spatial": nrm(ks[8], (DEPTH_2, GMLP_GROUPS, CHUNK, CHUNK), CHUNK ** -0.5),
        "b_spatial": 1.0 + nrm(ks[9], (DEPTH_2, GMLP_GROUPS, CHUNK), 0.01),
        "w_proj_a": nrm(ks[10], (DEPTH_2, ATTN_WIDTH, D_MODEL), ATTN_WIDTH ** -0.5),
        "w_proj_b": nrm(ks[11], (DEPTH_2, GMLP_WIDTH, D_MODEL), GMLP_WIDTH ** -0.5),
        "w_out": nrm(ks[12], (DEPTH_2, D_MODEL, D_MODEL), D_MODEL ** -0.5),
        "norm1_g": 1.0 + nrm(ks[13], (DEPTH_2, D_MODEL), 0.01),
        "norm2_g": 1.0 + nrm(ks[14], (DEPTH_2, D_MODEL), 0.01),
        "router_group_w": nrm(ks[15], (DEPTH_2, D_MODEL, N_GROUPS), D_MODEL ** -0.5),
        "router_group_b": nrm(ks[16], (DEPTH_2, N_GROUPS), 0.01),
        "router_expert_w": nrm(ks[17], (DEPTH_2, D_MODEL, N_EXPERTS), D_MODEL ** -0.5),
        "router_expert_b": nrm(ks[18], (DEPTH_2, N_EXPERTS), 0.01),
        "w_gate": nrm(ks[19], (DEPTH_2, N_EXPERTS, D_MODEL, D_FF_EXPERT), D_MODEL ** -0.5),
        "w_up": nrm(ks[20], (DEPTH_2, N_EXPERTS, D_MODEL, D_FF_EXPERT), D_MODEL ** -0.5),
        "w_down": nrm(ks[21], (DEPTH_2, N_EXPERTS, D_FF_EXPERT, D_MODEL), D_FF_EXPERT ** -0.5),
        "final_norm_g": 1.0 + nrm(ks[22], (D_MODEL,), 0.01),
    }

def second_block(x, w_in, kv_norm_g, w_uk, w_uv, rel_bias, ln_v_g, ln_v_b, w_spatial, b_spatial, w_proj_a, w_proj_b, w_out, norm1_g, norm2_g, router_group_w, router_group_b, router_expert_w, router_expert_b, w_gate, w_up, w_down, final_norm_g):
    B, T, D = x.shape
    splits = [int(c) for c in np.cumsum(IN_SIZES)[:-1]]
    idx_scale = (IDX_HEADS ** -0.5) * (IDX_DIM ** -0.5)
    for l in range(DEPTH_2):
        h = rms_norm_2(x, norm1_g[l])
        proj = h @ w_in[l]
        q, ckv, qi, ki, wi, u, v, ga, gb = jnp.split(proj, splits, axis=-1)
        q = q.reshape(B, T, N_HEADS, HEAD_DIM)
        c_kv = rms_norm_2(ckv, kv_norm_g[l])
        q_lat = jnp.einsum('bthd,rhd->bthr', q, w_uk[l])
        q_idx = qi.reshape(B, T, IDX_HEADS, IDX_DIM)
        w_idx = wi * idx_scale
        o_lat = sparse_attention(q_lat, q_idx, w_idx, c_kv, ki, rel_bias)
        o_a = jnp.einsum('bthr,rhd->bthd', o_lat, w_uv[l]).reshape(B, T, ATTN_WIDTH)
        y_a = o_a @ w_proj_a[l]
        y_b = chunked_gmlp(u, v, ln_v_g[l], ln_v_b[l], w_spatial[l], b_spatial[l]) @ w_proj_b[l]
        merged = jax.nn.sigmoid(ga) * y_a + jax.nn.sigmoid(gb) * y_b
        x = x + merged @ w_out[l]
        h2 = rms_norm_2(x, norm2_g[l]).reshape(B * T, D)
        y = hier_moe(h2, router_group_w[l], router_group_b[l], router_expert_w[l], router_expert_b[l], w_gate[l], w_up[l], w_down[l])
        x = x + y.reshape(B, T, D)
    return rms_norm_2(x, final_norm_g)


def setup_inputs(seed=0):
    out = dict(first_inputs(seed))
    for name, value in second_inputs(seed + 1).items():
        if name != "x":
            out[name + "_2"] = value
    return out


def reference(
    x, w_in, b_gate, conv_w, conv_b, conv_ln_g, conv_ln_b, w_conv_out, lam_q1, lam_k1, lam_q2,
    lam_k2, diff_subln_g, w_diff_out, w_moba_out, w_o, ln1_g, ln1_b, w_ff1, b_ff1, w_ff2, b_ff2,
    ln2_g, ln2_b, w_in_2, kv_norm_g_2, w_uk_2, w_uv_2, rel_bias_2, ln_v_g_2, ln_v_b_2,
    w_spatial_2, b_spatial_2, w_proj_a_2, w_proj_b_2, w_out_2, norm1_g_2, norm2_g_2,
    router_group_w_2, router_group_b_2, router_expert_w_2, router_expert_b_2, w_gate_2, w_up_2,
    w_down_2, final_norm_g_2,
):
    x = first_block(
        x, w_in, b_gate, conv_w, conv_b, conv_ln_g, conv_ln_b, w_conv_out, lam_q1, lam_k1,
        lam_q2, lam_k2, diff_subln_g, w_diff_out, w_moba_out, w_o, ln1_g, ln1_b, w_ff1, b_ff1,
        w_ff2, b_ff2, ln2_g, ln2_b,
    )
    return second_block(
        x, w_in_2, kv_norm_g_2, w_uk_2, w_uv_2, rel_bias_2, ln_v_g_2, ln_v_b_2, w_spatial_2,
        b_spatial_2, w_proj_a_2, w_proj_b_2, w_out_2, norm1_g_2, norm2_g_2, router_group_w_2,
        router_group_b_2, router_expert_w_2, router_expert_b_2, w_gate_2, w_up_2, w_down_2,
        final_norm_g_2,
    )


_drawn_inputs = setup_inputs


def setup_inputs(seed=0):
    import zlib

    import numpy as np

    out = dict(_drawn_inputs(seed))
    spreads = {}
    factors = {'b_gate': 5.037,
     'conv_b': 4.14,
     'conv_ln_g': 10.295,
     'conv_ln_b': 4.185,
     'lam_q1': 5.681,
     'lam_k1': 2.8,
     'lam_q2': 3.899,
     'lam_k2': 5.542,
     'diff_subln_g': 4.717,
     'b_ff1': 3.237,
     'kv_norm_g_2': 64.0,
     'ln_v_g_2': 162.52,
     'ln_v_b_2': 63.808,
     'b_spatial_2': 143.972,
     'norm1_g_2': 3.248,
     'norm2_g_2': 16.386,
     'router_group_b_2': 20.917,
     'router_expert_b_2': 50.815,
     'final_norm_g_2': 200.0,
     'rel_bias_2': 5.256}
    for name, (base, spread) in spreads.items():
        noise = np.random.default_rng([zlib.crc32(name.encode()), seed]).standard_normal(out[name].shape)
        drawn = base * np.exp(spread * noise) if base else spread * noise
        out[name] = __import__('jax').numpy.asarray(drawn.astype(out[name].dtype))
    for name, factor in factors.items():
        out[name] = (out[name] * factor).astype(out[name].dtype)
    return out
```

```python
import math
from contextlib import ExitStack

import numpy as np

import concourse.bass as bass
from concourse import mybir

F32, F32R, I32 = mybir.dt.float32, mybir.dt.float32r, mybir.dt.int32
ALU, ACT, AX = mybir.AluOpType, mybir.ActivationFunctionType, mybir.AxisListType

P = 128
T = 256
TT = T // P
D = 1024
KC = D // P
BANK = 512
NEG = -1e30

LAYERS = 2
CONV_CH, CONV_W = 512, 31
CC = CONV_CH // P
PAD = CONV_W - 1
D_FF = 4 * D
FFJ = D_FF // 256
ALPHA = (2.0 * LAYERS) ** 0.25
LN_EPS = 1e-5
HD = 64
TASKS = 16

U_QK = (4, 5, 6, 7, 10, 11, 12, 13)
U_V = (8, 9, 14, 15)
U_GATE = 16
U_BR = 28
U_WO = U_BR + KC
U_FF = U_WO + 4
UNITS = U_FF + 2 * FFJ
RAW, SPLIT = 4, 2
RAW_CREDIT, SPLIT_CREDIT = RAW, SPLIT
UCOLS = 2048

C_CB, C_CG, C_CBT, C_GB, C_F1 = 0, 4, 8, 12, 36
C_CW = 68
C_ALL = C_CW + CONV_W * CC


def unit_cols(u):
    return 12 * P if U_BR <= u < U_WO else UCOLS

N_HEADS, KV_RANK, TOPK, EPS = 8, 128, 64, 1e-6
N_EXPERTS = 32
IDX_SCALE = float(8 ** -0.5 * 64 ** -0.5)
GELU_C = math.sqrt(2.0 / math.pi)
O_Q, O_KV, O_QI, O_KI, O_WI, O_U, O_V, O_GA, O_GB = (int(c) for c in np.cumsum((0, 512, 128, 512, 64, 8, 512, 512, 1024)))
G2 = LAYERS * UNITS
W_QI, W_K, W_WI, W_Q, W_V, W_U, W_GA, W_GB, W_PB, W_PA, W_OUT, W_R = 0, 2, 3, 4, 6, 8, 10, 14, 18, 20, 22, 26
LOADS = {W_K: 3, W_R: 2}
W_COLS = {W_WI: KC * 8, W_R: KC * 36}
E0 = G2 + W_R + 1
E_LOOP = (N_EXPERTS - 4) // 4
PROJ_BANKS = ((5, 6), (7, 1))
X_IX, X_QL, X_LNV, X_SP, X_YB, X_S = 4, 6, 9, 11, 12, 12


def raw_inc(u):
    return 48 if U_BR <= u % UNITS < U_WO else 16


def raw_count(u):
    return sum(raw_inc(v) for v in range(u % RAW, u + 1, RAW))


RAW_INCS = [raw_count(UNITS - RAW + s) for s in range(RAW)]
CONSTS, BCASTS = 11 * 16, 6 * 16
POOL_LINKS, ACT_LINKS, DVE_LINKS = 1, 1, 109


def bc(ap, axis, n):
    a = ap.unsqueeze(axis)
    shape = list(a.shape)
    shape[axis] = n
    return a.broadcast_to(shape)


def build(nc, t, out):
    ctx = ExitStack()
    with ctx:
        def sb(name, shape, dt=F32):
            return ctx.enter_context(nc.sbuf_tensor(name, shape, dt))

        def sem(name):
            return ctx.enter_context(nc.semaphore(name))

        raw = sb("raw", [P, RAW, UCOLS])
        w_hi = sb("w_hi", [P, SPLIT, UCOLS], F32R)
        w_lo = sb("w_lo", [P, SPLIT, UCOLS], F32R)
        xT_hi = sb("xT_hi", [P, KC, T], F32R)
        xT_lo = sb("xT_lo", [P, KC, T], F32R)
        br_hi = sb("br_hi", [P, 3, CC, T], F32R)
        br_lo = sb("br_lo", [P, 3, CC, T], F32R)
        h_hi = br_hi[:, 0].rearrange("p (s c) t -> p s c t", s=2)
        h_lo = br_lo[:, 0].rearrange("p (s c) t -> p s c t", s=2)
        x_nat = sb("x_nat", [P, TT, D])
        lnb = sb("lnb", [P, 3, D])
        gT = sb("gT", [P, 24, T])
        cv = sb("cv", [P, CC, T])
        hpad = sb("hpad", [P, CC, PAD + T])
        rope = sb("rope", [P, 3, 512])
        E = sb("E", [P, 2, 2, T])
        pT = sb("pT", [P, 512])
        o_nat = sb("o_nat", [P, TT, 4, P])
        qkT = sb("qkT", [P, 4, 4, T])
        vv = sb("vv", [P, 2, TT, 512])
        mix = rope[:].rearrange("p a b -> p (a b)").rearrange("p (s b t) -> p s b t", s=2, b=3)
        ff_r = E[:].rearrange("p s i t -> p s (i t)")
        ff_s = o_nat[:].rearrange("p s h d -> p s (h d)")
        ident = sb("ident", [P, P])
        ones = sb("ones", [P, P])
        alpha = sb("alpha", [P, 1])
        mask = sb("mask", [P, P])
        rot = sb("rot", [P, 4, TT, HD])
        prm_all = sb("prm_all", [P, LAYERS, C_ALL])
        prm = sb("prm", [P, C_ALL])
        gsub = sb("gsub", [P, LAYERS, P])
        linit = sb("linit", [P, 2, LAYERS])
        lamv = sb("lamv", [P, 4, LAYERS * HD])
        lams = sb("lams", [P, 2, LAYERS])
        nlam = sb("nlam", [P, LAYERS])
        row_cw = E[0:CONV_W * CC].rearrange("p s i t -> p (s i t)")[:, 0:LAYERS * P].rearrange("p (l c) -> p l c", l=LAYERS)
        row_v = pT[0:C_CW, 0:LAYERS * P].rearrange("p (l c) -> p l c", l=LAYERS)
        nm = sb("nm", [P, 2, 2])
        rs = sb("rs", [P, 2, 2])
        rr = sb("rr", [P, 2])
        ss = sb("ss", [P, TT * 4])
        st = sb("st", [P, TT, 2, 6])
        mv = sb("mv", [P, TT, 2])
        nmr = sb("nmr", [P, TT])
        nw = sb("nw", [P, 3, 8])
        junk = sb("junk", [P, P])

        ps = ctx.enter_context(nc.psum_tensor("ps", [P, 8, BANK], F32))
        ACC, PT_B, O_B, TB, UB = 0, 2, 3, 4, 5

        hn = gT[:, 16:24, :].rearrange("p (a c) t -> p a (c t)", a=TT)
        gel_s = gT[:, 16:18, :].rearrange("p c t -> p (c t)")
        gel_x = gT[:, 18:20, :].rearrange("p c t -> p (c t)")
        w_uk = gT[:, 20:22, :].rearrange("p c t -> p (c t)")
        w_uv = gT[:, 22:24, :].rearrange("p c t -> p (c t)")
        w_ukT = lnb[:, 0, 0:512].rearrange("p (c r) -> p c r", c=4)
        q2T, qiT = qkT[:, 0], qkT[:, 1]
        q_latT = qkT[:, 2:4].rearrange("p a c t -> p (a c) t")
        E2 = qkT[:, 0:2].rearrange("p a (b i) t -> p (a b) i t", i=2)
        ug, vg = vv[:, 0], vv[:, 1]
        hflat = hpad[:].rearrange("p c t -> p (c t)")
        ckv = hflat[:, 0:256].rearrange("p (a r) -> p a r", a=TT)
        ckvT = hflat[:, 256:512]
        kiT = hflat[:, 512:768]
        o_lat = hflat[:, 768:1024].rearrange("p (i q) -> p i q", i=2)
        idx = rope[:, 0, :].rearrange("p (a k) -> p a k", a=TT)
        rel = rope[:, 1:3, :].rearrange("p s (i k) -> p s i k", i=2)
        selm = cv[:, 0:2, :]
        bias_t = o_nat[:].rearrange("p s h d -> p s (h d)").rearrange("p s (i k) -> p s i k", i=2)
        ws_nat = lamv[:].rearrange("p a d -> p (a d)").rearrange("p (g j) -> p g j", g=4)
        wsT = rot[:].rearrange("p k a d -> p (k a d)").rearrange("p (g i) -> p g i", g=4)
        kvg = gsub[:, 0, :]
        lnv_g, lnv_b = lnb[:, 2, 0:512], lnb[:, 2, 512:1024]
        he_hi = br_hi[:, 2].rearrange("p (s c) t -> p s c t", s=2)
        he_lo = br_lo[:, 2].rearrange("p (s c) t -> p s c t", s=2)
        comb_b = E[:].rearrange("p s i t -> p (s i) t")
        eg = gT[:, 0:4, :].rearrange("p (s c) t -> p s c t", s=2)
        ec = gT[:, 4:8, :].rearrange("p (s c) t -> p s c t", s=2)
        t5 = o_nat[0:32].rearrange("p s h d -> p (s h d)")[:, 0:512]
        relb = cv[0:32, 0, 0:N_HEADS]
        t5_row = lnb[0:N_HEADS, 2, 0:512]
        nm2, rs2 = sb("nm2", [P, 4, 2]), sb("rs2", [P, 4, 2])
        wi = sb("wi", [P, TT, 8])
        bsT = sb("bsT", [P, 4])
        rb = sb("rb", [P, 36])
        wdesc = sb("wdesc", [P, 8])
        rt = prm_all[:].rearrange("p l (r c) -> p (l r c)", r=3).rearrange("p (r a c) -> p r a c", r=6, a=TT)
        lg = prm[:, 0:TT * 36].rearrange("p (a c) -> p a c", a=TT)
        comb = prm[:, TT * 36:TT * 68].rearrange("p (a c) -> p a c", a=TT)
        combT = lamv[0:32].rearrange("p a d -> p (a d)")[:, 0:T]
        z_dram = nc.dram_tensor("z_dram", (N_HEADS, P, 512), F32, kind="Internal")
        comb_dram = nc.dram_tensor("comb_dram", (N_EXPERTS, T), F32, kind="Internal").ap()

        t5_mm, t5_copied, z_stored, late_in, late2_in, late3_in = [sem(x) for x in ("t5_mm", "t5_copied", "z_stored", "late_in", "late2_in", "late3_in")]
        sq_sum, normed, ev2, bank_d, small_T, small_c = [sem(x) for x in ("sq_sum", "normed", "ev2", "bank_d", "small_T", "small_c")]
        ukT_done, ukT_c, ws_masked, wsT_done, wsT_c = [sem(x) for x in ("ukT_done", "ukT_c", "ws_masked", "wsT_done", "wsT_c")]
        kv_normed, kvT_done, kvT_c, ql_done, ql_c = [sem(x) for x in ("kv_normed", "kvT_done", "kvT_c", "ql_done", "ql_c")]
        ix_done, ix_rel, ix_sum, sel_ready, bm_ready = [sem(x) for x in ("ix_done", "ix_rel", "ix_sum", "sel_ready", "bm_ready")]
        gel_in, gel_poly, gel_th, gel_out, lnv_stat, lnv_hat, lnv_out = [sem(x) for x in (
            "gel_in", "gel_poly", "gel_th", "gel_out", "lnv_stat", "lnv_hat", "lnv_out")]
        sp_done, sp_out, ybT_done, yb_hi, yb_lo = [sem(x) for x in ("sp_done", "sp_out", "ybT_done", "yb_hi", "yb_lo")]
        s2_done, s2_max, s2_exp, s2_prob, t2_done, t2_c, v2_done, v2_c, a2_done, a2_hi, a2_lo = [sem(x) for x in (
            "s2_done", "s2_max", "s2_exp", "s2_prob", "t2_done", "t2_c", "v2_done", "v2_c", "a2_done", "a2_hi", "a2_lo")]
        proj_b, proj_a, pm_hi, pm_lo = [sem(x) for x in ("proj_b", "proj_a", "pm_hi", "pm_lo")]
        rt_log, rt_in, rt_exp, comb_ready, combT_done, combT_c, comb_stored = [sem(x) for x in (
            "rt_log", "rt_in", "rt_exp", "comb_ready", "combT_done", "combT_c", "comb_stored")]
        bias_in = [sem(f"bias_in{q}") for q in range(2)]
        comb_in = [sem(f"comb_in{q}") for q in range(4)]
        th_done, g_out, weighted, he_ready, he_hid, he_lod = [sem(x) for x in (
            "th_done", "g_out", "weighted", "he_ready", "he_hid", "he_lod")]
        dve_link2 = sem("dve_link2")
        pool_link2 = sem("pool_link2")
        raw_in = [sem(f"raw_in{s}") for s in range(RAW)]
        hi_done, split_done, unit_done = sem("hi_done"), sem("split_done"), sem("unit_done")
        evac_a, evac_d = sem("evac_a"), sem("evac_d")
        const_in, bcast_in, x_in, lnb1_in, lnb2_in = sem("const_in"), sem("bcast_in"), sem("x_in"), sem("lnb1_in"), sem("lnb2_in")
        setup_p, rows_T, prm_ready, lam_sum, lam_exp = sem("setup_p"), sem("rows_T"), sem("prm_ready"), sem("lam_sum"), sem("lam_exp")
        xT_done, xT_hid, xT_lod = sem("xT_done"), sem("xT_hid"), sem("xT_lod")
        x_scaled, ln_stat, ln_hat, ln_gain, x_out = sem("x_scaled"), sem("ln_stat"), sem("ln_hat"), sem("ln_gain"), sem("x_out")
        rotated, roped, qk_T, qk_copied = sem("rotated"), sem("roped"), sem("qk_T"), sem("qk_copied")
        prm_cur, conv_link = sem("prm_cur"), sem("conv_link")
        csum_done, c_dev, c_sq, c_norm, c_tanh, c_silu, c_hi, c_lo = [sem(x) for x in (
            "csum_done", "c_dev", "c_sq", "c_norm", "c_tanh", "c_silu", "c_hi", "c_lo")]
        score_done, neg_max, exp_done, prob_done = sem("score_done"), sem("neg_max"), sem("exp_done"), sem("prob_done")
        probT_done, probT_copied, pv_done, pv_copied, moba_lo = [sem(x) for x in (
            "probT_done", "probT_copied", "pv_done", "pv_copied", "moba_lo")]
        o_normed, oT_done, oT_hid, oT_lod = sem("o_normed"), sem("oT_done"), sem("oT_hid"), sem("oT_lod")
        mixed, m_hi, m_lo = sem("mixed"), sem("m_hi"), sem("m_lo")
        ff_sq, ff_hi, ff_lo = sem("ff_sq"), sem("ff_hi"), sem("ff_lo")
        dve_link, act_link, pool_link = sem("dve_link"), sem("act_link"), sem("pool_link")
        stored = sem("stored")

        block = ctx.enter_context(nc.Block())

        def split_counts(g):
            return LAYERS * RAW_INCS[g % RAW] + sum(16 * LOADS.get(v - G2, 1) for v in range(G2 + (g - G2) % RAW, g + 1, RAW))

        def rows(ap, k):
            return ap.rearrange("l (k p) n -> p (l k) n", p=P), k

        w_in, w_in_k = rows(t["w_in"], KC)
        w_br = [rows(t[n], CC)[0] for n in ("w_conv_out", "w_diff_out", "w_moba_out")]
        w_o, w_o_k = rows(t["w_o"], KC)
        w_f1, w_f1_k = rows(t["w_ff1"], KC)
        w_f2, w_f2_k = rows(t["w_ff2"], D_FF // P)

        def unit3(ring, slot, k, n):
            return ring[:, slot, 0:k * n].rearrange("p (k n) -> p k n", k=k)

        def evac_before(u):
            return len([v for v in range(u) if v not in U_QK]), len([v for v in range(u) if v in U_QK])

        EV_A = U_BR - len(U_QK) + FFJ
        EV_D = len(U_QK) + KC
        EV_A_IN = U_BR - len(U_QK)

        def latent_steps(w):
            order = []
            for j in range(4):
                at = []
                for s in (2 * j, 2 * j + 1):
                    at += [("transpose", s)] + ([("values", s - 1)] if s >= 1 else []) + ([("output", s - 2)] if s >= 2 else [])
                order.append(at)
            order.append([("values", 7), ("output", 6), ("output", 7)])
            if w is None:
                return order[4]
            return order[w - X_S - 2] if 0 <= w - X_S - 2 < 4 else []

        def latent_pe(pe, kind, s):
            a, p = s // 4, s % 4
            if kind == "transpose":
                pe.wait_ge(s2_prob, s + 1)
                if s >= 1:
                    pe.wait_ge(t2_c, s)
                for i in range(2):
                    for b in range(a + 1):
                        last = nc.tensor.transpose(ps[:, PT_B, (2 * i + b) * P:(2 * i + b + 1) * P], E2[:, s % 4, i, b * P:(b + 1) * P], ident[:])
                last.then_inc(t2_done, 1)
            elif kind == "values":
                pe.wait_ge(t2_c, s + 1)
                if s >= 1:
                    pe.wait_ge(v2_c, s)
                else:
                    pe.wait_ge(sp_out, TT)
                for i in range(2):
                    for b in range(a + 1):
                        last = nc.tensor.matmul(ps[:, O_B, i * P:(i + 1) * P], ckv[:, b, :], pT[:, (2 * i + b) * P:(2 * i + b + 1) * P], start=b == 0, stop=b == a)
                last.then_inc(v2_done, 1)
            else:
                pe.wait_ge(v2_c, s + 1)
                if s >= 1:
                    pe.wait_ge(a2_lo, s)
                else:
                    pe.wait_ge(yb_lo, 2)
                for i in range(2):
                    last = nc.tensor.matmul(ps[i * HD:(i + 1) * HD, TB, 0:P], w_uv[:, (2 * p + i) * HD:(2 * p + i + 1) * HD], o_lat[:, i, :], start=True, stop=True)
                last.then_inc(a2_done, 1)

        def latent_act(act, kind, s):
            a, p = s // 4, s % 4
            nk = P * (a + 1)
            if kind == "transpose":
                act.wait_ge(t2_done, s + 1)
                if s >= 1:
                    act.wait_ge(v2_done, s)
                nc.scalar.activation(pT[:].rearrange("p (i k) -> p i k", i=2)[:, :, 0:nk],
                                     ps[:, PT_B, :].rearrange("p (i k) -> p i k", i=2)[:, :, 0:nk], ACT.Copy).then_inc(t2_c, 1)
            elif kind == "values":
                act.wait_ge(v2_done, s + 1)
                if s >= 1:
                    act.wait_ge(a2_done, s)
                nc.scalar.activation(o_lat, ps[:, O_B, 0:256].rearrange("p (i q) -> p i q", i=2), ACT.Copy).then_inc(v2_c, 1)
            else:
                act.wait_ge(a2_done, s + 1)
                nc.scalar.activation(br_hi[:, 0, p, a * P:(a + 1) * P], ps[:, TB, 0:P], ACT.Copy).then_inc(a2_hi, 1)

        def latent_dve(dve, kind, s):
            a, p = s // 4, s % 4
            if kind == "output":
                dve.wait_ge(a2_hi, s + 1)
                nc.vector.tensor_tensor(br_lo[:, 0, p, a * P:(a + 1) * P], ps[:, TB, 0:P], br_hi[:, 0, p, a * P:(a + 1) * P].bitcast(F32), ALU.subtract).then_inc(a2_lo, 1)

        @block.sync
        def _(sp):
            sp.dma_start(x_nat[:], t["x"].rearrange("o (a p) d -> p (o a) d", p=P)).then_inc(x_in, 16)

            def load(base, u, dst, src):
                sp.wait_ge(split_done, base + u + 1)
                sp.dma_start(dst, src).then_inc(raw_in[u % RAW], 16)

            with sp.Fori(0, LAYERS) as l:
                base = l * UNITS
                for u in range(U_BR):
                    load(base, u, unit3(raw, u % RAW, KC, 256), w_in[:, bass.ds(l * KC, KC), u * 256:(u + 1) * 256])
                    if u == 12:
                        sp.wait_ge(x_out, l * 2 * TT + 1)
                        sp.wait_ge(z_stored, 16)
                        for i, name in enumerate(("ln1_g", "ln1_b", "b_ff2")):
                            sp.dma_start(lnb[:, i, :], t[name][bass.ds(l, 1), :].rearrange("o d -> (o d)").partition_broadcast(P)).then_inc(lnb1_in, 16)
                for c in range(KC):
                    u = U_BR + c
                    sp.wait_ge(split_done, base + u + 1)
                    for b in range(3):
                        sp.dma_start(unit3(raw, u % RAW, 12, P)[:, b * CC:(b + 1) * CC, :],
                                     w_br[b][:, bass.ds(l * CC, CC), c * P:(c + 1) * P]).then_inc(raw_in[u % RAW], 16)
                for k in range(4):
                    load(base, U_WO + k, unit3(raw, (U_WO + k) % RAW, 2, D), w_o[:, bass.ds(l * KC + 2 * k, 2), :])

                def ff1(u, j):
                    load(base, u, unit3(raw, u % RAW, KC, 256), w_f1[:, bass.ds(l * KC, KC), bass.ds(j * 256, 256)])

                def ff2(u, j):
                    load(base, u, unit3(raw, u % RAW, 2, D), w_f2[:, bass.ds(l * (D_FF // P) + j * 2, 2), :])

                ff1(U_FF, 0)
                ff1(U_FF + 1, 1)
                ff2(U_FF + 2, 0)
                sp.wait_ge(x_out, l * 2 * TT + TT + 1)
                for i, name in enumerate(("ln2_g", "ln2_b")):
                    sp.dma_start(lnb[:, i, :], t[name][bass.ds(l, 1), :].rearrange("o d -> (o d)").partition_broadcast(P)).then_inc(lnb2_in, 16)
                with sp.Fori(0, FFJ // 2 - 1) as i:
                    for q in range(2):
                        u = U_FF + 3 + 2 * q
                        j = i * 2 + (2 + q)
                        sp.wait_ge(split_done, base + i * 4 + (u + 1))
                        sp.dma_start(unit3(raw, u % RAW, KC, 256), w_f1[:, bass.ds(l * KC, KC), bass.ds(j * 256, 256)]).then_inc(raw_in[u % RAW], 16)
                        sp.wait_ge(split_done, base + i * 4 + (u + 2))
                        sp.dma_start(unit3(raw, (u + 1) % RAW, 2, D), w_f2[:, bass.ds(l * (D_FF // P) + i * 4 + 2 * (1 + q), 2), :]).then_inc(raw_in[(u + 1) % RAW], 16)
                ff2(UNITS - 1, FFJ - 1)

            w2 = t["w_in_2"].rearrange("o (k p) n -> p (o k) n", p=P)

            def load2(w, src, k, n, at=0, m=None):
                m = n if m is None else m
                if at == 0:
                    sp.wait_ge(split_done, G2 + w + 1)
                u = G2 + w
                sp.dma_start(unit3(raw, u % RAW, k, n)[:, :, at:at + m], src).then_inc(raw_in[u % RAW], 16)

            for j in range(2):
                load2(W_QI + j, w2[:, :, O_QI + 256 * j:O_QI + 256 * (j + 1)], KC, 256)
            load2(W_K, w2[:, :, O_KV:O_KV + 128], KC, 256, 0, 128)
            load2(W_K, w2[:, :, O_KI:O_KI + 64], KC, 256, 128, 64)
            load2(W_K, w2[:, :, O_KI:O_KI + 64], KC, 256, 192, 64)
            load2(W_WI, w2[:, :, O_WI:O_WI + 8], KC, 8)
            for w0, o, n in ((W_Q, O_Q, 2), (W_V, O_V, 2), (W_U, O_U, 2), (W_GA, O_GA, 4), (W_GB, O_GB, 4)):
                for j in range(n):
                    load2(w0 + j, w2[:, :, o + 256 * j:o + 256 * (j + 1)], KC, 256)
            for w0, name in ((W_PB, "w_proj_b_2"), (W_PA, "w_proj_a_2")):
                for j in range(2):
                    load2(w0 + j, t[name].rearrange("o (k p) n -> p (o k) n", p=P)[:, :, 512 * j:512 * (j + 1)], CC, 512)
            for k in range(4):
                load2(W_OUT + k, t["w_out_2"].rearrange("o (k p) n -> p (o k) n", p=P)[:, 2 * k:2 * k + 2, :], 2, D)
            load2(W_R, t["router_group_w_2"].rearrange("o (k p) n -> p (o k) n", p=P), KC, 36, 0, 4)
            load2(W_R, t["router_expert_w_2"].rearrange("o (k p) n -> p (o k) n", p=P), KC, 36, 4, 32)
            e_in = [t[n].rearrange("o e (k p) n -> p (o e k) n", p=P) for n in ("w_gate_2", "w_up_2", "w_down_2")]

            def load_e(kind, e, u, i=None):
                turn = u + 1 if i is None else i * 12 + (u + 1)
                sp.wait_ge(split_done, turn)
                k, n = (KC, 256) if kind < 2 else (2, D)
                src = e_in[kind][:, e * k:(e + 1) * k, :] if i is None else e_in[kind][:, bass.ds(e * k, k), :]
                sp.dma_start(unit3(raw, u % RAW, k, n), src).then_inc(raw_in[u % RAW], 16)

            def load_step(e, u, i=None):
                load_e(0, e, u, i)
                load_e(1, e, u + 1, i)
                load_e(2, e - 1, u + 2, i)

            load_e(0, 0, E0)
            load_e(1, 0, E0 + 1)
            load_step(1, E0 + 2)
            with sp.Fori(0, E_LOOP) as i:
                for q in range(4):
                    load_step(i * 4 + (2 + q), E0 + 5 + 3 * q, i)
            for e in (N_EXPERTS - 2, N_EXPERTS - 1):
                load_step(e, E0 + 3 * e - 1)
            load_e(2, N_EXPERTS - 1, E0 + 3 * N_EXPERTS - 1)
            for a in range(TT):
                sp.wait_ge(normed, 2 * TT + a + 1)
                sp.dma_start(out.rearrange("o (a p) d -> p (o a) d", p=P)[:, a, :], x_nat[:, a, :]).then_inc(stored, 16)
            sp.wait_ge(stored, 16 * TT)

        @block.gpsimd
        def _(pool):
            links = [0]

            def link(ins, base=0):
                links[0] += 1
                ins.then_inc(pool_link, 1)
                pool.wait_ge(pool_link, base + links[0])

            nc.gpsimd.memset(hpad[:, :, 0:PAD], 0.0).then_inc(setup_p, 1)
            nc.gpsimd.memset(ones[:], 1.0).then_inc(setup_p, 1)
            for i, name in enumerate(("lam_q1", "lam_k1", "lam_q2", "lam_k2")):
                pool.dma_start(lamv[:, i, :], t[name].rearrange("l d -> (l d)").partition_broadcast(P)).then_inc(bcast_in, 16)
            pool.dma_start(gsub[:].rearrange("p l d -> p (l d)"), t["diff_subln_g"].rearrange("l d -> (l d)").partition_broadcast(P)).then_inc(bcast_in, 16)
            pool.dma_start(linit[:].rearrange("p l d -> p (l d)"), t["c_lam"].rearrange("l d -> (l d)").partition_broadcast(P)).then_inc(bcast_in, 16)
            nc.gpsimd.memset(alpha[:], ALPHA).then_inc(setup_p, 1)
            pool.wait_ge(setup_p, 3)
            alphas = bc(alpha[:], 1, TT).broadcast_to([P, TT, D])
            with pool.Fori(0, LAYERS) as l:
                links[0] = 0
                base = l * POOL_LINKS
                pool.wait_ge(xT_done, l * 8 + 4)
                pool.wait_ge(x_in, 16)
                nc.gpsimd.tensor_tensor(x_nat[:], x_nat[:], alphas, ALU.mult).then_inc(x_scaled, 1)
                for n in range(len(U_QK)):
                    pool.wait_ge(rotated, l * 8 + n + 1)
                    nc.gpsimd.tensor_tensor(rope[:, n % 2, :], rope[:, n % 2, :], rope[:, 2, :], ALU.add).then_inc(roped, 1)
                for k in range(2):
                    if k == 0:
                        pool.wait_ge(lnb1_in, l * 48 + 48)
                    else:
                        pool.wait_ge(lnb2_in, l * 32 + 32)
                    for a in range(TT):
                        pool.wait_ge(ln_gain, l * 2 * TT + k * TT + a + 1)
                        nc.gpsimd.tensor_tensor(x_nat[:, a, :], x_nat[:, a, :], lnb[:, 1, :], ALU.add).then_inc(x_out, 1)
                    if k == 0:
                        pool.wait_ge(xT_done, l * 8 + 8)
                        link(nc.gpsimd.tensor_tensor(x_nat[:], x_nat[:], alphas, ALU.mult), base)
                        nc.gpsimd.tensor_tensor(x_nat[:], x_nat[:], bc(lnb[:, 2, :], 1, TT), ALU.add).then_inc(x_scaled, 1)
            assert links[0] == POOL_LINKS

            for i in range(8):
                nc.gpsimd.memset(wdesc[:, i:i + 1], float(8 - i))
            pool.wait_ge(ln_gain, LAYERS * 2 * TT)
            pool.dma_start(lnb[:, 0, :], t["norm1_g_2"].rearrange("o d -> (o d)").partition_broadcast(P)).then_inc(late_in, 16)
            pool.wait_ge(x_out, LAYERS * 2 * TT + 1)
            for dst, name in ((lnb[:, 1, :], "norm2_g_2"), (lnv_g, "ln_v_g_2"), (lnv_b, "ln_v_b_2"), (kvg, "kv_norm_g_2")):
                pool.dma_start(dst, t[name].rearrange("o d -> (o d)").partition_broadcast(P)).then_inc(late2_in, 16)
            pool.dma_start(rb[:, 0:4], t["router_group_b_2"].rearrange("o d -> (o d)").partition_broadcast(P)).then_inc(late2_in, 16)
            pool.dma_start(rb[:, 4:36], t["router_expert_b_2"].rearrange("o d -> (o d)").partition_broadcast(P)).then_inc(late2_in, 16)
            pool.dma_start(ws_nat, t["w_spatial_2"].rearrange("o g i j -> i (o g) j")).then_inc(late2_in, 16)
            pool.dma_start(bsT[:], t["b_spatial_2"].rearrange("o g i -> i (o g)"), allow_slow_non_contiguous=True).then_inc(late2_in, 16)
            pool.wait_ge(xT_done, LAYERS * 8 + 4)
            pool.dma_start(w_uk, t["w_uk_2"].rearrange("o r h d -> (o r) (h d)")).then_inc(late3_in, 16)
            pool.dma_start(w_uv, t["w_uv_2"].rearrange("o r h d -> (o r) (h d)")).then_inc(late3_in, 16)
            pool.wait_ge(late2_in, 8 * 16)
            nc.gpsimd.affine_select(out=ws_nat, in_=ws_nat, compare_op=ALU.is_ge, fill=0.0, base=0,
                                    pattern=[[0, 4], [-1, P]], channel_multiplier=1).then_inc(ws_masked, 1)
            pool.wait_ge(z_stored, 16)

            def bias_load(s):
                a, p = s // 4, s % 4
                if s >= 2:
                    pool.wait_ge(s2_max, s - 1)
                src = bass.AP(z_dram, 2 * p * P * 512 + 255 - a * P, [[511, P], [P * 512, 2], [1, P * (a + 1)]])
                pool.dma_start(bias_t[:, s % 2, :, 0:P * (a + 1)], src).then_inc(bias_in[s % 2], 16)

            bias_load(0)
            for s in range(8):
                if s < 7:
                    bias_load(s + 1)
                nk = P * (s // 4 + 1)
                pool.wait_ge(bias_in[s % 2], 16 * (s // 2 + 1))
                pool.wait_ge(sel_ready, s // 4 + 1)
                b = bias_t[:, s % 2, :, 0:nk]
                nc.gpsimd.tensor_tensor(b, b, bc(selm[:, s // 4, 0:nk], 1, 2), ALU.add).then_inc(bm_ready, 1)
            pool.wait_ge(ql_done, 4)
            pool.dma_start(lnb[:, 0, :], t["final_norm_g_2"].partition_broadcast(P)).then_inc(late_in, 16)
            pool.wait_ge(comb_stored, 16)

            def comb_load(e, q, i=None):
                if i is not None:
                    pool.wait_ge(weighted, i * 4 + (q + 1))
                elif e >= 4:
                    pool.wait_ge(weighted, e - 3)
                src = comb_dram[e:e + 1, :] if i is None else comb_dram[bass.ds(e, 1), :]
                pool.dma_start(comb_b[:, q, :], src.rearrange("o t -> (o t)").partition_broadcast(P)).then_inc(comb_in[q], 16)

            for e in range(4):
                comb_load(e, e)
            with pool.Fori(0, N_EXPERTS // 4 - 1) as i:
                for q in range(4):
                    comb_load(i * 4 + (4 + q), q, i)

        @block.scalar
        def _(act):
            links = [0]

            def link(ins, base=0):
                links[0] += 1
                ins.then_inc(act_link, 1)
                act.wait_ge(act_link, base + links[0])

            for dst, src in ((ident[:], t["c_ident"]), (mask[:], t["c_mask"]),
                             (rot[:], t["c_rot"].rearrange("k (a p) d -> p k a d", p=P)),
                             (row_cw, t["conv_w"].rearrange("l k o (c p) -> (k o c) l p", p=P)),
                             (row_v[C_CB:C_CG], t["conv_b"].rearrange("l (c p) -> c l p", p=P)),
                             (row_v[C_CG:C_CBT], t["conv_ln_g"].rearrange("l (c p) -> c l p", p=P)),
                             (row_v[C_CBT:C_GB], t["conv_ln_b"].rearrange("l (c p) -> c l p", p=P)),
                             (row_v[C_GB:C_F1], t["b_gate"].rearrange("l (c p) -> c l p", p=P)),
                             (row_v[C_F1:C_CW], t["b_ff1"].rearrange("l (c p) -> c l p", p=P)),
                             (t5, t["c_t5"]), (relb, t["rel_bias_2"])):
                act.dma_start(dst, src).then_inc(const_in, 16)

            def hi(base, u, n=UCOLS, i=None):
                turn = (base + u) if i is None else (base + i + u)
                act.wait_ge(unit_done, turn + 1)
                nc.scalar.activation(w_hi[:, u % SPLIT, 0:n], raw[:, u % RAW, 0:n], ACT.Copy).then_inc(hi_done, 1)

            act.wait_ge(t5_mm, 1)
            nc.scalar.activation(t5_row, ps[0:N_HEADS, 6, :], ACT.Copy).then_inc(t5_copied, 1)
            act.wait_ge(t5_copied, 1)
            act.dma_start(z_dram.ap(), bc(t5_row, 1, P)).then_inc(z_stored, 16)
            act.wait_ge(rows_T, 1)
            rows_v = ps[:, 7, :].rearrange("p (l c) -> p l c", l=LAYERS)
            for a, b, scale in ((C_CB, C_CG, 1.0), (C_CG, C_F1, 0.5), (C_F1, C_ALL, 1.0)):
                last = nc.scalar.activation(prm_all[:, :, a:b], rows_v[:, :, a:b], ACT.Copy, scale=scale)
            last.then_inc(prm_ready, 1)
            act.wait_ge(lam_sum, 1)
            nc.scalar.activation(lams[:], lams[:], ACT.Exp).then_inc(lam_exp, 1)
            for u in range(2):
                act.wait_ge(raw_in[u], 16)
                hi(0, u)
            act.wait_ge(prm_ready, 1)

            with act.Fori(0, LAYERS) as l:
                links[0] = 0
                base, lbase = l * UNITS, l * ACT_LINKS
                ev = [0]

                def arrived(u, n=16):
                    act.wait_ge(raw_in[u % RAW], l * RAW_INCS[u % RAW] + raw_count(u))

                def split_hi(u):
                    arrived(u)
                    hi(base, u, unit_cols(u))

                def make_xT(k):
                    for b in range(4):
                        act.wait_ge(xT_done, l * 8 + k * 4 + b + 1)
                        nc.scalar.activation(xT_hi[:, 2 * b:2 * b + 2, :], ps[:, ACC + b, :].rearrange("p (c t) -> p c t", c=2), ACT.Copy).then_inc(xT_hid, 1)

                def ln_hat_rows(k):
                    act.wait_ge(ln_stat, l * 2 + k + 1)
                    for a in range(TT):
                        nc.scalar.activation(x_nat[:, a, :], x_nat[:, a, :], ACT.Identity, scale=nw[:, 1, a:a + 1], bias=nmr[:, a:a + 1]).then_inc(ln_hat, 1)

                act.wait_ge(x_out, l * 2 * TT + 1)
                nc.scalar.activation(prm[:], prm_all[:, bass.ds(l, 1), :].rearrange("p o c -> p (o c)"), ACT.Copy).then_inc(prm_cur, 1)
                make_xT(0)
                act.wait_ge(prm_cur, l + 1)
                for u in range(U_BR):
                    split_hi(u + 2)
                    bank = ps[:, UB + u % 3, :]
                    two = bank.rearrange("p (c t) -> p c t", c=2)
                    if u not in U_QK:
                        act.wait_ge(unit_done, base + u + 1 + SPLIT_CREDIT)
                    if u < 2:
                        nc.scalar.activation(cv[:, 2 * u:2 * u + 2, :], two, ACT.Copy, scale=0.5).then_inc(evac_a, 1)
                    elif u < 4:
                        nc.scalar.activation(hpad[:, 2 * u - 4:2 * u - 2, PAD:], two, ACT.Tanh, scale=0.5).then_inc(evac_a, 1)
                    elif u in U_V:
                        n = U_V.index(u)
                        nc.scalar.activation(vv[:, n // 2, :, 256 * (n % 2):256 * (n % 2) + 256], two, ACT.Copy).then_inc(evac_a, 1)
                    elif u >= U_GATE:
                        for c in range(2):
                            g = 2 * (u - U_GATE) + c
                            last = nc.scalar.activation(gT[:, g, :], two[:, c, :], ACT.Tanh, scale=0.5, bias=prm[:, C_GB + g:C_GB + g + 1])
                        last.then_inc(evac_a, 1)
                    if u - 2 in U_QK:
                        n = U_QK.index(u - 2)
                        act.wait_ge(qk_T, l * 8 + n + 1)
                        nc.scalar.activation(qkT[:, n // 2, 2 * (n % 2):2 * (n % 2) + 2, :], ps[:, TB, :].rearrange("p (c t) -> p c t", c=2), ACT.Copy).then_inc(qk_copied, 1)
                    s = u - 10
                    if 0 <= s < TASKS:
                        act.wait_ge(neg_max, l * TASKS + s + 1)
                        if s >= 2:
                            act.wait_ge(probT_done, l * TASKS + s - 1)
                        nk = P * (s % 2 + 1)
                        for i in range(2):
                            last = nc.scalar.activation(E[:, s % 2, i, 0:nk], ps[:, i, 0:nk], ACT.Exp,
                                                        bias=nm[:, s % 2, i:i + 1], accum_out=rs[:, s % 2, i:i + 1])
                        last.then_inc(exp_done, 1)
                    s = u - 12
                    if 0 <= s < TASKS:
                        act.wait_ge(probT_done, l * TASKS + s + 1)
                        if s >= 1:
                            act.wait_ge(pv_done, l * TASKS + s)
                        nk = P * (s % 2 + 1)
                        if s < 8:
                            nc.scalar.activation(pT[:, 0:nk], ps[:, PT_B, 0:nk], ACT.Copy).then_inc(probT_copied, 1)
                        else:
                            nc.scalar.activation(pT[:].rearrange("p (i k) -> p i k", i=2)[:, :, 0:nk],
                                                 ps[:, PT_B, :].rearrange("p (i k) -> p i k", i=2)[:, :, 0:nk], ACT.Copy).then_inc(probT_copied, 1)
                    for s in (u - 13,) + ((TASKS - 1,) if u == U_BR - 1 else ()):
                        if not 0 <= s < TASKS:
                            continue
                        a, h = s % 2, (s % 8) // 2
                        act.wait_ge(pv_done, l * TASKS + s + 1)
                        o = ps[:, O_B, 0:P]
                        if s < 8:
                            nc.scalar.activation(o_nat[:, a, h, :], o, ACT.Copy)
                            nc.scalar.activation(junk[:], o, ACT.Square, accum_out=ss[:, a * 4 + h:a * 4 + h + 1]).then_inc(pv_copied, 1)
                        else:
                            nc.scalar.activation(br_hi[:, 2, h, a * P:(a + 1) * P], o, ACT.Copy).then_inc(pv_copied, 1)
                    if u == 20:
                        act.wait_ge(c_dev, l + 1)
                        nc.scalar.activation(hpad[:, :, PAD:], cv[:], ACT.Square).then_inc(c_sq, 1)
                    if u == 23:
                        act.wait_ge(c_norm, l + 1)
                        for c in range(CC):
                            last = nc.scalar.activation(cv[:, c, :], cv[:, c, :], ACT.Identity, scale=prm[:, C_CG + c:C_CG + c + 1], bias=prm[:, C_CBT + c:C_CBT + c + 1])
                        link(last, lbase)
                        nc.scalar.activation(hpad[:, :, PAD:], cv[:], ACT.Tanh).then_inc(c_tanh, 1)
                    if u == 24:
                        act.wait_ge(c_silu, l + 1)
                        nc.scalar.activation(br_hi[:, 0], cv[:], ACT.Copy).then_inc(c_hi, 1)
                    if u in (25, 26):
                        r = u - 25
                        act.wait_ge(oT_done, l * 2 + r + 1)
                        nc.scalar.activation(br_hi[:, 1, 2 * r:2 * r + 2, :], ps[:, TB, :].rearrange("p (c t) -> p c t", c=2), ACT.Copy).then_inc(oT_hid, 1)
                for c in range(KC):
                    split_hi(U_BR + c + 2)
                    act.wait_ge(mixed, l * KC + c + 1)
                    nc.scalar.activation(xT_hi[:, c, :], mix[:, c % 2, 0, :], ACT.Copy, scale=0.5).then_inc(m_hi, 1)
                for k in range(3):
                    split_hi(U_WO + k + 2)
                ln_hat_rows(0)
                split_hi(U_FF + 1)
                make_xT(1)

                def relu(u, j, i=0, j0=0):
                    act.wait_ge(unit_done, base + i * 4 + (u + 1 + SPLIT_CREDIT))
                    for c in range(2):
                        b = prm[:, C_F1 + 2 * j + c:C_F1 + 2 * j + c + 1] if isinstance(j, int) else prm[:, bass.ds(j * 2 + (C_F1 + c), 1)]
                        last = nc.scalar.activation(ff_r[:, j0, c * T:(c + 1) * T], ps[:, 4 + j0, c * T:(c + 1) * T], ACT.Relu, bias=b)
                    last.then_inc(evac_a, 1)

                def square_hi(j, j0):
                    act.wait_ge(ff_sq, l * FFJ + j + 1)
                    nc.scalar.activation(h_hi[:, j0], ff_s[:, j0, :].rearrange("p (c t) -> p c t", c=2), ACT.Copy).then_inc(ff_hi, 1)

                relu(U_FF, 0, 0, 0)
                split_hi(U_FF + 2)
                square_hi(0, 0)
                relu(U_FF + 1, 1, 0, 1)
                split_hi(U_FF + 3)
                square_hi(1, 1)
                split_hi(U_FF + 4)
                with act.Fori(0, FFJ // 2 - 1) as i:
                    for q in range(2):
                        u = U_FF + 3 + 2 * q
                        j = i * 2 + (2 + q)
                        relu(u, j, i, q)
                        for v in (u + 2, u + 3):
                            act.wait_ge(raw_in[v % RAW], l * RAW_INCS[v % RAW] + i * 16 + raw_count(v))
                            hi(base, v, UCOLS, i * 4)
                            if v == u + 2:
                                square_hi(j, q)
                split_hi(UNITS + 1)
                ln_hat_rows(1)
            assert links[0] == ACT_LINKS

            def hi2(u, n=UCOLS, i=None):
                if i is None:
                    act.wait_ge(raw_in[u % RAW], split_counts(u))
                else:
                    act.wait_ge(raw_in[u % RAW], i * 48 + split_counts(u))
                hi(0, u, n, None if i is None else i * 12)

            def square_sums(src, k):
                for a in range(TT):
                    last = nc.scalar.activation(hn[:, a, :], src[:, a, :], ACT.Square, accum_out=ss[:, a:a + 1])
                last.then_inc(sq_sum, 1)

            def make_xT2(k):
                for b in range(4):
                    act.wait_ge(xT_done, LAYERS * 8 + k * 4 + b + 1)
                    nc.scalar.activation(xT_hi[:, 2 * b:2 * b + 2, :], ps[:, ACC + b, :].rearrange("p (c t) -> p c t", c=2), ACT.Copy).then_inc(xT_hid, 1)

            act.wait_ge(x_out, LAYERS * 2 * TT + 1)
            square_sums(x_nat, 0)
            make_xT2(0)
            for w in range(W_PB):
                hi2(G2 + w + 2, W_COLS.get(w + 2, UCOLS))
                bank = ps[:, UB + w % 3, :]
                two = bank.rearrange("p (c t) -> p c t", c=2)
                act.wait_ge(unit_done, G2 + w + 1 + SPLIT_CREDIT)
                if w == W_K:
                    nc.scalar.activation(kiT, bank[:, 256:512], ACT.Copy)
                    for a in range(TT):
                        nc.scalar.activation(pT[:, a * P:(a + 1) * P], bank[:, a * P:(a + 1) * P], ACT.Square, accum_out=ss[:, 4 + a:5 + a])
                    nc.scalar.activation(ckv, bank[:, 0:256].rearrange("p (a r) -> p a r", a=TT), ACT.Copy).then_inc(ev2, 1)
                elif w == W_WI:
                    nc.scalar.activation(wi[:], bank[:, 0:16].rearrange("p (a h) -> p a h", a=TT), ACT.Copy, scale=IDX_SCALE).then_inc(ev2, 1)
                elif w < W_Q:
                    nc.scalar.activation(qiT[:, 2 * (w - W_QI):2 * (w - W_QI) + 2, :], two, ACT.Copy).then_inc(ev2, 1)
                elif w < W_V:
                    nc.scalar.activation(q2T[:, 2 * (w - W_Q):2 * (w - W_Q) + 2, :], two, ACT.Copy).then_inc(ev2, 1)
                elif w < W_GA:
                    n = w - W_V
                    if n >= 1:
                        act.wait_ge(gel_out, n)
                    nc.scalar.activation(gel_s, bank, ACT.Square)
                    nc.scalar.activation(gel_x, bank, ACT.Copy, scale=0.5).then_inc(ev2, 1)
                    act.wait_ge(gel_poly, n + 1)
                    nc.scalar.activation(gel_s, gel_s, ACT.Tanh, scale=2.0 * GELU_C).then_inc(gel_th, 1)
                else:
                    g = 2 * (w - W_GA)
                    nc.scalar.activation(gT[:, g:g + 2, :], two, ACT.Tanh, scale=0.5).then_inc(ev2, 1)
                if w == 0:
                    act.wait_ge(ukT_done, 1)
                    nc.scalar.activation(w_ukT, ps[:, TB, :].rearrange("p (c r) -> p c r", c=4), ACT.Copy).then_inc(ukT_c, 1)
                    act.wait_ge(wsT_done, 1)
                    nc.scalar.activation(wsT, ps[:, O_B, :].rearrange("p (g i) -> p g i", g=4), ACT.Copy).then_inc(wsT_c, 1)
                if w == W_WI + 1:
                    act.wait_ge(kvT_done, 1)
                    nc.scalar.activation(ckvT, ps[:, TB, 0:T], ACT.Copy).then_inc(kvT_c, 1)
                n = w - X_IX
                if 0 <= n < 8:
                    nk = P * (n // 4 + 1)
                    act.wait_ge(ix_done, n + 1)
                    if n >= 2:
                        act.wait_ge(ix_sum, n - 1)
                    nc.scalar.activation(rel[:, n % 2, :, 0:nk], ps[:, 0:2, 0:nk], ACT.Relu).then_inc(ix_rel, 1)
                n = w - X_QL
                if 0 <= n < 4:
                    act.wait_ge(ql_done, n + 1)
                    nc.scalar.activation(q_latT[:, 2 * n:2 * n + 2, :], ps[:, O_B:O_B + 2, 0:T], ACT.Copy, scale=HD ** -0.5).then_inc(ql_c, 1)
                if w == X_LNV:
                    act.wait_ge(lnv_stat, 1)
                    for a in range(TT):
                        last = nc.scalar.activation(vg[:, a, :], vg[:, a, :], ACT.Identity, scale=nw[:, 1, a:a + 1], bias=nmr[:, a:a + 1])
                    last.then_inc(lnv_hat, 1)
                if w in (X_YB, X_YB + 1):
                    r = w - X_YB
                    act.wait_ge(ybT_done, r + 1)
                    nc.scalar.activation(br_hi[:, 1, 2 * r:2 * r + 2, :], ps[:, TB, :].rearrange("p (c t) -> p c t", c=2), ACT.Copy).then_inc(yb_hi, 1)
                for kind, s in latent_steps(w):
                    latent_act(act, kind, s)
                if X_S <= w < X_S + 4:
                    for s in (2 * (w - X_S), 2 * (w - X_S) + 1):
                        act.wait_ge(s2_max, s + 1)
                        nk = P * (s // 4 + 1)
                        for i in range(2):
                            last = nc.scalar.activation(E2[:, s % 4, i, 0:nk], E2[:, s % 4, i, 0:nk], ACT.Exp, bias=nm2[:, s % 4, i:i + 1], accum_out=rs2[:, s % 4, i:i + 1])
                        last.then_inc(s2_exp, 1)
            for kind, s in latent_steps(None):
                latent_act(act, kind, s)
            for w in range(W_PB, W_OUT):
                hi2(G2 + w + 2, W_COLS.get(w + 2, UCOLS))
                if w >= W_PA:
                    j = w - W_PA
                    act.wait_ge(proj_a, j + 1)
                    nc.scalar.activation(xT_hi[:, 4 * j:4 * j + 4, :], gT[:, 4 * j:4 * j + 4, :], ACT.Copy, scale=0.5).then_inc(pm_hi, 1)
            for w in range(W_OUT, W_OUT + 3):
                hi2(G2 + w + 2, W_COLS.get(w + 2, UCOLS))
            act.wait_ge(x_out, LAYERS * 2 * TT + 2)
            square_sums(x_nat, 1)
            hi2(G2 + W_OUT + 5)
            make_xT2(1)
            hi2(G2 + W_R + 2)
            act.wait_ge(rt_in, 1)
            nc.scalar.activation(rt[:, 0, :, 0:4], rt[:, 0, :, 0:4], ACT.Exp).then_inc(rt_exp, 1)
            act.wait_ge(rt_in, 2)
            nc.scalar.activation(rt[:, 2, :, 0:8], rt[:, 2, :, 0:8], ACT.Exp).then_inc(rt_exp, 1)

            def gate_tanh(e, q, u, i=None):
                act.wait_ge(unit_done, u + 1 + SPLIT_CREDIT if i is None else i * 12 + (u + 1 + SPLIT_CREDIT))
                nc.scalar.activation(eg[:, q], ps[:, 4 + 2 * q, :].rearrange("p (c t) -> p c t", c=2), ACT.Tanh, scale=0.5).then_inc(th_done, 1)

            def hidden_hi(e, q):
                act.wait_ge(he_ready, e + 1)
                nc.scalar.activation(he_hi[:, q], ec[:, q], ACT.Copy).then_inc(he_hid, 1)

            def expert(e, q, u, i=None):
                gate_tanh(e, q, u, i)
                hi2(u + 2, UCOLS, i)
                hi2(u + 3, UCOLS, i)
                hidden_hi(e, q)
                if i is not None or u + 4 < E0 + 3 * N_EXPERTS:
                    hi2(u + 4, UCOLS, i)

            gate_tanh(0, 0, E0)
            hi2(E0 + 2)
            act.wait_ge(combT_done, 1)
            nc.scalar.activation(combT, ps[0:32, 7, 0:T], ACT.Copy, scale=0.5).then_inc(combT_c, 1)
            act.wait_ge(combT_c, 1)
            act.dma_start(comb_dram, combT).then_inc(comb_stored, 16)
            hi2(E0 + 3)
            hidden_hi(0, 0)
            expert(1, 1, E0 + 2)
            with act.Fori(0, E_LOOP) as i:
                for q in range(4):
                    expert(i * 4 + (2 + q), q % 2, E0 + 5 + 3 * q, i)
            for e in (N_EXPERTS - 2, N_EXPERTS - 1):
                expert(e, e % 2, E0 + 3 * e - 1)
            act.wait_ge(x_out, LAYERS * 2 * TT + 3)
            square_sums(x_nat, 2)

        @block.vector
        def _(dve):
            links = [0]

            def link(ins, base=0):
                links[0] += 1
                ins.then_inc(dve_link, 1)
                dve.wait_ge(dve_link, base + links[0])

            def rsqrt(v, y, z, base):
                link(nc.vector.tensor_scalar(y.bitcast(I32), v.bitcast(I32), -0.5, float(0x5F3759DF), ALU.mult, ALU.add), base)
                for _ in range(3):
                    link(nc.vector.tensor_tensor(z, y, y, ALU.mult), base)
                    link(nc.vector.scalar_tensor_tensor(out=z, in0=z, scalar=-0.5, in1=v, op0=ALU.mult, op1=ALU.mult), base)
                    link(nc.vector.scalar_tensor_tensor(out=y, in0=z, scalar=1.5, in1=y, op0=ALU.add, op1=ALU.mult), base)

            def split(base, u, n=UCOLS, i=None):
                turn = (base + u) if i is None else (base + i + u)
                dve.wait_ge(hi_done, turn + 1)
                nc.vector.tensor_tensor(w_lo[:, u % SPLIT, 0:n], raw[:, u % RAW, 0:n], w_hi[:, u % SPLIT, 0:n].bitcast(F32), ALU.subtract).then_inc(split_done, 1)

            dve.sem_inc(split_done, RAW_CREDIT)
            dve.wait_ge(setup_p, 2)
            dve.wait_ge(const_in, CONSTS)
            dve.wait_ge(bcast_in, BCASTS)
            pairs = lamv[:].rearrange("p (a b) d -> p b a d", b=2)
            link(nc.vector.tensor_tensor(pairs[:, 0], pairs[:, 0], pairs[:, 1], ALU.mult))
            nc.vector.tensor_reduce(lams[:], pairs[:, 0].rearrange("p a (l d) -> p a l d", l=LAYERS), AX.X, ALU.add).then_inc(lam_sum, 1)
            for i in range(LAYERS):
                nc.vector.tensor_scalar(gsub[:, i, :], gsub[:, i, :], linit[:, 1, i:i + 1], None, ALU.mult)
            dve.wait_ge(lam_exp, 1)
            link(nc.vector.tensor_tensor(nlam[:], lams[:, 1, :], lams[:, 0, :], ALU.subtract))
            link(nc.vector.tensor_tensor(nlam[:], nlam[:], linit[:, 0, :], ALU.subtract))
            first_links = links[0]
            for u in range(2):
                split(0, u)

            with dve.Fori(0, LAYERS) as l:
                links[0] = first_links
                base, lbase = l * UNITS, l * DVE_LINKS
                conv = [(k, c) for k in range(CONV_W) for c in range(CC)]

                def make_xT(k):
                    for b in range(4):
                        dve.wait_ge(xT_hid, l * 8 + k * 4 + b + 1)
                        nc.vector.tensor_tensor(xT_lo[:, 2 * b:2 * b + 2, :], ps[:, ACC + b, :].rearrange("p (c t) -> p c t", c=2),
                                                xT_hi[:, 2 * b:2 * b + 2, :].bitcast(F32), ALU.subtract).then_inc(xT_lod, 1)

                def ln_stats(k, u):
                    dve.wait_ge(x_scaled, l * 2 + k + 1)
                    dve.wait_ge(unit_done, base + u + 1 + SPLIT_CREDIT)
                    for a in range(TT):
                        for h in range(2):
                            cols = slice(h * BANK, (h + 1) * BANK)
                            last = nc.vector.tensor_tensor(x_nat[:, a, cols], x_nat[:, a, cols], ps[:, ACC + 2 * a + h, :], ALU.add)
                    link(last, lbase)
                    for a in range(TT):
                        for h in range(2):
                            last = nc.vector.bn_stats(st[:, a, h, :], x_nat[:, a, h * BANK:(h + 1) * BANK])
                    link(last, lbase)
                    nc.vector.memset(nw[:, 2, 0:1], 0.0)
                    for a in range(TT):
                        last = nc.vector.bn_aggr(mv[:, a, :], st[:, a].rearrange("p h s -> p (h s)"))
                    link(last, lbase)
                    link(nc.vector.tensor_scalar(nw[:, 0, 0:TT], mv[:, :, 1], LN_EPS, None, ALU.add), lbase)
                    rsqrt(nw[:, 0, 0:TT], nw[:, 1, 0:TT], nw[:, 2, 0:TT], lbase)
                    nc.vector.scalar_tensor_tensor(out=nmr[:], in0=mv[:, :, 0], scalar=-1.0, in1=nw[:, 1, 0:TT], op0=ALU.mult, op1=ALU.mult).then_inc(ln_stat, 1)

                def ln_gains(k):
                    if k == 0:
                        dve.wait_ge(lnb1_in, l * 48 + 48)
                    else:
                        dve.wait_ge(lnb2_in, l * 32 + 32)
                    for a in range(TT):
                        dve.wait_ge(ln_hat, l * 2 * TT + k * TT + a + 1)
                        nc.vector.tensor_tensor(x_nat[:, a, :], x_nat[:, a, :], lnb[:, 0, :], ALU.mult).then_inc(ln_gain, 1)

                make_xT(0)
                dve.wait_ge(prm_cur, l + 1)
                for u in range(U_BR):
                    split(base, u + 2, unit_cols(u + 2))
                    s = u - 11
                    if 0 <= s < TASKS:
                        nk = P * (s % 2 + 1)
                        e = E[:, s % 2, :, 0:nk]
                        dve.wait_ge(exp_done, l * TASKS + s + 1)
                        link(nc.vector.reciprocal(rr[:], rs[:, s % 2, :]), lbase)
                        if s < 8:
                            link(nc.vector.tensor_tensor(rr[:, 1:2], rr[:, 1:2], nlam[:, bass.ds(l, 1)], ALU.mult), lbase)
                            link(nc.vector.tensor_scalar(e[:, 1], e[:, 1], rr[:, 1:2], None, ALU.mult), lbase)
                            nc.vector.scalar_tensor_tensor(out=e[:, 0], in0=e[:, 0], scalar=rr[:, 0:1], in1=e[:, 1], op0=ALU.mult, op1=ALU.add).then_inc(prob_done, 1)
                        else:
                            nc.vector.tensor_tensor(e, e, bc(rr[:], 2, nk), ALU.mult).then_inc(prob_done, 1)
                    s = u - 10
                    if 0 <= s < TASKS:
                        dve.wait_ge(score_done, l * TASKS + s + 1)
                        nk = P * (s % 2 + 1)
                        diag = ps[:, 0:2, nk - P:nk]
                        link(nc.vector.tensor_tensor(diag, diag, bc(mask[:], 1, 2), ALU.add), lbase)
                        nc.vector.tensor_reduce(nm[:, s % 2, :], ps[:, 0:2, 0:nk], AX.X, ALU.max, negate=True).then_inc(neg_max, 1)
                    if u in (2, 3):
                        dve.wait_ge(evac_a, l * EV_A + u + 1)
                        cs = slice(2 * u - 4, 2 * u - 2)
                        link(nc.vector.scalar_tensor_tensor(out=hpad[:, cs, PAD:], in0=hpad[:, cs, PAD:], scalar=1.0, in1=cv[:, cs, :], op0=ALU.add, op1=ALU.mult), lbase)
                    if u in U_QK:
                        n = U_QK.index(u)
                        q = 0 if n // 2 in (0, 2) else 2
                        x = ps[:, UB + u % 3, :].rearrange("p (a h d) -> p a h d", a=TT, d=HD)
                        r1 = rope[:, n % 2, :].rearrange("p (a h d) -> p a h d", a=TT, d=HD)
                        r2 = rope[:, 2, :].rearrange("p (a h d) -> p a h d", a=TT, d=HD)
                        dve.wait_ge(unit_done, base + u + 1 + SPLIT_CREDIT)
                        if n >= 2:
                            dve.wait_ge(qk_T, l * 8 + n - 1)
                        if n >= 1:
                            dve.wait_ge(roped, l * 8 + n)
                        half = HD // 2
                        for a in range(TT):
                            nc.vector.tensor_tensor(r1[:, a], x[:, a], bc(rot[:, q, a, :], 1, 4), ALU.mult)
                            nc.vector.tensor_tensor(r2[:, a, :, 0:half], x[:, a, :, half:HD], bc(rot[:, q + 1, a, 0:half], 1, 4), ALU.mult)
                            last = nc.vector.tensor_tensor(r2[:, a, :, half:HD], x[:, a, :, 0:half], bc(rot[:, q + 1, a, half:HD], 1, 4), ALU.mult)
                        last.then_inc(rotated, 1)
                    for n in range(8 * (u - 4), 8 * (u - 3)):
                        if 0 <= n < len(conv):
                            k, c = conv[n]
                            w = prm[:, C_CW + n:C_CW + n + 1]
                            if k == 0:
                                nc.vector.tensor_scalar(cv[:, c, :], hpad[:, c, 0:T], w, prm[:, C_CB + c:C_CB + c + 1], ALU.mult, ALU.add).then_inc(conv_link, 1)
                            else:
                                dve.wait_ge(conv_link, l * len(conv) + n - CC + 1)
                                nc.vector.scalar_tensor_tensor(out=cv[:, c, :], in0=hpad[:, c, k:k + T], scalar=w, in1=cv[:, c, :], op0=ALU.mult, op1=ALU.add).then_inc(conv_link, 1)
                    for s in (u - 13,) + ((TASKS - 1,) if u == U_BR - 1 else ()):
                        if 8 <= s < TASKS:
                            a, h = s % 2, (s % 8) // 2
                            dve.wait_ge(pv_copied, l * TASKS + s + 1)
                            nc.vector.tensor_tensor(br_lo[:, 2, h, a * P:(a + 1) * P], ps[:, O_B, 0:P],
                                                    br_hi[:, 2, h, a * P:(a + 1) * P].bitcast(F32), ALU.subtract).then_inc(moba_lo, 1)
                    if u == 20:
                        dve.wait_ge(csum_done, l * 2 + 1)
                        nc.vector.scalar_tensor_tensor(out=cv[:], in0=bc(ps[:, TB, 0:T], 1, CC), scalar=-1.0 / CONV_CH, in1=cv[:], op0=ALU.mult, op1=ALU.add).then_inc(c_dev, 1)
                    if u == 22:
                        dve.wait_ge(csum_done, l * 2 + 2)
                        v, y, z = (rope[:, 0, 0:T], rope[:, 1, 0:T], rope[:, 2, 0:T])
                        link(nc.vector.tensor_scalar(v, ps[:, TB, T:2 * T], 1.0 / CONV_CH, LN_EPS, ALU.mult, ALU.add), lbase)
                        rsqrt(v, y, z, lbase)
                        nc.vector.tensor_tensor(cv[:], cv[:], bc(y, 1, CC), ALU.mult).then_inc(c_norm, 1)
                    if u == 24:
                        dve.wait_ge(c_tanh, l + 1)
                        nc.vector.scalar_tensor_tensor(out=cv[:], in0=hpad[:, :, PAD:], scalar=1.0, in1=cv[:], op0=ALU.add, op1=ALU.mult).then_inc(c_silu, 1)
                    if u == 25:
                        dve.wait_ge(c_hi, l + 1)
                        nc.vector.tensor_tensor(br_lo[:, 0], cv[:], br_hi[:, 0].bitcast(F32), ALU.subtract).then_inc(c_lo, 1)
                    if u == 23:
                        dve.wait_ge(pv_copied, l * TASKS + 8)
                        link(nc.vector.tensor_scalar(nw[:, 0, :], ss[:], 1.0 / P, LN_EPS, ALU.mult, ALU.add), lbase)
                        rsqrt(nw[:, 0, :], nw[:, 1, :], nw[:, 2, :], lbase)
                        heads = o_nat[:].rearrange("p a h d -> p (a h) d")
                        link(nc.vector.tensor_tensor(heads, heads, bc(nw[:, 1, :], 2, P), ALU.mult), lbase)
                        nc.vector.tensor_tensor(heads, heads, bc(gsub[:, bass.ds(l, 1), :].rearrange("p o d -> p (o d)"), 1, 8), ALU.mult).then_inc(o_normed, 1)
                    if u in (25, 26):
                        r = u - 25
                        dve.wait_ge(oT_hid, l * 2 + r + 1)
                        nc.vector.tensor_tensor(br_lo[:, 1, 2 * r:2 * r + 2, :], ps[:, TB, :].rearrange("p (c t) -> p c t", c=2),
                                                br_hi[:, 1, 2 * r:2 * r + 2, :].bitcast(F32), ALU.subtract).then_inc(oT_lod, 1)

                def mixed_lo(c):
                    dve.wait_ge(m_hi, l * KC + c + 1)
                    nc.vector.scalar_tensor_tensor(out=xT_lo[:, c, :], in0=mix[:, c % 2, 0, :], scalar=0.5, in1=xT_hi[:, c, :].bitcast(F32), op0=ALU.mult, op1=ALU.subtract).then_inc(m_lo, 1)

                for c in range(KC):
                    u = U_BR + c
                    split(base, u + 2, unit_cols(u + 2))
                    dve.wait_ge(unit_done, base + u + 1 + SPLIT_CREDIT)
                    if c >= 2:
                        dve.wait_ge(m_lo, l * KC + c - 1)
                    m = mix[:, c % 2]
                    b0 = 4 + 2 * (c % 2)
                    ys = (ps[:, b0, 0:T], ps[:, b0, T:2 * T], ps[:, b0 + 1, 0:T])
                    for b in range(3):
                        last = nc.vector.scalar_tensor_tensor(out=m[:, b, :], in0=gT[:, b * KC + c, :], scalar=1.0, in1=ys[b], op0=ALU.add, op1=ALU.mult)
                    last.then_inc(evac_d, 1)
                    dve.wait_ge(evac_d, l * KC + c + 1)
                    link(nc.vector.tensor_tensor(m[:, 0, :], m[:, 0, :], m[:, 1, :], ALU.add), lbase)
                    nc.vector.tensor_tensor(m[:, 0, :], m[:, 0, :], m[:, 2, :], ALU.add).then_inc(mixed, 1)
                    if c >= 1:
                        mixed_lo(c - 1)
                mixed_lo(KC - 1)
                for k in range(3):
                    split(base, U_WO + k + 2, UCOLS)
                ln_stats(0, U_WO + 3)
                split(base, U_FF + 1)
                ln_gains(0)
                make_xT(1)

                def square(j, j0):
                    if not isinstance(j, int):
                        dve.wait_ge(ff_lo, l * FFJ + j - 1)
                    dve.wait_ge(evac_a, l * EV_A + EV_A_IN + j + 1)
                    nc.vector.tensor_tensor(ff_s[:, j0, :], ff_r[:, j0, :], ff_r[:, j0, :], ALU.mult).then_inc(ff_sq, 1)

                def square_lo(j, j0):
                    dve.wait_ge(ff_hi, l * FFJ + j + 1)
                    nc.vector.tensor_tensor(h_lo[:, j0], ff_s[:, j0, :].rearrange("p (c t) -> p c t", c=2), h_hi[:, j0].bitcast(F32), ALU.subtract).then_inc(ff_lo, 1)

                for j in range(2):
                    square(j, j)
                    split(base, U_FF + 2 + j)
                    square_lo(j, j)
                split(base, U_FF + 4)
                with dve.Fori(0, FFJ // 2 - 1) as i:
                    for q in range(2):
                        u = U_FF + 3 + 2 * q
                        j = i * 2 + (2 + q)
                        square(j, q)
                        split(base, u + 2, UCOLS, i * 4)
                        square_lo(j, q)
                        split(base, u + 3, UCOLS, i * 4)
                ln_stats(1, UNITS - 1)
                split(base, UNITS + 1)
                ln_gains(1)
            assert links[0] == first_links + DVE_LINKS, links[0] - first_links

            n2 = [0]

            def then(ins):
                n2[0] += 1
                ins.then_inc(dve_link2, 1)
                dve.wait_ge(dve_link2, n2[0])

            def rsqrt2(v, y, z):
                then(nc.vector.tensor_scalar(y.bitcast(I32), v.bitcast(I32), -0.5, float(0x5F3759DF), ALU.mult, ALU.add))
                for _ in range(3):
                    then(nc.vector.tensor_tensor(z, y, y, ALU.mult))
                    then(nc.vector.scalar_tensor_tensor(out=z, in0=z, scalar=-0.5, in1=v, op0=ALU.mult, op1=ALU.mult))
                    then(nc.vector.scalar_tensor_tensor(out=y, in0=z, scalar=1.5, in1=y, op0=ALU.add, op1=ALU.mult))

            def split2(u, n=UCOLS, i=None):
                split(0, u, n, None if i is None else i * 12)

            def rms_rows(k, dst, gain):
                dve.wait_ge(sq_sum, k + 1)
                then(nc.vector.tensor_scalar(nw[:, 0, 0:TT], ss[:, 0:TT], 1.0 / D, EPS, ALU.mult, ALU.add))
                rsqrt2(nw[:, 0, 0:TT], nw[:, 1, 0:TT], nw[:, 2, 0:TT])
                if k == 0:
                    dve.wait_ge(late_in, 16)
                elif k == 1:
                    dve.wait_ge(late2_in, 8 * 16)
                else:
                    dve.wait_ge(late_in, 32)
                for a in range(TT):
                    nc.vector.scalar_tensor_tensor(out=dst[:, a, :], in0=x_nat[:, a, :], scalar=nw[:, 1, a:a + 1], in1=gain, op0=ALU.mult, op1=ALU.mult).then_inc(normed, 1)

            def make_xT2(k):
                for b in range(4):
                    dve.wait_ge(xT_hid, LAYERS * 8 + k * 4 + b + 1)
                    nc.vector.tensor_tensor(xT_lo[:, 2 * b:2 * b + 2, :], ps[:, ACC + b, :].rearrange("p (c t) -> p c t", c=2),
                                            xT_hi[:, 2 * b:2 * b + 2, :].bitcast(F32), ALU.subtract).then_inc(xT_lod, 1)

            def add_product(u):
                dve.wait_ge(unit_done, u + 1 + SPLIT_CREDIT)
                for a in range(TT):
                    for h in range(2):
                        cols = slice(h * BANK, (h + 1) * BANK)
                        last = nc.vector.tensor_tensor(x_nat[:, a, cols], x_nat[:, a, cols], ps[:, ACC + 2 * a + h, :], ALU.add)
                last.then_inc(x_out, 1)

            def top_keys(a):
                nk = P * (a + 1)
                x, work, tmp, m8 = idx[:, a, 0:nk], cv[:, 2, 0:nk], cv[:, 3, 0:nk], nw[:, 0, :]
                diag = x[:, nk - P:nk]
                then(nc.vector.tensor_tensor(diag, diag, mask[:], ALU.add))
                then(nc.vector.max(m8, x))
                then(nc.vector.match_replace(work, m8, x, -3.0e38))
                for r in range(TOPK // 8 - 2):
                    then(nc.vector.max(m8, work))
                    then(nc.vector.match_replace(work, m8, work, -3.0e38))
                then(nc.vector.max(m8, work))
                least = m8[:, 7:8]
                then(nc.vector.tensor_scalar(tmp, x, least, None, ALU.is_gt))
                then(nc.vector.tensor_reduce(rr[:, 0:1], tmp, AX.X, ALU.add))
                then(nc.vector.tensor_scalar(rr[:, 1:2], rr[:, 0:1], -1.0, float(TOPK), ALU.mult, ALU.add))
                then(nc.vector.tensor_scalar(work, x, least, None, ALU.is_equal))
                sel = selm[:, a, 0:nk]
                then(nc.vector.tensor_tensor_scan(sel, ones[:, 0:1].broadcast_to([P, nk]), work, 0.0, ALU.mult, ALU.add))
                then(nc.vector.scalar_tensor_tensor(out=work, in0=sel, scalar=rr[:, 1:2], in1=work, op0=ALU.is_le, op1=ALU.mult))
                then(nc.vector.tensor_tensor(tmp, tmp, work, ALU.add))
                then(nc.vector.tensor_scalar(sel, tmp, -NEG, NEG, ALU.mult, ALU.add))
                nc.vector.tensor_tensor(sel[:, nk - P:nk], sel[:, nk - P:nk], mask[:], ALU.add).then_inc(sel_ready, 1)

            rms_rows(0, hn, lnb[:, 0, :])
            make_xT2(0)
            for w in range(W_PB):
                split2(G2 + w + 2, W_COLS.get(w + 2, UCOLS))
                if w == W_K + 1:
                    dve.wait_ge(ev2, 1)
                    dve.wait_ge(late2_in, 8 * 16)
                    then(nc.vector.tensor_scalar(nw[:, 0, 0:TT], ss[:, 4:4 + TT], 1.0 / KV_RANK, EPS, ALU.mult, ALU.add))
                    rsqrt2(nw[:, 0, 0:TT], nw[:, 1, 0:TT], nw[:, 2, 0:TT])
                    for a in range(TT):
                        last = nc.vector.scalar_tensor_tensor(out=ckv[:, a, :], in0=ckv[:, a, :], scalar=nw[:, 1, a:a + 1], in1=kvg, op0=ALU.mult, op1=ALU.mult)
                    last.then_inc(kv_normed, 1)
                for s in (2 * (w - X_S - 1), 2 * (w - X_S - 1) + 1):
                    if 0 <= s < 8:
                        nk = P * (s // 4 + 1)
                        e = E2[:, s % 4, :, 0:nk]
                        dve.wait_ge(s2_exp, s + 1)
                        then(nc.vector.reciprocal(rs2[:, s % 4, :], rs2[:, s % 4, :]))
                        nc.vector.tensor_tensor(e, e, bc(rs2[:, s % 4, :], 2, nk), ALU.mult).then_inc(s2_prob, 1)
                for kind, s in latent_steps(w):
                    latent_dve(dve, kind, s)
                if X_S <= w < X_S + 4:
                    for s in (2 * (w - X_S), 2 * (w - X_S) + 1):
                        nk = P * (s // 4 + 1)
                        e = E2[:, s % 4, :, 0:nk]
                        dve.wait_ge(s2_done, s + 1)
                        dve.wait_ge(bm_ready, s + 1)
                        if s >= 4:
                            dve.wait_ge(t2_done, s - 3)
                        then(nc.vector.tensor_tensor(e, ps[:, s % 2, :].rearrange("p (i k) -> p i k", i=2)[:, :, 0:nk], bias_t[:, s % 2, :, 0:nk], ALU.add))
                        nc.vector.tensor_reduce(nm2[:, s % 4, :], e, AX.X, ALU.max, negate=True).then_inc(s2_max, 1)
                if W_V <= w < W_GA:
                    n = w - W_V
                    dve.wait_ge(ev2, w + 1)
                    then(nc.vector.tensor_scalar(gel_s, gel_s, 4.0 * 0.044715 / 4.0, 1.0, ALU.mult, ALU.add))
                    nc.vector.tensor_tensor(gel_s, gel_s, gel_x, ALU.mult).then_inc(gel_poly, 1)
                    dst = (vg, ug)[n // 2][:, :, 256 * (n % 2):256 * (n % 2) + 256]
                    dve.wait_ge(gel_th, n + 1)
                    nc.vector.scalar_tensor_tensor(out=dst, in0=gel_s.rearrange("p (a c) -> p a c", a=TT), scalar=1.0,
                                                   in1=gel_x.rearrange("p (a c) -> p a c", a=TT), op0=ALU.add, op1=ALU.mult).then_inc(gel_out, 1)
                if w == W_U:
                    dve.wait_ge(gel_out, 2)
                    for a in range(TT):
                        last = nc.vector.bn_stats(st[:, a, 0, :], vg[:, a, :])
                    then(last)
                    for a in range(TT):
                        last = nc.vector.bn_aggr(mv[:, a, :], st[:, a, 0, :])
                    then(last)
                    then(nc.vector.tensor_scalar(nw[:, 0, 0:TT], mv[:, :, 1], EPS, None, ALU.add))
                    rsqrt2(nw[:, 0, 0:TT], nw[:, 1, 0:TT], nw[:, 2, 0:TT])
                    nc.vector.scalar_tensor_tensor(out=nmr[:], in0=mv[:, :, 0], scalar=-1.0, in1=nw[:, 1, 0:TT], op0=ALU.mult, op1=ALU.mult).then_inc(lnv_stat, 1)
                if w == X_LNV:
                    dve.wait_ge(lnv_hat, 1)
                    then(nc.vector.tensor_tensor(vg, vg, bc(lnv_g, 1, TT), ALU.mult))
                    nc.vector.tensor_tensor(vg, vg, bc(lnv_b, 1, TT), ALU.add).then_inc(lnv_out, 1)
                n = w - X_IX
                if 0 <= n < 8:
                    a, p = n // 4, n % 4
                    nk = P * (a + 1)
                    dve.wait_ge(ix_rel, n + 1)
                    for i in range(2):
                        wt = wi[:, a, 2 * p + i:2 * p + i + 1]
                        if p == 0 and i == 0:
                            then(nc.vector.tensor_scalar(idx[:, a, 0:nk], rel[:, n % 2, i, 0:nk], wt, None, ALU.mult))
                        else:
                            then(nc.vector.scalar_tensor_tensor(out=idx[:, a, 0:nk], in0=rel[:, n % 2, i, 0:nk], scalar=wt, in1=idx[:, a, 0:nk], op0=ALU.mult, op1=ALU.add))
                    nc.vector.memset(nw[:, 2, 7:8], 0.0).then_inc(ix_sum, 1)
                if w in (X_IX + 4, X_IX + 8):
                    top_keys((w - X_IX) // 4 - 1)
                if w == X_SP:
                    for a in range(TT):
                        dve.wait_ge(sp_done, a + 1)
                        for g in range(4):
                            cols = slice(g * P, (g + 1) * P)
                            last = nc.vector.scalar_tensor_tensor(out=ug[:, a, cols], in0=ps[:, (TB, O_B)[a], cols], scalar=bsT[:, g:g + 1], in1=ug[:, a, cols], op0=ALU.add, op1=ALU.mult)
                        last.then_inc(sp_out, 1)
                if w in (X_YB, X_YB + 1):
                    r = w - X_YB
                    dve.wait_ge(yb_hi, r + 1)
                    nc.vector.tensor_tensor(br_lo[:, 1, 2 * r:2 * r + 2, :], ps[:, TB, :].rearrange("p (c t) -> p c t", c=2),
                                            br_hi[:, 1, 2 * r:2 * r + 2, :].bitcast(F32), ALU.subtract).then_inc(yb_lo, 1)
            for kind, s in latent_steps(None):
                latent_dve(dve, kind, s)
            for w in range(W_PB, W_OUT):
                split2(G2 + w + 2, W_COLS.get(w + 2, UCOLS))
                dve.wait_ge(unit_done, G2 + w + 1 + SPLIT_CREDIT)
                j = (w - W_PB) % 2
                c0 = 4 * j + (8 if w < W_PA else 0)
                for r in range(2):
                    g = gT[:, c0 + 2 * r:c0 + 2 * r + 2, :]
                    y = ps[:, PROJ_BANKS[j][r], :].rearrange("p (c t) -> p c t", c=2)
                    last = nc.vector.scalar_tensor_tensor(out=g, in0=g, scalar=1.0, in1=y, op0=ALU.add, op1=ALU.mult)
                last.then_inc(proj_b if w < W_PA else bank_d, 1)
                if w >= W_PA:
                    dve.wait_ge(bank_d, j + 1)
                    m, other = gT[:, 4 * j:4 * j + 4, :], gT[:, 8 + 4 * j:8 + 4 * j + 4, :]
                    nc.vector.tensor_tensor(m, m, other, ALU.add).then_inc(proj_a, 1)
                    dve.wait_ge(pm_hi, j + 1)
                    nc.vector.scalar_tensor_tensor(out=xT_lo[:, 4 * j:4 * j + 4, :], in0=m, scalar=0.5, in1=xT_hi[:, 4 * j:4 * j + 4, :].bitcast(F32), op0=ALU.mult, op1=ALU.subtract).then_inc(pm_lo, 1)
            for w in range(W_OUT, W_OUT + 3):
                split2(G2 + w + 2, W_COLS.get(w + 2, UCOLS))
            add_product(G2 + W_OUT + 3)
            split2(G2 + W_OUT + 5)
            rms_rows(1, hn, lnb[:, 1, :])
            make_xT2(1)

            dve.wait_ge(unit_done, G2 + W_R + 1 + SPLIT_CREDIT)
            nc.vector.tensor_tensor(lg, ps[:, 7, 0:72].rearrange("p (a c) -> p a c", a=TT), bc(rb[:], 1, TT), ALU.add).then_inc(rt_log, 1)
            dve.wait_ge(rt_log, 1)
            col = [st[:, :, 0, i] for i in range(6)]

            def over(x, n):
                return bc(x, 2, n)

            def first_of(out_, x, top, n, tmp):
                then(nc.vector.tensor_tensor(tmp, x, over(top, n), ALU.is_equal))
                then(nc.vector.tensor_tensor(tmp, tmp, bc(wdesc[:, 0:n], 1, TT), ALU.mult))
                then(nc.vector.tensor_reduce(col[5], tmp, AX.X, ALU.max))
                then(nc.vector.tensor_tensor(out_, tmp, over(col[5], n), ALU.is_equal))

            gl, ge = lg[:, :, 0:4], rt[:, 0, :, 0:4]
            then(nc.vector.tensor_reduce(col[0], gl, AX.X, ALU.max))
            nc.vector.tensor_tensor(ge, gl, over(col[0], 4), ALU.subtract).then_inc(rt_in, 1)
            split2(G2 + W_R + 2)
            dve.wait_ge(rt_exp, 1)
            then(nc.vector.tensor_reduce(col[1], ge, AX.X, ALU.add))
            then(nc.vector.reciprocal(col[1], col[1]))
            then(nc.vector.tensor_tensor(ge, ge, over(col[1], 4), ALU.mult))
            then(nc.vector.tensor_reduce(col[1], ge, AX.X, ALU.max))
            oh = rt[:, 1, :, 0:4]
            first_of(oh, ge, col[1], 4, rt[:, 3, :, 0:4])
            prod = rt[:, 4]
            el = lg[:, :, 4:36]
            for a in range(TT):
                last = nc.vector.tensor_tensor(prod[:, a].rearrange("p (g e) -> p g e", g=4), el[:, a].rearrange("p (g e) -> p g e", g=4), bc(oh[:, a], 2, 8), ALU.mult)
            then(last)
            es = rt[:, 2, :, 0:8]
            then(nc.vector.tensor_reduce(es, prod.rearrange("p a (g e) -> p a e g", g=4), AX.X, ALU.add))
            then(nc.vector.tensor_reduce(col[0], es, AX.X, ALU.max))
            nc.vector.tensor_tensor(es, es, over(col[0], 8), ALU.subtract).then_inc(rt_in, 1)
            dve.wait_ge(rt_exp, 2)
            then(nc.vector.tensor_reduce(col[0], es, AX.X, ALU.add))
            then(nc.vector.reciprocal(col[0], col[0]))
            then(nc.vector.tensor_tensor(es, es, over(col[0], 8), ALU.mult))
            then(nc.vector.tensor_reduce(col[2], es, AX.X, ALU.max))
            o1, o2 = rt[:, 3, :, 8:16], rt[:, 3, :, 16:24]
            first_of(o1, es, col[2], 8, rt[:, 3, :, 0:8])
            then(nc.vector.scalar_tensor_tensor(out=es, in0=o1, scalar=-2.0, in1=es, op0=ALU.mult, op1=ALU.add))
            then(nc.vector.tensor_reduce(col[3], es, AX.X, ALU.max))
            first_of(o2, es, col[3], 8, rt[:, 3, :, 0:8])
            then(nc.vector.tensor_tensor(col[4], col[2], col[3], ALU.add))
            then(nc.vector.reciprocal(col[4], col[4]))
            then(nc.vector.tensor_tensor(col[4], col[4], col[1], ALU.mult))
            then(nc.vector.tensor_tensor(o1, o1, over(col[2], 8), ALU.mult))
            then(nc.vector.tensor_tensor(o2, o2, over(col[3], 8), ALU.mult))
            then(nc.vector.tensor_tensor(o1, o1, o2, ALU.add))
            then(nc.vector.tensor_tensor(o1, o1, over(col[4], 8), ALU.mult))
            for a in range(TT):
                last = nc.vector.tensor_tensor(comb[:, a].rearrange("p (g e) -> p g e", g=4), bc(oh[:, a], 2, 8), bc(o1[:, a], 1, 4), ALU.mult)
            last.then_inc(comb_ready, 1)

            def gated(e, q):
                dve.wait_ge(th_done, e + 1)
                g = ps[:, 4 + 2 * q, :].rearrange("p (c t) -> p c t", c=2)
                nc.vector.scalar_tensor_tensor(out=eg[:, q], in0=eg[:, q], scalar=1.0, in1=g, op0=ALU.add, op1=ALU.mult).then_inc(g_out, 1)

            def hidden(e, before, q, c, loads, u, i=None):
                dve.wait_ge(comb_in[c], loads)
                dve.wait_ge(g_out, e + 1)
                nc.vector.tensor_tensor(eg[:, q], eg[:, q], bc(comb_b[:, c, :], 1, 2), ALU.mult).then_inc(weighted, 1)
                dve.wait_ge(unit_done, u + 1 + SPLIT_CREDIT if i is None else i * 12 + (u + 1 + SPLIT_CREDIT))
                if before is not None:
                    dve.wait_ge(he_lod, before)
                dve.wait_ge(weighted, e + 1)
                up = ps[:, 5 + 2 * q, :].rearrange("p (c t) -> p c t", c=2)
                nc.vector.tensor_tensor(ec[:, q], eg[:, q], up, ALU.mult).then_inc(he_ready, 1)

            def hidden_lo(e, q):
                dve.wait_ge(he_hid, e + 1)
                nc.vector.tensor_tensor(he_lo[:, q], ec[:, q], he_hi[:, q].bitcast(F32), ALU.subtract).then_inc(he_lod, 1)

            def expert(e, before, q, c, loads, u, i=None):
                gated(e, q)
                split2(u + 2, UCOLS, i)
                hidden(e, before, q, c, loads, u + 1, i)
                split2(u + 3, UCOLS, i)
                hidden_lo(e, q)
                if i is not None or u + 4 < E0 + 3 * N_EXPERTS:
                    split2(u + 4, UCOLS, i)

            gated(0, 0)
            split2(E0 + 2)
            hidden(0, None, 0, 0, 16, E0 + 1)
            split2(E0 + 3)
            hidden_lo(0, 0)
            expert(1, None, 1, 1, 16, E0 + 2)
            with dve.Fori(0, E_LOOP) as i:
                for q in range(4):
                    expert(i * 4 + (2 + q), i * 4 + (1 + q), q % 2, (2 + q) % 4, i * 16 + 16 * (1 + (2 + q) // 4), E0 + 5 + 3 * q, i)
            for e in (N_EXPERTS - 2, N_EXPERTS - 1):
                expert(e, e - 1, e % 2, e % 4, 16 * (e // 4 + 1), E0 + 3 * e - 1)
            add_product(E0 + 3 * N_EXPERTS - 1)
            rms_rows(2, x_nat, lnb[:, 0, :])

        @block.tensor
        def _(pe):
            def mm3(out_, left, right, start, stop):
                nc.tensor.matmul(out_, left[1], right[0], start=start, stop=False)
                nc.tensor.matmul(out_, left[0], right[1], start=False, stop=False)
                return nc.tensor.matmul(out_, left[0], right[0], start=False, stop=stop)

            def weights(u, k, n):
                return unit3(w_hi, u % SPLIT, k, n), unit3(w_lo, u % SPLIT, k, n)

            def transposed(u, bank, xT, ready=None):
                w = weights(u, KC, 256)
                for c in range(2):
                    for k in range(KC):
                        if ready is not None and c == 0 and k % 2 == 0:
                            pe.wait_ge(xT_lod, ready + (k // 2 + 1))
                        cols = slice(c * P, (c + 1) * P)
                        last = mm3(ps[:, bank, c * T:(c + 1) * T], [x[:, k, cols] for x in w], [x[:, k, :] for x in xT], k == 0, k == KC - 1)
                last.then_inc(unit_done, 1)

            def natural(u, bank, xT):
                w = weights(u, KC, 256)
                for a in range(TT):
                    for k in range(KC):
                        last = mm3(ps[:, bank, a * 256:(a + 1) * 256], [x[:, k, a * P:(a + 1) * P] for x in xT], [x[:, k, :] for x in w], k == 0, k == KC - 1)
                last.then_inc(unit_done, 1)

            def rows_unit(u, left, start, stop, ready=None):
                w = weights(u, 2, D)
                for k in range(2):
                    for a in range(TT):
                        for h in range(2):
                            last = mm3(ps[:, ACC + 2 * a + h, :], [x[:, k, a * P:(a + 1) * P] for x in left],
                                       [x[:, k, h * BANK:(h + 1) * BANK] for x in w], start and k == 0, stop and k == 1)
                last.then_inc(unit_done, 1)

            pe.sem_inc(unit_done, SPLIT_CREDIT)
            pe.wait_ge(const_in, CONSTS)
            for i in range(LAYERS):
                nc.tensor.transpose(ps[:, 7, i * 256:i * 256 + C_CW], row_v[:, i, :], ident[0:C_CW, 0:C_CW])
                last = nc.tensor.transpose(ps[:, 7, i * 256 + C_CW:i * 256 + C_ALL], row_cw[:, i, :], ident[0:CONV_W * CC, 0:CONV_W * CC])
            last.then_inc(rows_T, 1)
            nc.tensor.matmul(ps[0:N_HEADS, 6, :], relb, t5, start=True, stop=True).then_inc(t5_mm, 1)
            pe.wait_ge(setup_p, 2)
            pe.wait_ge(x_in, 16)
            pe.wait_ge(prm_ready, 1)
            pe.sem_inc(x_out, 1)

            xT = (xT_hi, xT_lo)
            with pe.Fori(0, LAYERS) as l:
                base = l * UNITS

                def ready(u):
                    pe.wait_ge(split_done, base + u + 1 + RAW_CREDIT)

                def make_xT(k):
                    for a in range(TT):
                        if k == 1:
                            pe.wait_ge(x_out, l * 2 * TT + a + 1 + 1)
                        elif a == 0:
                            pe.wait_ge(x_out, l * 2 * TT + 1)
                        for c in range(KC):
                            last = nc.tensor.transpose(ps[:, ACC + c // 2, (c % 2) * T + a * P:(c % 2) * T + (a + 1) * P], x_nat[:, a, c * P:(c + 1) * P], ident[:])
                            if a == TT - 1 and c % 2 == 1:
                                last.then_inc(xT_done, 1)

                def scores(s):
                    pe.wait_ge(qk_copied, l * 8 + (4 if s < 8 else 8))
                    if s >= 1:
                        pe.wait_ge(exp_done, l * TASKS + s)
                    kind, c, a = 2 * (s // 8), (s % 8) // 2, s % 2
                    nk = P * (a + 1)
                    for i in range(2):
                        part = slice(i * HD, (i + 1) * HD)
                        last = nc.tensor.matmul(ps[:, i, 0:nk], qkT[part, kind, c, a * P:(a + 1) * P], qkT[part, kind + 1, c, 0:nk], start=True, stop=True)
                    last.then_inc(score_done, 1)

                def prob_transposes(s):
                    pe.wait_ge(prob_done, l * TASKS + s + 1)
                    if s >= 1:
                        pe.wait_ge(probT_copied, l * TASKS + s)
                    for i in range(1 if s < 8 else 2):
                        for b in range(s % 2 + 1):
                            last = nc.tensor.transpose(ps[:, PT_B, (2 * i + b) * P:(2 * i + b + 1) * P], E[:, s % 2, i, b * P:(b + 1) * P], ident[:])
                    last.then_inc(probT_done, 1)

                def values(s):
                    a, h = s % 2, (s % 8) // 2
                    pe.wait_ge(probT_copied, l * TASKS + s + 1)
                    pe.wait_ge(evac_a, l * EV_A + evac_before((U_V[1] if s < 8 else U_V[3]) + 1)[0])
                    if 1 <= s < 9:
                        pe.wait_ge(pv_copied, l * TASKS + s)
                    elif s >= 9:
                        pe.wait_ge(moba_lo, l * 8 + s - 8)
                    cols = slice(0, P)
                    for i in range(1 if s < 8 else 2):
                        for b in range(a + 1):
                            p = pT[:, (2 * i + b) * P:(2 * i + b + 1) * P]
                            if s < 8:
                                last = nc.tensor.matmul(ps[:, O_B, cols], p, vv[:, 0, b, h * P:(h + 1) * P], start=b == 0, stop=b == a)
                            else:
                                last = nc.tensor.matmul(ps[i * HD:(i + 1) * HD, O_B, cols], vv[:, 1, b, (2 * h + i) * HD:(2 * h + i + 1) * HD], p, start=b == 0, stop=b == a)
                    last.then_inc(pv_done, 1)

                make_xT(0)
                for u in range(U_BR):
                    ready(u)
                    if u >= 3:
                        v = u - 3
                        if v in U_QK:
                            pe.wait_ge(rotated, l * 8 + U_QK.index(v) + 1)
                        else:
                            pe.wait_ge(evac_a, l * EV_A + evac_before(v + 1)[0])
                    if u in U_QK or u in U_V:
                        natural(u, UB + u % 3, xT)
                    else:
                        transposed(u, UB + u % 3, xT, l * 8 if u == 0 else None)
                    if u - 2 in U_QK:
                        n = U_QK.index(u - 2)
                        pe.wait_ge(roped, l * 8 + n + 1)
                        if n >= 1:
                            pe.wait_ge(qk_copied, l * 8 + n)
                        for c in range(2):
                            for a in range(TT):
                                last = nc.tensor.transpose(ps[:, TB, c * T + a * P:c * T + (a + 1) * P], rope[:, n % 2, a * 256 + c * P:a * 256 + (c + 1) * P], ident[:])
                        last.then_inc(qk_T, 1)
                    if 0 <= u - 10 < TASKS:
                        scores(u - 10)
                    if 0 <= u - 12 < TASKS:
                        prob_transposes(u - 12)
                    if 0 <= u - 13 < TASKS:
                        values(u - 13)
                    if u == 20:
                        pe.wait_ge(conv_link, (l + 1) * CONV_W * CC)
                        pe.wait_ge(qk_copied, l * 8 + 8)
                        for c in range(CC):
                            last = nc.tensor.matmul(ps[:, TB, 0:T], ones[:], cv[:, c, :], start=c == 0, stop=c == CC - 1)
                        last.then_inc(csum_done, 1)
                    if u == 21:
                        pe.wait_ge(c_sq, l + 1)
                        for c in range(CC):
                            last = nc.tensor.matmul(ps[:, TB, T:2 * T], ones[:], hpad[:, c, PAD:], start=c == 0, stop=c == CC - 1)
                        last.then_inc(csum_done, 1)
                    if u in (25, 26):
                        r = u - 25
                        pe.wait_ge(o_normed, l + 1)
                        if r == 0:
                            pe.wait_ge(c_norm, l + 1)
                        else:
                            pe.wait_ge(oT_lod, l * 2 + 1)
                        for c in range(2):
                            for a in range(TT):
                                last = nc.tensor.transpose(ps[:, TB, c * T + a * P:c * T + (a + 1) * P], o_nat[:, a, 2 * r + c, :], ident[:])
                        last.then_inc(oT_done, 1)
                values(TASKS - 1)

                for c in range(KC):
                    u = U_BR + c
                    ready(u)
                    w = weights(u, 12, P)
                    b0 = 4 + 2 * (c % 2)
                    if c == 0:
                        pe.wait_ge(evac_a, l * EV_A + EV_A_IN)
                        pe.wait_ge(oT_lod, l * 2 + 2)
                    if c >= 2:
                        pe.wait_ge(evac_d, l * KC + c - 1)
                    for b in range(3):
                        if c == 0:
                            pe.wait_ge(*((c_lo, l + 1), (oT_lod, l * 2 + 2), (moba_lo, l * 8 + 8))[b])
                        o = ps[:, b0 + b // 2, (b % 2) * T:(b % 2 + 1) * T]
                        for k in range(CC):
                            last = mm3(o, [x[:, b * CC + k, :] for x in w], [x[:, b, k, :] for x in (br_hi, br_lo)], k == 0, k == CC - 1)
                    last.then_inc(unit_done, 1)
                for k in range(4):
                    ready(U_WO + k)
                    pe.wait_ge(m_lo, l * KC + 2 * k + 2)
                    rows_unit(U_WO + k, [x[:, 2 * k:2 * k + 2, :] for x in xT], k == 0, k == 3)
                make_xT(1)

                def ff2(j, u, i=0, jj=None, start=False, stop=False):
                    pe.wait_ge(split_done, base + i * 4 + (u + 1 + RAW_CREDIT))
                    pe.wait_ge(ff_lo, l * FFJ + jj + 1)
                    rows_unit(u, (h_hi[:, j], h_lo[:, j]), start, stop)

                for j in range(2):
                    ready(U_FF + j)
                    transposed(U_FF + j, 4 + j, xT, l * 8 + 4 if j == 0 else None)
                ff2(0, U_FF + 2, 0, 0, start=True)
                with pe.Fori(0, FFJ // 2 - 1) as i:
                    for q in range(2):
                        u = U_FF + 3 + 2 * q
                        pe.wait_ge(split_done, base + i * 4 + (u + 1 + RAW_CREDIT))
                        pe.wait_ge(evac_a, l * EV_A + i * 2 + (EV_A_IN + q + 1))
                        transposed(u, 4 + q, xT)
                        ff2(1 - q, u + 1, i, i * 2 + (1 + q))
                ff2(1, UNITS - 1, 0, FFJ - 1, stop=True)

            def ready2(u, i=None):
                pe.wait_ge(split_done, u + 1 + RAW_CREDIT if i is None else i * 12 + (u + 1 + RAW_CREDIT))

            def make_xT2(k):
                for a in range(TT):
                    pe.wait_ge(normed, k * TT + a + 1)
                    for c in range(KC):
                        last = nc.tensor.transpose(ps[:, ACC + c // 2, (c % 2) * T + a * P:(c % 2) * T + (a + 1) * P], hn[:, a, c * P:(c + 1) * P], ident[:])
                        if a == TT - 1 and c % 2 == 1:
                            last.then_inc(xT_done, 1)

            def bank_free(w):
                if w >= 3:
                    pe.wait_ge(ev2, w - 2)

            make_xT2(0)
            for w in range(W_PB):
                u = G2 + w
                ready2(u)
                bank_free(w)
                if w == W_K:
                    k_w = weights(u, KC, 256)
                    for a in range(TT):
                        for k in range(KC):
                            mm3(ps[:, UB + w % 3, a * P:(a + 1) * P], [x[:, k, a * P:(a + 1) * P] for x in xT], [x[:, k, 0:P] for x in k_w], k == 0, k == KC - 1)
                    for k in range(KC):
                        last = mm3(ps[:, UB + w % 3, 256:512], [x[:, k, P:256] for x in k_w], [x[:, k, :] for x in xT], k == 0, k == KC - 1)
                    last.then_inc(unit_done, 1)
                elif w == W_WI:
                    k_w = weights(u, KC, 8)
                    for a in range(TT):
                        for k in range(KC):
                            last = mm3(ps[:, UB + w % 3, a * 8:(a + 1) * 8], [x[:, k, a * P:(a + 1) * P] for x in xT], [x[:, k, :] for x in k_w], k == 0, k == KC - 1)
                    last.then_inc(unit_done, 1)
                elif W_V <= w < W_GA:
                    natural(u, UB + w % 3, xT)
                else:
                    transposed(u, UB + w % 3, xT, LAYERS * 8 if w == 0 else None)
                if w == 0:
                    pe.wait_ge(late3_in, 32)
                    for c in range(4):
                        last = nc.tensor.transpose(ps[:, TB, c * P:(c + 1) * P], w_uk[:, c * P:(c + 1) * P], ident[:])
                    last.then_inc(ukT_done, 1)
                    pe.wait_ge(ws_masked, 1)
                    for g in range(4):
                        last = nc.tensor.transpose(ps[:, O_B, g * P:(g + 1) * P], ws_nat[:, g, :], ident[:])
                    last.then_inc(wsT_done, 1)
                if w == W_WI + 1:
                    pe.wait_ge(kv_normed, 1)
                    pe.wait_ge(ukT_c, 1)
                    for a in range(TT):
                        last = nc.tensor.transpose(ps[:, TB, a * P:(a + 1) * P], ckv[:, a, :], ident[:])
                    last.then_inc(kvT_done, 1)
                n = w - X_IX
                if 0 <= n < 8:
                    a, p = n // 4, n % 4
                    nk = P * (a + 1)
                    pe.wait_ge(ev2, W_WI + 1)
                    if n >= 1:
                        pe.wait_ge(ix_rel, n)
                    for i in range(2):
                        part = slice(i * HD, (i + 1) * HD)
                        last = nc.tensor.matmul(ps[:, i, 0:nk], qiT[part, p, a * P:(a + 1) * P], kiT[part, 0:nk], start=True, stop=True)
                    last.then_inc(ix_done, 1)
                n = w - X_QL
                if 0 <= n < 4:
                    pe.wait_ge(ev2, W_Q + 2)
                    pe.wait_ge(kvT_c, 1)
                    pe.wait_ge(wsT_c, 1)
                    if n >= 1:
                        pe.wait_ge(ql_c, n)
                    for i in range(2):
                        part = slice(i * HD, (i + 1) * HD)
                        last = nc.tensor.matmul(ps[:, O_B + i, 0:T], w_ukT[part, n, :], q2T[part, n, :], start=True, stop=True)
                    last.then_inc(ql_done, 1)
                if w == X_SP:
                    pe.wait_ge(lnv_out, 1)
                    pe.wait_ge(ql_c, 4)
                    for a in range(TT):
                        for g in range(4):
                            cols = slice(g * P, (g + 1) * P)
                            last = nc.tensor.matmul(ps[:, (TB, O_B)[a], cols], wsT[:, g, :], vg[:, a, cols], start=True, stop=True)
                        last.then_inc(sp_done, 1)
                if w in (X_YB, X_YB + 1):
                    r = w - X_YB
                    pe.wait_ge(sp_out, TT)
                    if r == 1:
                        pe.wait_ge(yb_lo, 1)
                    for c in range(2):
                        for a in range(TT):
                            last = nc.tensor.transpose(ps[:, TB, c * T + a * P:c * T + (a + 1) * P], ug[:, a, (2 * r + c) * P:(2 * r + c + 1) * P], ident[:])
                    last.then_inc(ybT_done, 1)
                for kind, s in latent_steps(w):
                    latent_pe(pe, kind, s)
                if X_S <= w < X_S + 4:
                    for s in (2 * (w - X_S), 2 * (w - X_S) + 1):
                        a, p = s // 4, s % 4
                        nk = P * (a + 1)
                        if s < 2:
                            pe.wait_ge(ix_rel, 8)
                        else:
                            pe.wait_ge(s2_max, s - 1)
                        for i in range(2):
                            last = nc.tensor.matmul(ps[:, s % 2, i * T:i * T + nk], q_latT[:, 2 * p + i, a * P:(a + 1) * P], ckvT[:, 0:nk], start=True, stop=True)
                        last.then_inc(s2_done, 1)
            for kind, s in latent_steps(None):
                latent_pe(pe, kind, s)
            for w in range(W_PB, W_OUT):
                u = G2 + w
                ready2(u)
                j = (w - W_PB) % 2
                if w < W_PA:
                    pe.wait_ge(ev2, W_PB)
                    pe.wait_ge(yb_lo, 2)
                    pe.wait_ge(s2_max, 8)
                else:
                    pe.wait_ge(proj_b, j + 1)
                    pe.wait_ge(a2_lo, 8)
                w_u = weights(u, CC, 512)
                b = 1 if w < W_PA else 0
                for c in range(4):
                    for k in range(CC):
                        last = mm3(ps[:, PROJ_BANKS[j][c // 2], (c % 2) * T:(c % 2 + 1) * T], [x[:, k, c * P:(c + 1) * P] for x in w_u],
                                   [x[:, b, k, :] for x in (br_hi, br_lo)], k == 0, k == CC - 1)
                last.then_inc(unit_done, 1)
            for k in range(4):
                u = G2 + W_OUT + k
                ready2(u)
                pe.wait_ge(pm_lo, k // 2 + 1)
                pe.wait_ge(bank_d, 2)
                rows_unit(u, [x[:, 2 * k:2 * k + 2, :] for x in xT], k == 0, k == 3)
            make_xT2(1)
            u = G2 + W_R
            ready2(u)
            pe.wait_ge(xT_lod, LAYERS * 8 + 8)
            r_w = weights(u, KC, 36)
            for a in range(TT):
                for k in range(KC):
                    last = mm3(ps[:, 7, a * 36:(a + 1) * 36], [x[:, k, a * P:(a + 1) * P] for x in xT], [x[:, k, :] for x in r_w], k == 0, k == KC - 1)
            last.then_inc(unit_done, 1)

            def down(e1, q, u, i=None, start=False, stop=False):
                ready2(u, i)
                pe.wait_ge(he_lod, e1)
                rows_unit(u, (he_hi[:, q], he_lo[:, q]), start, stop)

            def expert(e, before, q, u, i=None):
                ready2(u, i)
                if before is not None:
                    pe.wait_ge(g_out, before)
                transposed(u, 4 + 2 * q, xT)
                ready2(u + 1, i)
                if before is not None:
                    pe.wait_ge(he_ready, before)
                transposed(u + 1, 5 + 2 * q, xT)

            expert(0, None, 0, E0)
            pe.wait_ge(comb_ready, 1)
            for a in range(TT):
                last = nc.tensor.transpose(ps[0:32, 7, a * P:(a + 1) * P], comb[:, a, :], ident[:])
            last.then_inc(combT_done, 1)
            pe.wait_ge(combT_c, 1)
            expert(1, None, 1, E0 + 2)
            down(1, 0, E0 + 4, start=True)
            with pe.Fori(0, E_LOOP) as i:
                for q in range(4):
                    expert(i * 4 + (2 + q), i * 4 + (1 + q), q % 2, E0 + 5 + 3 * q, i)
                    down(i * 4 + (2 + q), (q + 1) % 2, E0 + 7 + 3 * q, i)
            for e in (N_EXPERTS - 2, N_EXPERTS - 1):
                expert(e, e - 1, e % 2, E0 + 3 * e - 1)
                down(e, (e - 1) % 2, E0 + 3 * e + 1)
            down(N_EXPERTS, (N_EXPERTS - 1) % 2, E0 + 3 * N_EXPERTS - 1, stop=True)


_OUT = ((1, T, D), "float32")


def constants():
    inv = np.float32(10000.0) ** (-np.arange(0, HD, 2, dtype=np.float32) / np.float32(HD))
    ang = np.arange(T, dtype=np.float32)[:, None] * inv[None, :].astype(np.float32)
    ang = np.concatenate([ang, ang], axis=-1)
    cos, sin = np.cos(ang), np.sin(ang)
    sin = np.concatenate([-sin[:, :HD // 2], sin[:, HD // 2:]], axis=-1)
    scale = np.float32(HD ** -0.5)
    lam = np.array([0.8 - 0.6 * math.exp(-0.3 * i) for i in range(LAYERS)])
    n = 255 - np.arange(512)
    nf = np.maximum(n, 1).astype(np.float32)
    large = 16 + (np.log(nf / np.float32(16)) / np.float32(np.log(128 / 16)) * np.float32(16)).astype(np.int32)
    bucket = np.where(n < 16, n, np.minimum(large, 31))
    t5 = (np.arange(32)[:, None] == bucket[None, :]) & (n >= 0)[None, :]
    keep = np.arange(P)[None, :] <= np.arange(P)[:, None]
    return {
        "c_ident": np.eye(P, dtype=np.float32),
        "c_mask": np.where(keep, 0.0, NEG).astype(np.float32),
        "c_rot": np.stack([cos * scale, sin * scale, cos, sin]).astype(np.float32),
        "c_t5": t5.astype(np.float32),
        "c_lam": np.stack([lam, 1.0 - lam]).astype(np.float32),
    }


def kernel(**inputs):
    import concourse.bacc as bacc
    from concourse.bass_utils import run_bass_kernel_spmd

    nc = bacc.Bacc("TRN2", target_bir_lowering=False, num_devices=1)
    arrays = {"in_" + n: np.ascontiguousarray(a) for n, a in {**inputs, **constants()}.items()}
    aps = {n[3:]: nc.dram_tensor(n, a.shape, mybir.dt.from_np(a.dtype), kind="ExternalInput").ap() for n, a in arrays.items()}
    out = nc.dram_tensor("out_0", _OUT[0], F32, kind="ExternalOutput").ap()
    build(nc, aps, out)
    return run_bass_kernel_spmd(nc, [arrays], core_ids=[0]).results[0]["out_0"]
```

```python
import math
from contextlib import ExitStack

import numpy as np

import concourse.bass as bass
from concourse import mybir

F32, F32R, I32 = mybir.dt.float32, mybir.dt.float32r, mybir.dt.int32
ALU, ACT, AX = mybir.AluOpType, mybir.ActivationFunctionType, mybir.AxisListType

P = 128
T = 256
TT = T // P
D = 1024
KC = D // P
BANK = 512
NEG = -1e30

LAYERS = 2
CONV_CH, CONV_W = 512, 31
CC = CONV_CH // P
PAD = CONV_W - 1
D_FF = 4 * D
FFJ = D_FF // 256
ALPHA = (2.0 * LAYERS) ** 0.25
LN_EPS = 1e-5
HD = 64
TASKS = 16

U_QK = (4, 5, 6, 7, 10, 11, 12, 13)
U_V = (8, 9, 14, 15)
U_GATE = 16
U_BR = 28
U_WO = U_BR + KC
U_FF = U_WO + 4
UNITS = U_FF + 2 * FFJ
U_POOL = (4, 10, 16, 18, 20)
RAW, SPLIT = 4, 2
RAW_CREDIT, SPLIT_CREDIT = RAW, SPLIT
UCOLS = 2048

C_CB, C_CG, C_CBT, C_GB, C_F1 = 0, 4, 8, 12, 36
C_CW = 68
C_ALL = C_CW + CONV_W * CC


def unit_cols(u):
    return 12 * P if U_BR <= u < U_WO else UCOLS

N_HEADS, KV_RANK, TOPK, EPS = 8, 128, 64, 1e-6
N_EXPERTS = 32
IDX_SCALE = float(8 ** -0.5 * 64 ** -0.5)
GELU_C = math.sqrt(2.0 / math.pi)
O_Q, O_KV, O_QI, O_KI, O_WI, O_U, O_V, O_GA, O_GB = (int(c) for c in np.cumsum((0, 512, 128, 512, 64, 8, 512, 512, 1024)))
G2 = LAYERS * UNITS
W_QI, W_K, W_Q, W_V, W_U, W_GA, W_GB, W_PB, W_PA, W_OUT, W_R = 0, 2, 3, 5, 7, 9, 13, 17, 19, 21, 25
K_COLS = KV_RANK + 64 + 8
LOADS = {W_K: 2, W_R: 2}
W_COLS = {W_K: KC * K_COLS, W_R: KC * 36}
E0 = G2 + W_R + 1
CAP = 64
PAIRS, ROUNDS = N_EXPERTS // 2, T // CAP
ROUND_UNITS = 6 * PAIRS
Y_BANKS = (7, 5)
PROJ_BANKS = ((5, 6), (7, 4))
X_IX, X_TOP, X_QL, X_LNV, X_SP, X_YB, X_S = 4, 6, 8, 8, 10, 11, 11


def raw_inc(u):
    return 48 if U_BR <= u % UNITS < U_WO else 16


def raw_count(u):
    return sum(raw_inc(v) for v in range(u % RAW, u + 1, RAW))


RAW_INCS = [raw_count(UNITS - RAW + s) for s in range(RAW)]
CONSTS, BCASTS = 11 * 16, 6 * 16
POOL_LINKS, ACT_LINKS, DVE_LINKS = 1, 1, 115


def bc(ap, axis, n):
    a = ap.unsqueeze(axis)
    shape = list(a.shape)
    shape[axis] = n
    return a.broadcast_to(shape)


def build(nc, t, out):
    ctx = ExitStack()
    with ctx:
        def sb(name, shape, dt=F32):
            return ctx.enter_context(nc.sbuf_tensor(name, shape, dt))

        def sem(name):
            return ctx.enter_context(nc.semaphore(name))

        raw = sb("raw", [P, RAW, UCOLS])
        w_hi = sb("w_hi", [P, SPLIT, UCOLS], F32R)
        w_lo = sb("w_lo", [P, SPLIT, UCOLS], F32R)
        xT_hi = sb("xT_hi", [P, KC, T], F32R)
        xT_lo = sb("xT_lo", [P, KC, T], F32R)
        br_hi = sb("br_hi", [P, 3, CC, T], F32R)
        br_lo = sb("br_lo", [P, 3, CC, T], F32R)
        h_hi = br_hi[:, 0].rearrange("p (s c) t -> p s c t", s=2)
        h_lo = br_lo[:, 0].rearrange("p (s c) t -> p s c t", s=2)
        x_nat = sb("x_nat", [P, TT, D])
        lnb = sb("lnb", [P, 3, D])
        gT = sb("gT", [P, 24, T])
        cv = sb("cv", [P, CC, T])
        hpad = sb("hpad", [P, CC, PAD + T])
        rope = sb("rope", [P, 3, 512])
        E = sb("E", [P, 2, 2, T])
        pT = sb("pT", [P, 512])
        o_nat = sb("o_nat", [P, TT, 4, P])
        qkT = sb("qkT", [P, 4, 4, T])
        vv = sb("vv", [P, 2, TT, 512])
        mix = rope[:].rearrange("p a b -> p (a b)").rearrange("p (s b t) -> p s b t", s=2, b=3)
        ff_r = E[:].rearrange("p s i t -> p s (i t)")
        ff_s = o_nat[:].rearrange("p s h d -> p s (h d)")
        ident = sb("ident", [P, P])
        ones = sb("ones", [P, P])
        alpha = sb("alpha", [P, 1])
        mask = sb("mask", [P, P])
        rot = sb("rot", [P, 4, TT, HD])
        prm_all = sb("prm_all", [P, LAYERS, C_ALL])
        prm = sb("prm", [P, C_ALL])
        gsub = sb("gsub", [P, LAYERS, P])
        linit = sb("linit", [P, 2, LAYERS])
        lamv = sb("lamv", [P, 4, LAYERS * HD])
        lams = sb("lams", [P, 2, LAYERS])
        nlam = sb("nlam", [P, LAYERS])
        row_cw = E[0:CONV_W * CC].rearrange("p s i t -> p (s i t)")[:, 0:LAYERS * P].rearrange("p (l c) -> p l c", l=LAYERS)
        row_v = pT[0:C_CW, 0:LAYERS * P].rearrange("p (l c) -> p l c", l=LAYERS)
        nm = sb("nm", [P, 2, 2])
        rs = sb("rs", [P, 2, 2])
        rr = sb("rr", [P, 2])
        ss = sb("ss", [P, TT * 4])
        st = sb("st", [P, TT, 2, 6])
        mv = sb("mv", [P, TT, 2])
        nmr = sb("nmr", [P, TT])
        counted = sb("counted", [1, 1])
        nw = sb("nw", [P, 3, 8])
        junk = lamv[:, 0, :]

        ps = ctx.enter_context(nc.psum_tensor("ps", [P, 8, BANK], F32))
        ACC, PT_B, O_B, TB, UB = 0, 2, 3, 4, 5

        hn = gT[:, 16:24, :].rearrange("p (a c) t -> p a (c t)", a=TT)
        gel_s = gT[:, 16:18, :].rearrange("p c t -> p (c t)")
        gel_x = gT[:, 18:20, :].rearrange("p c t -> p (c t)")
        w_uk = gT[:, 20:22, :].rearrange("p c t -> p (c t)")
        w_uv = gT[:, 22:24, :].rearrange("p c t -> p (c t)")
        w_ukT = lnb[:, 0, 0:512].rearrange("p (c r) -> p c r", c=4)
        q2T, qiT = qkT[:, 0], qkT[:, 1]
        q_latT = qkT[:, 2:4].rearrange("p a c t -> p (a c) t")
        E2 = qkT[:, 0:2].rearrange("p a (b i) t -> p (a b) i t", i=2)
        ug, vg = vv[:, 0], vv[:, 1]
        hflat = hpad[:].rearrange("p c t -> p (c t)")
        ckv = hflat[:, 0:256].rearrange("p (a r) -> p a r", a=TT)
        ckvT = hflat[:, 256:512]
        kiT = hflat[:, 512:768]
        ki2 = pT[:, 256:512].rearrange("p (a i d) -> p a i d", a=TT, i=2)
        o_lat = hflat[:, 768:1024].rearrange("p (i q) -> p i q", i=2)
        idx = rope[:, 0, :].rearrange("p (a k) -> p a k", a=TT)
        rel = rope[:, 1:3, :].rearrange("p s (i k) -> p s i k", i=2)
        selm = cv[:, 0:2, :]
        bias_t = o_nat[:].rearrange("p s h d -> p s (h d)").rearrange("p s (i k) -> p s i k", i=2)
        ws_nat = lamv[:].rearrange("p a d -> p (a d)").rearrange("p (g j) -> p g j", g=4)
        wsT = rot[:].rearrange("p k a d -> p (k a d)").rearrange("p (g i) -> p g i", g=4)
        kvg = gsub[:, 0, :]
        lnv_g, lnv_b = lnb[:, 2, 0:512], lnb[:, 2, 512:1024]
        h2_hi, h2_lo = [x[:, 0:2].rearrange("p a c t -> p a (c t)") for x in (br_hi, br_lo)]
        xg_hi, xg_lo = xT_hi[:, :, 0:3 * CAP], xT_lo[:, :, 0:3 * CAP]
        xg_parts = [x.rearrange("p c (e s) -> p c e s", e=2)[:, :, :, 0:CAP] for x in (xT_hi[:], xT_lo[:])]
        picks = xT_lo[:, :, 3 * CAP:].rearrange("p (a q e) s -> p a q e s", a=TT, q=2)
        place = [br_hi[:, 2, 2 + q, :].rearrange("p (a t) -> p a t", a=TT) for q in range(2)]
        heT_hi = br_lo[:, 2, 2:4, 0:3 * CAP].rearrange("p c (k s) -> p c k s", k=3)
        heT_lo = sb("heT_lo", [P, 2, 3, CAP], F32R)
        y_hi, y_lo = [x[:, 2, 0:2].rearrange("p c t -> p (c t)") for x in (br_hi, br_lo)]
        slot_rows = E[:]
        eg, he = gT[:, 0:2, :], gT[:, 2:4, :]
        rot_f = rot[:].rearrange("p k a d -> p (k a d)")
        slot_ids, slot_id, w_slot, most = rot_f[:, 0:CAP], rot_f[:, CAP:CAP + 1], rot_f[:, CAP + 2:CAP + 4], rot_f[:, CAP + 4:CAP + 5]
        later = pT[:, 0:P]
        placed = pT[:].rearrange("p (q t) -> p q t", q=2)
        more = sb("more", [1, 1], I32)
        t5 = o_nat[0:32].rearrange("p s h d -> p (s h d)")[:, 0:512]
        relb = cv[0:32, 0, 0:N_HEADS]
        t5_row = lnb[0:N_HEADS, 2, 0:512]
        nm2, rs2 = sb("nm2", [P, 4, 2]), sb("rs2", [P, 4, 2])
        wi = sb("wi", [P, TT, 8])
        bsT = sb("bsT", [P, 4])
        rb = sb("rb", [P, 36])
        wdesc = sb("wdesc", [P, 8])
        rtT = lnb[0:36, 1, 0:T]
        rt = prm_all[:].rearrange("p l (r c) -> p (l r c)", r=3).rearrange("p (r a c) -> p r a c", r=6, a=TT)
        lg = prm[:, 0:TT * 36].rearrange("p (a c) -> p a c", a=TT)
        comb = prm[:, TT * 36:TT * 68].rearrange("p (a c) -> p a c", a=TT)
        member, pos = rt[:, 5], rt[:, 4]
        rowsT = lamv[0:32].rearrange("p a d -> p (a d)").rearrange("p (k t) -> p k t", k=2)
        z_dram = nc.dram_tensor("z_dram", (N_HEADS, P, 512), F32, kind="Internal")
        rows_dram = nc.dram_tensor("rows_dram", (N_EXPERTS, 2, T), F32, kind="Internal").ap()

        t5_mm, t5_copied, z_stored, late_in, late2_in, late3_in = [sem(x) for x in ("t5_mm", "t5_copied", "z_stored", "late_in", "late2_in", "late3_in")]
        sq_sum, normed, ev2, bank_d = [sem(x) for x in ("sq_sum", "normed", "ev2", "bank_d")]
        ukT_done, ukT_c, ws_masked, wsT_done, wsT_c = [sem(x) for x in ("ukT_done", "ukT_c", "ws_masked", "wsT_done", "wsT_c")]
        kv_normed, kvT_done, kvT_c, ql_done, ql_c = [sem(x) for x in ("kv_normed", "kvT_done", "kvT_c", "ql_done", "ql_c")]
        ix_done, ix_rel, ix_sum, sel_ready, bm_ready = [sem(x) for x in ("ix_done", "ix_rel", "ix_sum", "sel_ready", "bm_ready")]
        gel_poly, gel_th, gel_out, lnv_stat, lnv_hat, lnv_out = [sem(x) for x in (
            "gel_poly", "gel_th", "gel_out", "lnv_stat", "lnv_hat", "lnv_out")]
        sp_done, sp_out, ybT_done, yb_hi, yb_lo = [sem(x) for x in ("sp_done", "sp_out", "ybT_done", "yb_hi", "yb_lo")]
        s2_done, s2_max, s2_exp, s2_prob, t2_done, t2_c, v2_done, v2_c, a2_done, a2_hi, a2_lo = [sem(x) for x in (
            "s2_done", "s2_max", "s2_exp", "s2_prob", "t2_done", "t2_c", "v2_done", "v2_c", "a2_done", "a2_hi", "a2_lo")]
        proj_b, proj_a, pm_hi, pm_lo = [sem(x) for x in ("proj_b", "proj_a", "pm_hi", "pm_lo")]
        rt_copied, rt_back, rt_log, rt_in, rt_exp, comb_ready, rowsT_done, rowsT_c, rows_stored = [sem(x) for x in (
            "rt_copied", "rt_back", "rt_log", "rt_in", "rt_exp", "comb_ready", "rowsT_done", "rowsT_c", "rows_stored")]
        bias_in = [sem(f"bias_in{q}") for q in range(2)]
        rows_in = [sem(f"rows_in{q}") for q in range(2)]
        slots_in, pos_done, pos_ready, more_ready, h2_hid, h2_lod = [sem(x) for x in (
            "slots_in", "pos_done", "pos_ready", "more_ready", "h2_hid", "h2_lod")]
        hi_half, lo_half, picked, gathered, gath_c, put_ready = [sem(x) for x in (
            "hi_half", "lo_half", "picked", "gathered", "gath_c", "put_ready")]
        th_done, g_out, he_ready, heT_done, heT_hid, heT_lod = [sem(x) for x in (
            "th_done", "g_out", "he_ready", "heT_done", "heT_hid", "heT_lod")]
        y_hid, y_lod, scattered = [[sem(f"{x}{h}") for h in range(2)] for x in ("y_hid", "y_lod", "scattered")]
        summed, shifted, zeroed = sem("summed"), sem("shifted"), sem("zeroed")
        dve_link2 = sem("dve_link2")
        raw_in = [sem(f"raw_in{s}") for s in range(RAW)]
        hi_done, split_done, unit_done = sem("hi_done"), sem("split_done"), sem("unit_done")
        evac_a, evac_d = sem("evac_a"), sem("evac_d")
        const_in, bcast_in, x_in, lnb1_in, lnb2_in = sem("const_in"), sem("bcast_in"), sem("x_in"), sem("lnb1_in"), sem("lnb2_in")
        setup_p, rows_T, prm_ready, lam_sum, lam_exp = sem("setup_p"), sem("rows_T"), sem("prm_ready"), sem("lam_sum"), sem("lam_exp")
        xT_done, xT_hid, xT_lod = sem("xT_done"), sem("xT_hid"), sem("xT_lod")
        x_scaled, tile_done, x_out = sem("x_scaled"), sem("tile_done"), sem("x_out")
        rotated, roped, qk_T, qk_copied = sem("rotated"), sem("roped"), sem("qk_T"), sem("qk_copied")
        prm_cur, conv_link = sem("prm_cur"), sem("conv_link")
        csum_done, c_dev, c_sq, c_norm, c_tanh, c_silu, c_hi, c_lo = [sem(x) for x in (
            "csum_done", "c_dev", "c_sq", "c_norm", "c_tanh", "c_silu", "c_hi", "c_lo")]
        score_done, neg_max, exp_done, prob_done = sem("score_done"), sem("neg_max"), sem("exp_done"), sem("prob_done")
        probT_done, probT_copied, pv_done, pv_copied, moba_lo = [sem(x) for x in (
            "probT_done", "probT_copied", "pv_done", "pv_copied", "moba_lo")]
        o_normed, oT_done, oT_hid, oT_lod = sem("o_normed"), sem("oT_done"), sem("oT_hid"), sem("oT_lod")
        mixed, m_hi, m_lo = sem("mixed"), sem("m_hi"), sem("m_lo")
        ff_sq, ff_hi, ff_lo = sem("ff_sq"), sem("ff_hi"), sem("ff_lo")
        dve_link, act_link, pool_link = sem("dve_link"), sem("act_link"), sem("pool_link")
        stored, pool_lo = sem("stored"), sem("pool_lo")

        block = ctx.enter_context(nc.Block())

        def split_counts(g):
            return LAYERS * RAW_INCS[g % RAW] + sum(16 * LOADS.get(v - G2, 1) for v in range(G2 + (g - G2) % RAW, g + 1, RAW))

        def rows(ap, k):
            return ap.rearrange("l (k p) n -> p (l k) n", p=P), k

        w_in, w_in_k = rows(t["w_in"], KC)
        w_br = [rows(t[n], CC)[0] for n in ("w_conv_out", "w_diff_out", "w_moba_out")]
        w_o, w_o_k = rows(t["w_o"], KC)
        w_f1, w_f1_k = rows(t["w_ff1"], KC)
        w_f2, w_f2_k = rows(t["w_ff2"], D_FF // P)

        def unit3(ring, slot, k, n):
            return ring[:, slot, 0:k * n].rearrange("p (k n) -> p k n", k=k)

        def evac_before(u):
            return len([v for v in range(u) if v not in U_QK]), len([v for v in range(u) if v in U_QK])

        EV_A = U_BR - len(U_QK) + FFJ
        EV_D = len(U_QK) + KC
        EV_A_IN = U_BR - len(U_QK)

        def moe_counts(r, i):
            def plus(count, per_round, per_turn):
                v = count if r is None else r * per_round + (count + per_round)
                return v if i is None else i * per_turn + v
            return plus

        def moe_steps(eng, step):
            for p in range(3):
                step(p)
            with eng.Fori(0, (PAIRS - 4) // 2) as i:
                for p in (3, 4):
                    step(p, i)
            step(PAIRS - 1)

        def first_unit(p):
            return 6 * p - 2 if p else 0

        def down_unit(d, h):
            return (6 * d + 8 if d < PAIRS - 1 else ROUND_UNITS - 2) + h

        def latent_steps(w, half):
            slot = 2 * (w - X_S) + half
            order = [("transpose", slot - 2), ("values", slot - 3), ("output", slot - 4)]
            return [(kind, s) for kind, s in order if 0 <= s < 8]

        def latent_task(w, half):
            slot = 2 * (w - X_S) + half
            return slot if 0 <= slot < 8 else None

        def latent_pe(pe, kind, s):
            a, p = s // 4, s % 4
            if kind == "transpose":
                pe.wait_ge(s2_prob, s + 1)
                if s >= 1:
                    pe.wait_ge(t2_c, s)
                for i in range(2):
                    for b in range(a + 1):
                        last = nc.tensor.transpose(ps[:, PT_B, (2 * i + b) * P:(2 * i + b + 1) * P], E2[:, s % 4, i, b * P:(b + 1) * P], ident[:])
                last.then_inc(t2_done, 1)
            elif kind == "values":
                pe.wait_ge(t2_c, s + 1)
                if s >= 1:
                    pe.wait_ge(v2_c, s)
                else:
                    pe.wait_ge(sp_out, TT)
                for i in range(2):
                    for b in range(a + 1):
                        last = nc.tensor.matmul(ps[:, O_B, i * P:(i + 1) * P], ckv[:, b, :], pT[:, (2 * i + b) * P:(2 * i + b + 1) * P], start=b == 0, stop=b == a)
                last.then_inc(v2_done, 1)
            else:
                pe.wait_ge(v2_c, s + 1)
                if s >= 1:
                    pe.wait_ge(a2_lo, s)
                else:
                    pe.wait_ge(yb_lo, 2)
                for i in range(2):
                    last = nc.tensor.matmul(ps[i * HD:(i + 1) * HD, TB, 0:P], w_uv[:, (2 * p + i) * HD:(2 * p + i + 1) * HD], o_lat[:, i, :], start=True, stop=True)
                last.then_inc(a2_done, 1)

        def latent_act(act, kind, s):
            a, p = s // 4, s % 4
            nk = P * (a + 1)
            if kind == "transpose":
                act.wait_ge(t2_done, s + 1)
                if s >= 1:
                    act.wait_ge(v2_done, s)
                nc.scalar.activation(pT[:].rearrange("p (i k) -> p i k", i=2)[:, :, 0:nk],
                                     ps[:, PT_B, :].rearrange("p (i k) -> p i k", i=2)[:, :, 0:nk], ACT.Copy).then_inc(t2_c, 1)
            elif kind == "values":
                act.wait_ge(v2_done, s + 1)
                if s >= 1:
                    act.wait_ge(a2_done, s)
                nc.scalar.activation(o_lat, ps[:, O_B, 0:256].rearrange("p (i q) -> p i q", i=2), ACT.Copy).then_inc(v2_c, 1)
            else:
                act.wait_ge(a2_done, s + 1)
                nc.scalar.activation(br_hi[:, 0, p, a * P:(a + 1) * P], ps[:, TB, 0:P], ACT.Copy).then_inc(a2_hi, 1)

        def latent_dve(dve, kind, s):
            a, p = s // 4, s % 4
            if kind == "output":
                dve.wait_ge(a2_hi, s + 1)
                nc.vector.tensor_tensor(br_lo[:, 0, p, a * P:(a + 1) * P], ps[:, TB, 0:P], br_hi[:, 0, p, a * P:(a + 1) * P].bitcast(F32), ALU.subtract).then_inc(a2_lo, 1)

        @block.sync
        def _(sp):
            sp.dma_start(x_nat[:], t["x"].rearrange("o (a p) d -> p (o a) d", p=P)).then_inc(x_in, 16)

            def load(base, u, dst, src):
                sp.wait_ge(split_done, base + u + 1)
                sp.dma_start(dst, src).then_inc(raw_in[u % RAW], 16)

            with sp.Fori(0, LAYERS) as l:
                base = l * UNITS
                for u in range(U_BR):
                    if u == 2:
                        sp.wait_ge(const_in, CONSTS)
                    load(base, u, unit3(raw, u % RAW, KC, 256), w_in[:, bass.ds(l * KC, KC), u * 256:(u + 1) * 256])
                    if u == 12:
                        sp.wait_ge(x_out, l * 2 * TT + 1)
                        sp.wait_ge(z_stored, 16)
                        for i, name in enumerate(("ln1_g", "ln1_b", "b_ff2")):
                            sp.dma_start(lnb[:, i, :], t[name][bass.ds(l, 1), :].rearrange("o d -> (o d)").partition_broadcast(P)).then_inc(lnb1_in, 16)
                for c in range(KC):
                    u = U_BR + c
                    sp.wait_ge(split_done, base + u + 1)
                    for b in range(3):
                        sp.dma_start(unit3(raw, u % RAW, 12, P)[:, b * CC:(b + 1) * CC, :],
                                     w_br[b][:, bass.ds(l * CC, CC), c * P:(c + 1) * P]).then_inc(raw_in[u % RAW], 16)
                for k in range(4):
                    load(base, U_WO + k, unit3(raw, (U_WO + k) % RAW, 2, D), w_o[:, bass.ds(l * KC + 2 * k, 2), :])

                def ff1(u, j):
                    load(base, u, unit3(raw, u % RAW, KC, 256), w_f1[:, bass.ds(l * KC, KC), bass.ds(j * 256, 256)])

                def ff2(u, j):
                    load(base, u, unit3(raw, u % RAW, 2, D), w_f2[:, bass.ds(l * (D_FF // P) + j * 2, 2), :])

                ff1(U_FF, 0)
                ff1(U_FF + 1, 1)
                ff2(U_FF + 2, 0)
                sp.wait_ge(x_out, l * 2 * TT + TT + 1)
                for i, name in enumerate(("ln2_g", "ln2_b")):
                    sp.dma_start(lnb[:, i, :], t[name][bass.ds(l, 1), :].rearrange("o d -> (o d)").partition_broadcast(P)).then_inc(lnb2_in, 16)
                with sp.Fori(0, FFJ // 2 - 1) as i:
                    for q in range(2):
                        u = U_FF + 3 + 2 * q
                        j = i * 2 + (2 + q)
                        sp.wait_ge(split_done, base + i * 4 + (u + 1))
                        sp.dma_start(unit3(raw, u % RAW, KC, 256), w_f1[:, bass.ds(l * KC, KC), bass.ds(j * 256, 256)]).then_inc(raw_in[u % RAW], 16)
                        sp.wait_ge(split_done, base + i * 4 + (u + 2))
                        sp.dma_start(unit3(raw, (u + 1) % RAW, 2, D), w_f2[:, bass.ds(l * (D_FF // P) + i * 4 + 2 * (1 + q), 2), :]).then_inc(raw_in[(u + 1) % RAW], 16)
                ff2(UNITS - 1, FFJ - 1)

            w2 = t["w_in_2"].rearrange("o (k p) n -> p (o k) n", p=P)

            def load2(w, src, k, n, at=0, m=None):
                m = n if m is None else m
                if at == 0:
                    sp.wait_ge(split_done, G2 + w + 1)
                u = G2 + w
                sp.dma_start(unit3(raw, u % RAW, k, n)[:, :, at:at + m], src).then_inc(raw_in[u % RAW], 16)

            for j in range(2):
                load2(W_QI + j, w2[:, :, O_QI + 256 * j:O_QI + 256 * (j + 1)], KC, 256)
            load2(W_K, w2[:, :, O_KV:O_KV + KV_RANK], KC, K_COLS, 0, KV_RANK)
            load2(W_K, w2[:, :, O_KI:O_KI + 72], KC, K_COLS, KV_RANK, 72)
            for w0, o, n in ((W_Q, O_Q, 2), (W_V, O_V, 2), (W_U, O_U, 2), (W_GA, O_GA, 4), (W_GB, O_GB, 4)):
                for j in range(n):
                    load2(w0 + j, w2[:, :, o + 256 * j:o + 256 * (j + 1)], KC, 256)
            for w0, name in ((W_PB, "w_proj_b_2"), (W_PA, "w_proj_a_2")):
                for j in range(2):
                    load2(w0 + j, t[name].rearrange("o (k p) n -> p (o k) n", p=P)[:, :, 512 * j:512 * (j + 1)], CC, 512)
            for k in range(4):
                load2(W_OUT + k, t["w_out_2"].rearrange("o (k p) n -> p (o k) n", p=P)[:, 2 * k:2 * k + 2, :], 2, D)
            load2(W_R, t["router_group_w_2"].rearrange("o (k p) n -> p (o k) n", p=P), KC, 36, 0, 4)
            load2(W_R, t["router_expert_w_2"].rearrange("o (k p) n -> p (o k) n", p=P), KC, 36, 4, 32)
            e_in = [t[n].rearrange("o e (k p) n -> p (o e k) n", p=P) for n in ("w_gate_2", "w_up_2", "w_down_2")]

            def moe_loads(r):
                def load_e(j, src, i):
                    plus = moe_counts(r, i)
                    u = E0 + j
                    sp.wait_ge(split_done, plus(u + 1, ROUND_UNITS, 12))
                    sp.dma_start(unit3(raw, u % RAW, src.shape[1], src.shape[2]), src).then_inc(raw_in[u % RAW], 16)

                def down_loads(d, j, i=None):
                    for h in range(2):
                        k0 = 4 * d if i is None else bass.ds(i * 8 + 4 * d, 4)
                        load_e(j + h, e_in[2][:, k0 if i is not None else slice(k0, k0 + 4), h * BANK:(h + 1) * BANK], i)

                def step(p, i=None):
                    j = first_unit(p)
                    for kind in range(2):
                        for e in range(2):
                            k0 = (2 * p + e) * KC
                            load_e(j + 2 * kind + e, e_in[kind][:, slice(k0, k0 + KC) if i is None else bass.ds(i * (4 * KC) + k0, KC), :], i)
                    plus = moe_counts(r, i)
                    sp.wait_ge(rows_stored, 16)
                    for e in range(2):
                        if p >= 2 or r is not None:
                            sp.wait_ge(put_ready, plus(p - 1, PAIRS, 2))
                        src = rows_dram[2 * p + e:2 * p + e + 1] if i is None else rows_dram[bass.ds(i * 4 + (2 * p + e), 1)]
                        sp.dma_start(slot_rows[e * CAP:(e + 1) * CAP, p % 2], src.rearrange("o k t -> (o k t)").partition_broadcast(CAP).rearrange("s (k t) -> s k t", k=2)).then_inc(rows_in[p % 2], 16)
                    if p >= 1:
                        down_loads(p - 1, j + 4, i)

                moe_steps(sp, step)
                down_loads(PAIRS - 1, ROUND_UNITS - 2)

            moe_loads(None)
            sp.wait_ge(more_ready, 1)
            with sp.If(sp.value_load(more[0:1, 0:1]) > 0):
                with sp.Fori(0, ROUNDS - 1) as r:
                    moe_loads(r)
            for a in range(TT):
                sp.wait_ge(normed, 2 * TT + a + 1)
                sp.dma_start(out.rearrange("o (a p) d -> p (o a) d", p=P)[:, a, :], x_nat[:, a, :]).then_inc(stored, 16)
            sp.wait_ge(stored, 16 * TT)

        @block.gpsimd
        def _(pool):
            links = [0]

            def link(ins, base=0):
                links[0] += 1
                ins.then_inc(pool_link, 1)
                pool.wait_ge(pool_link, base + links[0])

            nc.gpsimd.memset(hpad[:, :, 0:PAD], 0.0).then_inc(setup_p, 1)
            nc.gpsimd.memset(ones[:], 1.0).then_inc(setup_p, 1)
            for i, name in enumerate(("lam_q1", "lam_k1", "lam_q2", "lam_k2")):
                pool.dma_start(lamv[:, i, :], t[name].rearrange("l d -> (l d)").partition_broadcast(P)).then_inc(bcast_in, 16)
            pool.dma_start(gsub[:].rearrange("p l d -> p (l d)"), t["diff_subln_g"].rearrange("l d -> (l d)").partition_broadcast(P)).then_inc(bcast_in, 16)
            pool.dma_start(linit[:].rearrange("p l d -> p (l d)"), t["c_lam"].rearrange("l d -> (l d)").partition_broadcast(P)).then_inc(bcast_in, 16)
            nc.gpsimd.memset(alpha[:], ALPHA).then_inc(setup_p, 1)
            pool.wait_ge(setup_p, 3)
            alphas = bc(alpha[:], 1, TT).broadcast_to([P, TT, D])
            with pool.Fori(0, LAYERS) as l:
                links[0] = 0
                base = l * POOL_LINKS
                pool.wait_ge(xT_done, l * 8 + 4)
                pool.wait_ge(x_in, 16)
                nc.gpsimd.tensor_tensor(x_nat[:], x_nat[:], alphas, ALU.mult).then_inc(x_scaled, 1)
                for u in range(U_BR):
                    if u in U_QK:
                        n = U_QK.index(u)
                        pool.wait_ge(rotated, l * 8 + n + 1)
                        nc.gpsimd.tensor_tensor(rope[:, n % 2, :], rope[:, n % 2, :], rope[:, 2, :], ALU.add).then_inc(roped, 1)
                    if u + 2 in U_POOL:
                        pool.wait_ge(hi_done, l * UNITS + u + 3)
                        nc.gpsimd.tensor_tensor(w_lo[:, u % SPLIT, :], raw[:, (u + 2) % RAW, :], w_hi[:, u % SPLIT, :].bitcast(F32), ALU.subtract).then_inc(pool_lo, 1)
                for k in range(2):
                    if k == 0:
                        pool.wait_ge(lnb1_in, l * 48 + 48)
                        pool.wait_ge(xT_done, l * 8 + 8)
                        link(nc.gpsimd.tensor_tensor(x_nat[:], x_nat[:], alphas, ALU.mult), base)
                        nc.gpsimd.tensor_tensor(x_nat[:], x_nat[:], bc(lnb[:, 2, :], 1, TT), ALU.add).then_inc(x_scaled, 1)
            assert links[0] == POOL_LINKS

            for i in range(8):
                nc.gpsimd.memset(wdesc[:, i:i + 1], float(8 - i))
            pool.wait_ge(x_out, LAYERS * 2 * TT + 1)
            pool.dma_start(lnb[:, 0, :], t["norm1_g_2"].rearrange("o d -> (o d)").partition_broadcast(P)).then_inc(late_in, 16)
            for dst, name in ((lnb[:, 1, :], "norm2_g_2"), (lnv_g, "ln_v_g_2"), (lnv_b, "ln_v_b_2"), (kvg, "kv_norm_g_2")):
                pool.dma_start(dst, t[name].rearrange("o d -> (o d)").partition_broadcast(P)).then_inc(late2_in, 16)
            pool.dma_start(rb[:, 0:4], t["router_group_b_2"].rearrange("o d -> (o d)").partition_broadcast(P)).then_inc(late2_in, 16)
            pool.dma_start(rb[:, 4:36], t["router_expert_b_2"].rearrange("o d -> (o d)").partition_broadcast(P)).then_inc(late2_in, 16)
            pool.dma_start(ws_nat, t["w_spatial_2"].rearrange("o g i j -> i (o g) j")).then_inc(late2_in, 16)
            pool.dma_start(bsT[:], t["b_spatial_2"].rearrange("o g i -> i (o g)"), allow_slow_non_contiguous=True).then_inc(late2_in, 16)
            pool.wait_ge(xT_done, LAYERS * 8 + 4)
            pool.dma_start(w_uk, t["w_uk_2"].rearrange("o r h d -> (o r) (h d)")).then_inc(late3_in, 16)
            pool.dma_start(w_uv, t["w_uv_2"].rearrange("o r h d -> (o r) (h d)")).then_inc(late3_in, 16)
            pool.wait_ge(late2_in, 8 * 16)
            nc.gpsimd.affine_select(out=ws_nat, in_=ws_nat, compare_op=ALU.is_ge, fill=0.0, base=0,
                                    pattern=[[0, 4], [-1, P]], channel_multiplier=1).then_inc(ws_masked, 1)
            pool.wait_ge(z_stored, 16)

            def bias_load(s):
                a, p = s // 4, s % 4
                if s >= 2:
                    pool.wait_ge(s2_max, s - 1)
                src = bass.AP(z_dram, 2 * p * P * 512 + 255 - a * P, [[511, P], [P * 512, 2], [1, P * (a + 1)]])
                pool.dma_start(bias_t[:, s % 2, :, 0:P * (a + 1)], src).then_inc(bias_in[s % 2], 16)

            bias_load(0)
            for s in range(8):
                if s < 7:
                    bias_load(s + 1)
                nk = P * (s // 4 + 1)
                pool.wait_ge(bias_in[s % 2], 16 * (s // 2 + 1))
                pool.wait_ge(sel_ready, s // 4 + 1)
                b = bias_t[:, s % 2, :, 0:nk]
                nc.gpsimd.tensor_tensor(b, b, bc(selm[:, s // 4, 0:nk], 1, 2), ALU.add).then_inc(bm_ready, 1)
            pool.wait_ge(ql_done, 4)
            pool.dma_start(lnb[:, 0, :], t["final_norm_g_2"].partition_broadcast(P)).then_inc(late_in, 16)
            pool.wait_ge(sp_out, TT)
            pool.dma_start(slot_ids, t["c_slots"].partition_broadcast(P)).then_inc(slots_in, 16)
            for i in range(2):
                pool.dma_start(slot_id[i * CAP:(i + 1) * CAP], t["c_slots"].rearrange("(s o) -> s o", o=1)).then_inc(slots_in, 16)

        @block.scalar
        def _(act):
            links = [0]

            def link(ins, base=0):
                links[0] += 1
                ins.then_inc(act_link, 1)
                act.wait_ge(act_link, base + links[0])

            for dst, src in ((ident[:], t["c_ident"]), (mask[:], t["c_mask"]),
                             (rot[:], t["c_rot"].rearrange("k (a p) d -> p k a d", p=P)),
                             (row_cw, t["conv_w"].rearrange("l k o (c p) -> (k o c) l p", p=P)),
                             (row_v[C_CB:C_CG], t["conv_b"].rearrange("l (c p) -> c l p", p=P)),
                             (row_v[C_CG:C_CBT], t["conv_ln_g"].rearrange("l (c p) -> c l p", p=P)),
                             (row_v[C_CBT:C_GB], t["conv_ln_b"].rearrange("l (c p) -> c l p", p=P)),
                             (row_v[C_GB:C_F1], t["b_gate"].rearrange("l (c p) -> c l p", p=P)),
                             (row_v[C_F1:C_CW], t["b_ff1"].rearrange("l (c p) -> c l p", p=P)),
                             (t5, t["c_t5"]), (relb, t["rel_bias_2"])):
                act.dma_start(dst, src).then_inc(const_in, 16)

            def hi(base, u, n=UCOLS, i=None):
                turn = (base + u) if i is None else (base + i + u)
                act.wait_ge(unit_done, turn + 1)
                nc.scalar.activation(w_hi[:, u % SPLIT, 0:n], raw[:, u % RAW, 0:n], ACT.Copy).then_inc(hi_done, 1)

            for u in range(2):
                act.wait_ge(raw_in[u], 16)
                hi(0, u)
            act.wait_ge(rows_T, 1)
            rows_v = ps[:, 7, :].rearrange("p (l c) -> p l c", l=LAYERS)
            for a, b, scale in ((C_CB, C_CG, 1.0), (C_CG, C_F1, 0.5), (C_F1, C_ALL, 1.0)):
                last = nc.scalar.activation(prm_all[:, :, a:b], rows_v[:, :, a:b], ACT.Copy, scale=scale)
            last.then_inc(prm_ready, 1)
            act.wait_ge(prm_ready, 1)
            act.wait_ge(t5_mm, 1)
            nc.scalar.activation(t5_row, ps[0:N_HEADS, 6, :], ACT.Copy).then_inc(t5_copied, 1)
            act.wait_ge(t5_copied, 1)
            act.dma_start(z_dram.ap(), bc(t5_row, 1, P)).then_inc(z_stored, 16)
            act.wait_ge(lam_sum, 1)
            nc.scalar.activation(lams[:], lams[:], ACT.Exp).then_inc(lam_exp, 1)

            with act.Fori(0, LAYERS) as l:
                links[0] = 0
                base, lbase = l * UNITS, l * ACT_LINKS
                ev = [0]

                def arrived(u, n=16):
                    act.wait_ge(raw_in[u % RAW], l * RAW_INCS[u % RAW] + raw_count(u))

                def split_hi(u):
                    arrived(u)
                    hi(base, u, unit_cols(u))

                def make_xT(k):
                    for b in range(4):
                        act.wait_ge(xT_done, l * 8 + k * 4 + b + 1)
                        nc.scalar.activation(xT_hi[:, 2 * b:2 * b + 2, :], ps[:, ACC + b, :].rearrange("p (c t) -> p c t", c=2), ACT.Copy).then_inc(xT_hid, 1)

                act.wait_ge(x_out, l * 2 * TT + 1)
                nc.scalar.activation(prm[:], prm_all[:, bass.ds(l, 1), :].rearrange("p o c -> p (o c)"), ACT.Copy).then_inc(prm_cur, 1)
                make_xT(0)
                act.wait_ge(prm_cur, l + 1)
                for u in range(U_BR):
                    split_hi(u + 2)
                    bank = ps[:, UB + u % 3, :]
                    two = bank.rearrange("p (c t) -> p c t", c=2)
                    if u not in U_QK:
                        act.wait_ge(unit_done, base + u + 1 + SPLIT_CREDIT)
                    if u < 2:
                        nc.scalar.activation(cv[:, 2 * u:2 * u + 2, :], two, ACT.Copy, scale=0.5).then_inc(evac_a, 1)
                    elif u < 4:
                        nc.scalar.activation(hpad[:, 2 * u - 4:2 * u - 2, PAD:], two, ACT.Tanh, scale=0.5).then_inc(evac_a, 1)
                    elif u in U_V:
                        n = U_V.index(u)
                        nc.scalar.activation(vv[:, n // 2, :, 256 * (n % 2):256 * (n % 2) + 256], two, ACT.Copy).then_inc(evac_a, 1)
                    elif u >= U_GATE:
                        for c in range(2):
                            g = 2 * (u - U_GATE) + c
                            last = nc.scalar.activation(gT[:, g, :], two[:, c, :], ACT.Tanh, scale=0.5, bias=prm[:, C_GB + g:C_GB + g + 1])
                        last.then_inc(evac_a, 1)
                    if u - 2 in U_QK:
                        n = U_QK.index(u - 2)
                        act.wait_ge(qk_T, l * 8 + n + 1)
                        nc.scalar.activation(qkT[:, n // 2, 2 * (n % 2):2 * (n % 2) + 2, :], ps[:, TB, :].rearrange("p (c t) -> p c t", c=2), ACT.Copy).then_inc(qk_copied, 1)
                    s = u - 10
                    if 0 <= s < TASKS:
                        act.wait_ge(neg_max, l * TASKS + s + 1)
                        if s >= 2:
                            act.wait_ge(probT_done, l * TASKS + s - 1)
                        nk = P * (s % 2 + 1)
                        for i in range(2):
                            last = nc.scalar.activation(E[:, s % 2, i, 0:nk], ps[:, i, 0:nk], ACT.Exp,
                                                        bias=nm[:, s % 2, i:i + 1], accum_out=rs[:, s % 2, i:i + 1])
                        last.then_inc(exp_done, 1)
                    s = u - 12
                    if 0 <= s < TASKS:
                        act.wait_ge(probT_done, l * TASKS + s + 1)
                        if s >= 1:
                            act.wait_ge(pv_done, l * TASKS + s)
                        nk = P * (s % 2 + 1)
                        if s < 8:
                            nc.scalar.activation(pT[:, 0:nk], ps[:, PT_B, 0:nk], ACT.Copy).then_inc(probT_copied, 1)
                        else:
                            nc.scalar.activation(pT[:].rearrange("p (i k) -> p i k", i=2)[:, :, 0:nk],
                                                 ps[:, PT_B, :].rearrange("p (i k) -> p i k", i=2)[:, :, 0:nk], ACT.Copy).then_inc(probT_copied, 1)
                    for s in (u - 13,) + ((TASKS - 1,) if u == U_BR - 1 else ()):
                        if not 0 <= s < TASKS:
                            continue
                        a, h = s % 2, (s % 8) // 2
                        act.wait_ge(pv_done, l * TASKS + s + 1)
                        o = ps[:, O_B, 0:P]
                        if s < 8:
                            nc.scalar.activation(o_nat[:, a, h, :], o, ACT.Copy)
                            nc.scalar.activation(junk, o, ACT.Square, accum_out=ss[:, a * 4 + h:a * 4 + h + 1]).then_inc(pv_copied, 1)
                        else:
                            nc.scalar.activation(br_hi[:, 2, h, a * P:(a + 1) * P], o, ACT.Copy).then_inc(pv_copied, 1)
                    if u == 19:
                        act.wait_ge(c_dev, l + 1)
                        nc.scalar.activation(hpad[:, :, PAD:], cv[:], ACT.Square).then_inc(c_sq, 1)
                    if u == 22:
                        act.wait_ge(c_norm, l + 1)
                        for c in range(CC):
                            last = nc.scalar.activation(cv[:, c, :], cv[:, c, :], ACT.Identity, scale=prm[:, C_CG + c:C_CG + c + 1], bias=prm[:, C_CBT + c:C_CBT + c + 1])
                        link(last, lbase)
                        nc.scalar.activation(hpad[:, :, PAD:], cv[:], ACT.Tanh).then_inc(c_tanh, 1)
                    if u == 23:
                        act.wait_ge(c_silu, l + 1)
                        nc.scalar.activation(br_hi[:, 0], cv[:], ACT.Copy).then_inc(c_hi, 1)
                    if u in (24, 25):
                        r = u - 24
                        act.wait_ge(oT_done, l * 2 + r + 1)
                        nc.scalar.activation(br_hi[:, 1, 2 * r:2 * r + 2, :], ps[:, TB, :].rearrange("p (c t) -> p c t", c=2), ACT.Copy).then_inc(oT_hid, 1)
                for c in range(KC):
                    split_hi(U_BR + c + 2)
                    act.wait_ge(mixed, l * KC + c + 1)
                    nc.scalar.activation(xT_hi[:, c, :], mix[:, c % 2, 0, :], ACT.Copy, scale=0.5).then_inc(m_hi, 1)
                for k in range(3):
                    split_hi(U_WO + k + 2)
                split_hi(U_FF + 1)
                make_xT(1)

                def relu(u, j, i=0, j0=0):
                    act.wait_ge(unit_done, base + i * 4 + (u + 1 + SPLIT_CREDIT))
                    for c in range(2):
                        b = prm[:, C_F1 + 2 * j + c:C_F1 + 2 * j + c + 1] if isinstance(j, int) else prm[:, bass.ds(j * 2 + (C_F1 + c), 1)]
                        last = nc.scalar.activation(ff_r[:, j0, c * T:(c + 1) * T], ps[:, 4 + j0, c * T:(c + 1) * T], ACT.Relu, bias=b)
                    last.then_inc(evac_a, 1)

                def square_hi(j, j0):
                    act.wait_ge(ff_sq, l * FFJ + j + 1)
                    nc.scalar.activation(h_hi[:, j0], ff_s[:, j0, :].rearrange("p (c t) -> p c t", c=2), ACT.Copy).then_inc(ff_hi, 1)

                relu(U_FF, 0, 0, 0)
                split_hi(U_FF + 2)
                square_hi(0, 0)
                relu(U_FF + 1, 1, 0, 1)
                split_hi(U_FF + 3)
                square_hi(1, 1)
                split_hi(U_FF + 4)
                with act.Fori(0, FFJ // 2 - 1) as i:
                    for q in range(2):
                        u = U_FF + 3 + 2 * q
                        j = i * 2 + (2 + q)
                        relu(u, j, i, q)
                        for v in (u + 2, u + 3):
                            act.wait_ge(raw_in[v % RAW], l * RAW_INCS[v % RAW] + i * 16 + raw_count(v))
                            hi(base, v, UCOLS, i * 4)
                            if v == u + 2:
                                square_hi(j, q)
                split_hi(UNITS + 1)
            assert links[0] == ACT_LINKS

            def hi2(u, n=UCOLS, i=None):
                if i is None:
                    act.wait_ge(raw_in[u % RAW], split_counts(u))
                else:
                    act.wait_ge(raw_in[u % RAW], i * 48 + split_counts(u))
                hi(0, u, n, None if i is None else i * 12)

            def square_sums(src, k, count):
                for a in range(TT):
                    act.wait_ge(x_out, LAYERS * 2 * TT + 1 + count[a])
                    last = nc.scalar.activation(hn[:, a, :], src[:, a, :], ACT.Square, accum_out=ss[:, a:a + 1])
                last.then_inc(sq_sum, 1)

            def make_xT2(k):
                for b in range(4):
                    act.wait_ge(xT_done, LAYERS * 8 + k * 4 + b + 1)
                    nc.scalar.activation(xT_hi[:, 2 * b:2 * b + 2, :], ps[:, ACC + b, :].rearrange("p (c t) -> p c t", c=2), ACT.Copy).then_inc(xT_hid, 1)

            square_sums(x_nat, 0, (-1, 0))
            make_xT2(0)
            def small(w, half):
                n = 2 * (w - X_IX) + half
                if 0 <= n < 8:
                    nk = P * (n // 4 + 1)
                    act.wait_ge(ix_done, n + 1)
                    if n >= 2:
                        act.wait_ge(ix_sum, n - 1)
                    nc.scalar.activation(rel[:, n % 2, :, 0:nk], ps[:, 2 * (n % 2):2 * (n % 2) + 2, 0:nk], ACT.Relu).then_inc(ix_rel, 1)
                n = 2 * (w - X_QL) + half
                if 0 <= n < 4:
                    act.wait_ge(ql_done, n + 1)
                    nc.scalar.activation(q_latT[:, 2 * n:2 * n + 2, :], ps[:, O_B:O_B + 2, 0:T], ACT.Copy, scale=HD ** -0.5).then_inc(ql_c, 1)
                for kind, s in latent_steps(w, half):
                    latent_act(act, kind, s)

            def exponentials(w, half):
                s = latent_task(w, half)
                if s is not None:
                    act.wait_ge(s2_max, s + 1)
                    nk = P * (s // 4 + 1)
                    for i in range(2):
                        last = nc.scalar.activation(E2[:, s % 4, i, 0:nk], E2[:, s % 4, i, 0:nk], ACT.Exp, bias=nm2[:, s % 4, i:i + 1], accum_out=rs2[:, s % 4, i:i + 1])
                    last.then_inc(s2_exp, 1)

            for w in range(W_PB):
                small(w, 0)
                exponentials(w, 0)
                small(w, 1)
                hi2(G2 + w + 2, W_COLS.get(w + 2, UCOLS))
                exponentials(w, 1)
                bank = ps[:, UB + w % 3, :]
                two = bank.rearrange("p (c t) -> p c t", c=2)
                act.wait_ge(unit_done, G2 + w + 1 + SPLIT_CREDIT)
                if w == W_K:
                    rows = bank.rearrange("p (a c) -> p a c", a=TT)
                    for a in range(TT):
                        nc.scalar.activation(pT[:, a * P:(a + 1) * P], rows[:, a, 0:P], ACT.Square, accum_out=ss[:, 4 + a:5 + a])
                    nc.scalar.activation(ckv, rows[:, :, 0:P], ACT.Copy)
                    for i in range(2):
                        nc.scalar.activation(ki2[:, :, i, :], rows[:, :, P:P + HD], ACT.Copy)
                    nc.scalar.activation(wi[:], rows[:, :, P + HD:K_COLS], ACT.Copy, scale=IDX_SCALE).then_inc(ev2, 1)
                elif w < W_Q:
                    nc.scalar.activation(qiT[:, 2 * (w - W_QI):2 * (w - W_QI) + 2, :], two, ACT.Copy).then_inc(ev2, 1)
                elif w < W_V:
                    nc.scalar.activation(q2T[:, 2 * (w - W_Q):2 * (w - W_Q) + 2, :], two, ACT.Copy).then_inc(ev2, 1)
                elif w < W_GA:
                    n = w - W_V
                    if n >= 1:
                        act.wait_ge(gel_out, n)
                    nc.scalar.activation(gel_s, bank, ACT.Square)
                    nc.scalar.activation(gel_x, bank, ACT.Copy, scale=0.5).then_inc(ev2, 1)
                    act.wait_ge(gel_poly, n + 1)
                    nc.scalar.activation(gel_s, gel_s, ACT.Tanh, scale=2.0 * GELU_C).then_inc(gel_th, 1)
                else:
                    g = 2 * (w - W_GA)
                    nc.scalar.activation(gT[:, g:g + 2, :], two, ACT.Tanh, scale=0.5).then_inc(ev2, 1)
                if w == 0:
                    act.wait_ge(ukT_done, 1)
                    nc.scalar.activation(w_ukT, ps[:, TB, :].rearrange("p (c r) -> p c r", c=4), ACT.Copy).then_inc(ukT_c, 1)
                    act.wait_ge(wsT_done, 1)
                    nc.scalar.activation(wsT, ps[:, O_B, :].rearrange("p (g i) -> p g i", g=4), ACT.Copy).then_inc(wsT_c, 1)
                if w == W_K + 1:
                    act.wait_ge(kvT_done, 1)
                    nc.scalar.activation(ckvT, ps[:, TB, 0:T], ACT.Copy)
                    nc.scalar.activation(kiT, ps[:, TB, T:2 * T], ACT.Copy).then_inc(kvT_c, 1)
                if w == X_LNV:
                    act.wait_ge(lnv_stat, 1)
                    for a in range(TT):
                        last = nc.scalar.activation(vg[:, a, :], vg[:, a, :], ACT.Identity, scale=nw[:, 1, a:a + 1], bias=nmr[:, a:a + 1])
                    last.then_inc(lnv_hat, 1)
                if w in (X_YB, X_YB + 1):
                    r = w - X_YB
                    act.wait_ge(ybT_done, r + 1)
                    nc.scalar.activation(br_hi[:, 1, 2 * r:2 * r + 2, :], ps[:, TB, :].rearrange("p (c t) -> p c t", c=2), ACT.Copy).then_inc(yb_hi, 1)
            for w in range(W_PB, W_OUT):
                hi2(G2 + w + 2, W_COLS.get(w + 2, UCOLS))
                if w >= W_PA:
                    j = w - W_PA
                    act.wait_ge(proj_a, j + 1)
                    nc.scalar.activation(xT_hi[:, 4 * j:4 * j + 4, :], gT[:, 4 * j:4 * j + 4, :], ACT.Copy, scale=0.5).then_inc(pm_hi, 1)
            for w in range(W_OUT, W_OUT + 3):
                hi2(G2 + w + 2, W_COLS.get(w + 2, UCOLS))
            square_sums(x_nat, 1, (1, 2))
            make_xT2(1)
            for a in range(TT):
                last = nc.scalar.activation(h2_hi[:, a, :], hn[:, a, :], ACT.Copy)
            last.then_inc(h2_hid, 1)

            def hi_e(j, r=None, i=None):
                if j >= ROUND_UNITS:
                    return
                plus, u = moe_counts(r, i), E0 + j
                act.wait_ge(raw_in[u % RAW], plus(split_counts(u), 16 * ROUND_UNITS // RAW, 48))
                act.wait_ge(unit_done, plus(u + 1, ROUND_UNITS, 12))
                for half, done in ((slice(0, 1024), hi_half), (slice(1024, UCOLS), hi_done)):
                    nc.scalar.activation(w_hi[:, u % SPLIT, half], raw[:, u % RAW, half], ACT.Copy).then_inc(done, 1)

            hi_e(0)
            act.wait_ge(unit_done, G2 + W_R + 1 + SPLIT_CREDIT)
            act.wait_ge(normed, 2 * TT)
            nc.scalar.activation(rtT, ps[0:36, 7, 0:T], ACT.Copy).then_inc(rt_copied, 1)
            hi_e(1)
            act.wait_ge(rt_in, 1)
            nc.scalar.activation(rt[:, 0, :, 0:4], rt[:, 0, :, 0:4], ACT.Exp).then_inc(rt_exp, 1)
            act.wait_ge(rt_in, 2)
            nc.scalar.activation(rt[:, 2, :, 0:8], rt[:, 2, :, 0:8], ACT.Exp).then_inc(rt_exp, 1)

            act.wait_ge(rowsT_done, 1)
            for x in (xg_hi[:, :, CAP:2 * CAP], xg_lo[:, :, CAP:2 * CAP], heT_hi[:, :, 1, :], heT_lo[:, :, 1, :]):
                last = nc.scalar.activation(x, bc(ident[:, 0:CAP], 1, x.shape[1]), ACT.Copy, scale=0.0)
            last.then_inc(zeroed, 1)
            nc.scalar.activation(rowsT[:, 0], ps[0:32, 6, 0:T], ACT.Copy)
            nc.scalar.activation(rowsT[:, 1], ps[0:32, 6, T:2 * T], ACT.Copy, scale=0.5).then_inc(rowsT_c, 1)
            act.wait_ge(rowsT_c, 1)
            act.dma_start(rows_dram, rowsT).then_inc(rows_stored, 16)

            def moe_round(r):
                def gather_copy(p, g, i=None):
                    act.wait_ge(gathered, moe_counts(r, i)(4 * p + g + 1, 4 * PAIRS, 8))
                    b = ps[:, (4, 5)[g % 2] if p == 0 else 4, :].rearrange("p (c k s) -> p c k s", c=2, k=2)
                    for k in range(2):
                        last = nc.scalar.activation(xg_parts[k][:, 2 * g:2 * g + 2], b[:, :, k, :].rearrange("p c (e s) -> p c e s", e=2), ACT.Copy)
                    last.then_inc(gath_c, 1)

                def y_high(d, h, i=None, j=None):
                    plus = moe_counts(r, i)
                    act.wait_ge(unit_done, plus(E0 + down_unit(d, h) + 1 + SPLIT_CREDIT, ROUND_UNITS, 12))
                    if d + h >= 1:
                        act.wait_ge(scattered[1 - h], plus(d + h, PAIRS, 2))
                    nc.scalar.activation(y_hi, ps[:, Y_BANKS[h], :], ACT.Copy).then_inc(y_hid[h], 1)

                def step(p, i=None):
                    plus, j, q = moe_counts(r, i), first_unit(p), p % 2
                    hi_e(j + 2, r, i)
                    hi_e(j + 3, r, i)
                    act.wait_ge(unit_done, plus(E0 + j + 2 + SPLIT_CREDIT, ROUND_UNITS, 12))
                    nc.scalar.activation(eg[:, q, :], ps[:, 6, 0:T], ACT.Tanh, scale=0.5).then_inc(th_done, 1)
                    hi_e(j + 4, r, i)
                    hi_e(j + 5, r, i)
                    if p < PAIRS - 1:
                        gather_copy(p + 1, 0, i)
                    if p >= 1:
                        y_high(p - 1, 0, i)
                    if p < PAIRS - 1:
                        gather_copy(p + 1, 1, i)
                    if p >= 1:
                        hi_e(j + 6, r, i)
                    if p < PAIRS - 1:
                        gather_copy(p + 1, 2, i)
                    act.wait_ge(heT_done, plus(p + 1, PAIRS, 2))
                    nc.scalar.activation(heT_hi[:, :, 0:3:2, :], ps[:, 6, 0:2 * P].rearrange("p (c e s) -> p c e s", c=2, e=2), ACT.Copy).then_inc(heT_hid, 1)
                    if p < PAIRS - 1:
                        gather_copy(p + 1, 3, i)
                    if p >= 1:
                        y_high(p - 1, 1, i)
                        hi_e(j + 7, r, i)

                if r is not None:
                    hi_e(0, r)
                    hi_e(1, r)
                for g in range(4):
                    gather_copy(0, g)
                moe_steps(act, step)
                y_high(PAIRS - 1, 0)
                y_high(PAIRS - 1, 1)

            moe_round(None)
            act.wait_ge(more_ready, 1)
            with act.If(act.value_load(more[0:1, 0:1]) > 0):
                with act.Fori(0, ROUNDS - 1) as r:
                    moe_round(r)
            square_sums(x_nat, 2, (3, 3))

        @block.vector
        def _(dve):
            links = [0]

            def link(ins, base=0):
                links[0] += 1
                ins.then_inc(dve_link, 1)
                dve.wait_ge(dve_link, base + links[0])

            def rsqrt(v, y, z, base):
                link(nc.vector.tensor_scalar(y.bitcast(I32), v.bitcast(I32), -0.5, float(0x5F3759DF), ALU.mult, ALU.add), base)
                for _ in range(3):
                    link(nc.vector.tensor_tensor(z, y, y, ALU.mult), base)
                    link(nc.vector.scalar_tensor_tensor(out=z, in0=z, scalar=-0.5, in1=v, op0=ALU.mult, op1=ALU.mult), base)
                    link(nc.vector.scalar_tensor_tensor(out=y, in0=z, scalar=1.5, in1=y, op0=ALU.add, op1=ALU.mult), base)

            def split(base, u, n=UCOLS, i=None):
                turn = (base + u) if i is None else (base + i + u)
                dve.wait_ge(hi_done, turn + 1)
                nc.vector.tensor_tensor(w_lo[:, u % SPLIT, 0:n], raw[:, u % RAW, 0:n], w_hi[:, u % SPLIT, 0:n].bitcast(F32), ALU.subtract).then_inc(split_done, 1)

            dve.sem_inc(split_done, RAW_CREDIT)
            split(0, 0)
            dve.wait_ge(setup_p, 2)
            dve.wait_ge(const_in, CONSTS)
            dve.wait_ge(bcast_in, BCASTS)
            pairs = lamv[:].rearrange("p (a b) d -> p b a d", b=2)
            link(nc.vector.tensor_tensor(pairs[:, 0], pairs[:, 0], pairs[:, 1], ALU.mult))
            nc.vector.tensor_reduce(lams[:], pairs[:, 0].rearrange("p a (l d) -> p a l d", l=LAYERS), AX.X, ALU.add).then_inc(lam_sum, 1)
            for i in range(LAYERS):
                nc.vector.tensor_scalar(gsub[:, i, :], gsub[:, i, :], linit[:, 1, i:i + 1], None, ALU.mult)
            dve.wait_ge(lam_exp, 1)
            link(nc.vector.tensor_tensor(nlam[:], lams[:, 1, :], lams[:, 0, :], ALU.subtract))
            link(nc.vector.tensor_tensor(nlam[:], nlam[:], linit[:, 0, :], ALU.subtract))
            first_links = links[0]

            with dve.Fori(0, LAYERS) as l:
                links[0] = first_links
                base, lbase = l * UNITS, l * DVE_LINKS
                def conv_taps(u):
                    return min(len(conv), sum(7 if v in U_QK else 10 for v in range(4, u)))

                conv = [(k, c) for k in range(CONV_W) for c in range(CC)]

                def make_xT(k):
                    for b in range(4):
                        dve.wait_ge(xT_hid, l * 8 + k * 4 + b + 1)
                        nc.vector.tensor_tensor(xT_lo[:, 2 * b:2 * b + 2, :], ps[:, ACC + b, :].rearrange("p (c t) -> p c t", c=2),
                                                xT_hi[:, 2 * b:2 * b + 2, :].bitcast(F32), ALU.subtract).then_inc(xT_lod, 1)

                def layer_norm(k, u):
                    dve.wait_ge(x_scaled, l * 2 + k + 1)
                    for a in range(TT):
                        if a == 0:
                            dve.wait_ge(tile_done, l * 2 + k + 1)
                        else:
                            dve.wait_ge(unit_done, base + u + 1 + SPLIT_CREDIT)
                        for h in range(2):
                            cols = slice(h * BANK, (h + 1) * BANK)
                            last = nc.vector.tensor_tensor(x_nat[:, a, cols], x_nat[:, a, cols], ps[:, ACC + 2 * a + h, :], ALU.add)
                        link(last, lbase)
                        for h in range(2):
                            last = nc.vector.bn_stats(st[:, a, h, :], x_nat[:, a, h * BANK:(h + 1) * BANK])
                    link(last, lbase)
                    nc.vector.memset(nw[:, 2, 0:1], 0.0)
                    for a in range(TT):
                        last = nc.vector.bn_aggr(mv[:, a, :], st[:, a].rearrange("p h s -> p (h s)"))
                    link(last, lbase)
                    link(nc.vector.tensor_scalar(nw[:, 0, 0:TT], mv[:, :, 1], LN_EPS, None, ALU.add), lbase)
                    rsqrt(nw[:, 0, 0:TT], nw[:, 1, 0:TT], nw[:, 2, 0:TT], lbase)
                    if k == 0:
                        dve.wait_ge(lnb1_in, l * 48 + 48)
                    else:
                        dve.wait_ge(lnb2_in, l * 32 + 32)
                    for a in range(TT):
                        link(nc.vector.scalar_tensor_tensor(out=x_nat[:, a, :], in0=x_nat[:, a, :], scalar=mv[:, a, 0:1], in1=lnb[:, 0, :], op0=ALU.subtract, op1=ALU.mult), lbase)
                        nc.vector.scalar_tensor_tensor(out=x_nat[:, a, :], in0=x_nat[:, a, :], scalar=nw[:, 1, a:a + 1], in1=lnb[:, 1, :], op0=ALU.mult, op1=ALU.add).then_inc(x_out, 1)

                make_xT(0)
                split(base, 1)
                dve.wait_ge(prm_cur, l + 1)
                for u in range(U_BR):
                    if u + 2 not in U_POOL:
                        split(base, u + 2, unit_cols(u + 2))
                    s = u - 11
                    if 0 <= s < TASKS:
                        nk = P * (s % 2 + 1)
                        e = E[:, s % 2, :, 0:nk]
                        dve.wait_ge(exp_done, l * TASKS + s + 1)
                        link(nc.vector.reciprocal(rr[:], rs[:, s % 2, :]), lbase)
                        if s < 8:
                            link(nc.vector.tensor_tensor(rr[:, 1:2], rr[:, 1:2], nlam[:, bass.ds(l, 1)], ALU.mult), lbase)
                            link(nc.vector.tensor_scalar(e[:, 1], e[:, 1], rr[:, 1:2], None, ALU.mult), lbase)
                            nc.vector.scalar_tensor_tensor(out=e[:, 0], in0=e[:, 0], scalar=rr[:, 0:1], in1=e[:, 1], op0=ALU.mult, op1=ALU.add).then_inc(prob_done, 1)
                        else:
                            nc.vector.tensor_tensor(e, e, bc(rr[:], 2, nk), ALU.mult).then_inc(prob_done, 1)
                    s = u - 10
                    if 0 <= s < TASKS:
                        dve.wait_ge(score_done, l * TASKS + s + 1)
                        nk = P * (s % 2 + 1)
                        diag = ps[:, 0:2, nk - P:nk]
                        link(nc.vector.tensor_tensor(diag, diag, bc(mask[:], 1, 2), ALU.add), lbase)
                        nc.vector.tensor_reduce(nm[:, s % 2, :], ps[:, 0:2, 0:nk], AX.X, ALU.max, negate=True).then_inc(neg_max, 1)
                    if u in (2, 3):
                        dve.wait_ge(evac_a, l * EV_A + u + 1)
                        cs = slice(2 * u - 4, 2 * u - 2)
                        link(nc.vector.scalar_tensor_tensor(out=hpad[:, cs, PAD:], in0=hpad[:, cs, PAD:], scalar=1.0, in1=cv[:, cs, :], op0=ALU.add, op1=ALU.mult), lbase)
                    if u in U_QK:
                        n = U_QK.index(u)
                        q = 0 if n // 2 in (0, 2) else 2
                        x = ps[:, UB + u % 3, :].rearrange("p (a h d) -> p a h d", a=TT, d=HD)
                        r1 = rope[:, n % 2, :].rearrange("p (a h d) -> p a h d", a=TT, d=HD)
                        r2 = rope[:, 2, :].rearrange("p (a h d) -> p a h d", a=TT, d=HD)
                        dve.wait_ge(unit_done, base + u + 1 + SPLIT_CREDIT)
                        if n >= 2:
                            dve.wait_ge(qk_T, l * 8 + n - 1)
                        if n >= 1:
                            dve.wait_ge(roped, l * 8 + n)
                        half = HD // 2
                        for a in range(TT):
                            nc.vector.tensor_tensor(r1[:, a], x[:, a], bc(rot[:, q, a, :], 1, 4), ALU.mult)
                            nc.vector.tensor_tensor(r2[:, a, :, 0:half], x[:, a, :, half:HD], bc(rot[:, q + 1, a, 0:half], 1, 4), ALU.mult)
                            last = nc.vector.tensor_tensor(r2[:, a, :, half:HD], x[:, a, :, 0:half], bc(rot[:, q + 1, a, half:HD], 1, 4), ALU.mult)
                        last.then_inc(rotated, 1)
                    for n in range(conv_taps(u), conv_taps(u + 1)):
                        k, c = conv[n]
                        w = prm[:, C_CW + n:C_CW + n + 1]
                        if k == 0:
                            nc.vector.tensor_scalar(cv[:, c, :], hpad[:, c, 0:T], w, prm[:, C_CB + c:C_CB + c + 1], ALU.mult, ALU.add).then_inc(conv_link, 1)
                        else:
                            dve.wait_ge(conv_link, l * len(conv) + n - CC + 1)
                            nc.vector.scalar_tensor_tensor(out=cv[:, c, :], in0=hpad[:, c, k:k + T], scalar=w, in1=cv[:, c, :], op0=ALU.mult, op1=ALU.add).then_inc(conv_link, 1)
                    for s in (u - 13,) + ((TASKS - 1,) if u == U_BR - 1 else ()):
                        if 8 <= s < TASKS:
                            a, h = s % 2, (s % 8) // 2
                            dve.wait_ge(pv_copied, l * TASKS + s + 1)
                            nc.vector.tensor_tensor(br_lo[:, 2, h, a * P:(a + 1) * P], ps[:, O_B, 0:P],
                                                    br_hi[:, 2, h, a * P:(a + 1) * P].bitcast(F32), ALU.subtract).then_inc(moba_lo, 1)
                    if u + 2 in U_POOL:
                        dve.wait_ge(pool_lo, l * len(U_POOL) + U_POOL.index(u + 2) + 1)
                        nc.vector.memset(counted[:], 0.0).then_inc(split_done, 1)
                    if u == 19:
                        dve.wait_ge(csum_done, l * 2 + 1)
                        nc.vector.scalar_tensor_tensor(out=cv[:], in0=bc(ps[:, TB, 0:T], 1, CC), scalar=-1.0 / CONV_CH, in1=cv[:], op0=ALU.mult, op1=ALU.add).then_inc(c_dev, 1)
                    if u == 21:
                        dve.wait_ge(csum_done, l * 2 + 2)
                        v, y, z = (rope[:, 0, 0:T], rope[:, 1, 0:T], rope[:, 2, 0:T])
                        link(nc.vector.tensor_scalar(v, ps[:, TB, T:2 * T], 1.0 / CONV_CH, LN_EPS, ALU.mult, ALU.add), lbase)
                        rsqrt(v, y, z, lbase)
                        nc.vector.tensor_tensor(cv[:], cv[:], bc(y, 1, CC), ALU.mult).then_inc(c_norm, 1)
                    if u == 23:
                        dve.wait_ge(c_tanh, l + 1)
                        nc.vector.scalar_tensor_tensor(out=cv[:], in0=hpad[:, :, PAD:], scalar=1.0, in1=cv[:], op0=ALU.add, op1=ALU.mult).then_inc(c_silu, 1)
                    if u == 24:
                        dve.wait_ge(c_hi, l + 1)
                        nc.vector.tensor_tensor(br_lo[:, 0], cv[:], br_hi[:, 0].bitcast(F32), ALU.subtract).then_inc(c_lo, 1)
                    if u == 22:
                        dve.wait_ge(pv_copied, l * TASKS + 8)
                        link(nc.vector.tensor_scalar(nw[:, 0, :], ss[:], 1.0 / P, LN_EPS, ALU.mult, ALU.add), lbase)
                        rsqrt(nw[:, 0, :], nw[:, 1, :], nw[:, 2, :], lbase)
                        heads = o_nat[:].rearrange("p a h d -> p (a h) d")
                        link(nc.vector.tensor_tensor(heads, heads, bc(nw[:, 1, :], 2, P), ALU.mult), lbase)
                        nc.vector.tensor_tensor(heads, heads, bc(gsub[:, bass.ds(l, 1), :].rearrange("p o d -> p (o d)"), 1, 8), ALU.mult).then_inc(o_normed, 1)
                    if u in (24, 25):
                        r = u - 24
                        dve.wait_ge(oT_hid, l * 2 + r + 1)
                        nc.vector.tensor_tensor(br_lo[:, 1, 2 * r:2 * r + 2, :], ps[:, TB, :].rearrange("p (c t) -> p c t", c=2),
                                                br_hi[:, 1, 2 * r:2 * r + 2, :].bitcast(F32), ALU.subtract).then_inc(oT_lod, 1)

                def mixed_lo(c):
                    dve.wait_ge(m_hi, l * KC + c + 1)
                    nc.vector.scalar_tensor_tensor(out=xT_lo[:, c, :], in0=mix[:, c % 2, 0, :], scalar=0.5, in1=xT_hi[:, c, :].bitcast(F32), op0=ALU.mult, op1=ALU.subtract).then_inc(m_lo, 1)

                for c in range(KC):
                    u = U_BR + c
                    dve.wait_ge(unit_done, base + u + 1 + SPLIT_CREDIT)
                    if c >= 2:
                        dve.wait_ge(m_lo, l * KC + c - 1)
                    m = mix[:, c % 2]
                    b0 = 4 + 2 * (c % 2)
                    ys = (ps[:, b0, 0:T], ps[:, b0, T:2 * T], ps[:, b0 + 1, 0:T])
                    for b in range(3):
                        last = nc.vector.scalar_tensor_tensor(out=m[:, b, :], in0=gT[:, b * KC + c, :], scalar=1.0, in1=ys[b], op0=ALU.add, op1=ALU.mult)
                    last.then_inc(evac_d, 1)
                    split(base, u + 2, unit_cols(u + 2))
                    dve.wait_ge(evac_d, l * KC + c + 1)
                    link(nc.vector.tensor_tensor(m[:, 0, :], m[:, 0, :], m[:, 1, :], ALU.add), lbase)
                    nc.vector.tensor_tensor(m[:, 0, :], m[:, 0, :], m[:, 2, :], ALU.add).then_inc(mixed, 1)
                    if c >= 1:
                        mixed_lo(c - 1)
                mixed_lo(KC - 1)
                for k in range(3):
                    split(base, U_WO + k + 2, UCOLS)
                layer_norm(0, U_WO + 3)
                make_xT(1)
                split(base, U_FF + 1)

                def square(j, j0):
                    if not isinstance(j, int):
                        dve.wait_ge(ff_lo, l * FFJ + j - 1)
                    dve.wait_ge(evac_a, l * EV_A + EV_A_IN + j + 1)
                    nc.vector.tensor_tensor(ff_s[:, j0, :], ff_r[:, j0, :], ff_r[:, j0, :], ALU.mult).then_inc(ff_sq, 1)

                def square_lo(j, j0):
                    dve.wait_ge(ff_hi, l * FFJ + j + 1)
                    nc.vector.tensor_tensor(h_lo[:, j0], ff_s[:, j0, :].rearrange("p (c t) -> p c t", c=2), h_hi[:, j0].bitcast(F32), ALU.subtract).then_inc(ff_lo, 1)

                for j in range(2):
                    square(j, j)
                    split(base, U_FF + 2 + j)
                    square_lo(j, j)
                split(base, U_FF + 4)
                with dve.Fori(0, FFJ // 2 - 1) as i:
                    for q in range(2):
                        u = U_FF + 3 + 2 * q
                        j = i * 2 + (2 + q)
                        square(j, q)
                        split(base, u + 2, UCOLS, i * 4)
                        square_lo(j, q)
                        split(base, u + 3, UCOLS, i * 4)
                layer_norm(1, UNITS - 1)
            assert links[0] == first_links + DVE_LINKS, links[0] - first_links

            n2 = [0]

            def then(ins):
                n2[0] += 1
                ins.then_inc(dve_link2, 1)
                dve.wait_ge(dve_link2, n2[0])

            def rsqrt2(v, y, z):
                then(nc.vector.tensor_scalar(y.bitcast(I32), v.bitcast(I32), -0.5, float(0x5F3759DF), ALU.mult, ALU.add))
                for _ in range(3):
                    then(nc.vector.tensor_tensor(z, y, y, ALU.mult))
                    then(nc.vector.scalar_tensor_tensor(out=z, in0=z, scalar=-0.5, in1=v, op0=ALU.mult, op1=ALU.mult))
                    then(nc.vector.scalar_tensor_tensor(out=y, in0=z, scalar=1.5, in1=y, op0=ALU.add, op1=ALU.mult))

            def split2(u, n=UCOLS, i=None):
                split(0, u, n, None if i is None else i * 12)

            def rms_rows(k, dst, gain):
                dve.wait_ge(sq_sum, k + 1)
                then(nc.vector.tensor_scalar(nw[:, 0, 0:TT], ss[:, 0:TT], 1.0 / D, EPS, ALU.mult, ALU.add))
                rsqrt2(nw[:, 0, 0:TT], nw[:, 1, 0:TT], nw[:, 2, 0:TT])
                if k == 0:
                    dve.wait_ge(late_in, 16)
                elif k == 1:
                    dve.wait_ge(late2_in, 8 * 16)
                else:
                    dve.wait_ge(late_in, 32)
                for a in range(TT):
                    nc.vector.scalar_tensor_tensor(out=dst[:, a, :], in0=x_nat[:, a, :], scalar=nw[:, 1, a:a + 1], in1=gain, op0=ALU.mult, op1=ALU.mult).then_inc(normed, 1)

            def make_xT2(k):
                for b in range(4):
                    dve.wait_ge(xT_hid, LAYERS * 8 + k * 4 + b + 1)
                    nc.vector.tensor_tensor(xT_lo[:, 2 * b:2 * b + 2, :], ps[:, ACC + b, :].rearrange("p (c t) -> p c t", c=2),
                                            xT_hi[:, 2 * b:2 * b + 2, :].bitcast(F32), ALU.subtract).then_inc(xT_lod, 1)

            def add_product(u):
                for a in range(TT):
                    if a == 0:
                        dve.wait_ge(tile_done, 2 * LAYERS + 1)
                    else:
                        dve.wait_ge(unit_done, u + 1 + SPLIT_CREDIT)
                    for h in range(2):
                        cols = slice(h * BANK, (h + 1) * BANK)
                        last = nc.vector.tensor_tensor(x_nat[:, a, cols], x_nat[:, a, cols], ps[:, ACC + 2 * a + h, :], ALU.add)
                    last.then_inc(x_out, 1)

            def top_keys(a, part):
                nk = P * (a + 1)
                x, work, tmp, m8 = idx[:, a, 0:nk], cv[:, 2, 0:nk], cv[:, 3, 0:nk], nw[:, 0, :]
                diag = x[:, nk - P:nk]
                if part == 0:
                    then(nc.vector.tensor_tensor(diag, diag, mask[:], ALU.add))
                    then(nc.vector.max(m8, x))
                    then(nc.vector.match_replace(work, m8, x, -3.0e38))
                if part < 2:
                    for r in range(TOPK // 16 - 1):
                        then(nc.vector.max(m8, work))
                        then(nc.vector.match_replace(work, m8, work, -3.0e38))
                    return
                then(nc.vector.max(m8, work))
                least = m8[:, 7:8]
                then(nc.vector.tensor_scalar(tmp, x, least, None, ALU.is_gt))
                then(nc.vector.tensor_reduce(rr[:, 0:1], tmp, AX.X, ALU.add))
                then(nc.vector.tensor_scalar(rr[:, 1:2], rr[:, 0:1], -1.0, float(TOPK), ALU.mult, ALU.add))
                then(nc.vector.tensor_scalar(work, x, least, None, ALU.is_equal))
                sel = selm[:, a, 0:nk]
                then(nc.vector.tensor_tensor_scan(sel, ones[:, 0:1].broadcast_to([P, nk]), work, 0.0, ALU.mult, ALU.add))
                then(nc.vector.scalar_tensor_tensor(out=work, in0=sel, scalar=rr[:, 1:2], in1=work, op0=ALU.is_le, op1=ALU.mult))
                then(nc.vector.tensor_tensor(tmp, tmp, work, ALU.add))
                then(nc.vector.tensor_scalar(sel, tmp, -NEG, NEG, ALU.mult, ALU.add))
                nc.vector.tensor_tensor(sel[:, nk - P:nk], sel[:, nk - P:nk], mask[:], ALU.add).then_inc(sel_ready, 1)

            rms_rows(0, hn, lnb[:, 0, :])
            make_xT2(0)
            split2(G2 + 1)
            def probabilities(s):
                nk = P * (s // 4 + 1)
                e = E2[:, s % 4, :, 0:nk]
                dve.wait_ge(s2_exp, s + 1)
                then(nc.vector.reciprocal(rs2[:, s % 4, :], rs2[:, s % 4, :]))
                nc.vector.tensor_tensor(e, e, bc(rs2[:, s % 4, :], 2, nk), ALU.mult).then_inc(s2_prob, 1)

            def small(w, half):
                n = 2 * (w - X_IX) + half
                if 0 <= n < 8:
                    a, p = n // 4, n % 4
                    nk = P * (a + 1)
                    dve.wait_ge(ix_rel, n + 1)
                    for i in range(2):
                        wt = wi[:, a, 2 * p + i:2 * p + i + 1]
                        if p == 0 and i == 0:
                            then(nc.vector.tensor_scalar(idx[:, a, 0:nk], rel[:, n % 2, i, 0:nk], wt, None, ALU.mult))
                        else:
                            then(nc.vector.scalar_tensor_tensor(out=idx[:, a, 0:nk], in0=rel[:, n % 2, i, 0:nk], scalar=wt, in1=idx[:, a, 0:nk], op0=ALU.mult, op1=ALU.add))
                    nc.vector.memset(nw[:, 2, 7:8], 0.0).then_inc(ix_sum, 1)
                for kind, s in latent_steps(w, half):
                    latent_dve(dve, kind, s)
                s = latent_task(w, half)
                if s is not None and s >= 1:
                    probabilities(s - 1)
                if s is not None:
                    nk = P * (s // 4 + 1)
                    e = E2[:, s % 4, :, 0:nk]
                    dve.wait_ge(s2_done, s + 1)
                    dve.wait_ge(bm_ready, s + 1)
                    if s >= 4:
                        dve.wait_ge(t2_done, s - 3)
                    then(nc.vector.tensor_tensor(e, ps[:, s % 2, :].rearrange("p (i k) -> p i k", i=2)[:, :, 0:nk], bias_t[:, s % 2, :, 0:nk], ALU.add))
                    nc.vector.tensor_reduce(nm2[:, s % 4, :], e, AX.X, ALU.max, negate=True).then_inc(s2_max, 1)
                if (w, half) == (X_S + 4, 0):
                    probabilities(7)

            for w in range(W_PB):
                if w == W_K + 1:
                    dve.wait_ge(ev2, W_K + 1)
                    dve.wait_ge(late2_in, 8 * 16)
                    then(nc.vector.tensor_scalar(nw[:, 0, 0:TT], ss[:, 4:4 + TT], 1.0 / KV_RANK, EPS, ALU.mult, ALU.add))
                    rsqrt2(nw[:, 0, 0:TT], nw[:, 1, 0:TT], nw[:, 2, 0:TT])
                    for a in range(TT):
                        last = nc.vector.scalar_tensor_tensor(out=ckv[:, a, :], in0=ckv[:, a, :], scalar=nw[:, 1, a:a + 1], in1=kvg, op0=ALU.mult, op1=ALU.mult)
                    last.then_inc(kv_normed, 1)
                small(w, 0)
                small(w, 1)
                split2(G2 + w + 2, W_COLS.get(w + 2, UCOLS))
                if W_V <= w < W_GA:
                    n = w - W_V
                    dve.wait_ge(ev2, w + 1)
                    then(nc.vector.tensor_scalar(gel_s, gel_s, 0.044715, 1.0, ALU.mult, ALU.add))
                    nc.vector.tensor_tensor(gel_s, gel_s, gel_x, ALU.mult).then_inc(gel_poly, 1)
                    dst = (vg, ug)[n // 2][:, :, 256 * (n % 2):256 * (n % 2) + 256]
                    dve.wait_ge(gel_th, n + 1)
                    nc.vector.scalar_tensor_tensor(out=dst, in0=gel_s.rearrange("p (a c) -> p a c", a=TT), scalar=1.0,
                                                   in1=gel_x.rearrange("p (a c) -> p a c", a=TT), op0=ALU.add, op1=ALU.mult).then_inc(gel_out, 1)
                if w == W_U:
                    dve.wait_ge(gel_out, 2)
                    for a in range(TT):
                        last = nc.vector.bn_stats(st[:, a, 0, :], vg[:, a, :])
                    then(last)
                    for a in range(TT):
                        last = nc.vector.bn_aggr(mv[:, a, :], st[:, a, 0, :])
                    then(last)
                    then(nc.vector.tensor_scalar(nw[:, 0, 0:TT], mv[:, :, 1], EPS, None, ALU.add))
                    rsqrt2(nw[:, 0, 0:TT], nw[:, 1, 0:TT], nw[:, 2, 0:TT])
                    nc.vector.scalar_tensor_tensor(out=nmr[:], in0=mv[:, :, 0], scalar=-1.0, in1=nw[:, 1, 0:TT], op0=ALU.mult, op1=ALU.mult).then_inc(lnv_stat, 1)
                if w == X_LNV:
                    dve.wait_ge(lnv_hat, 1)
                    then(nc.vector.tensor_tensor(vg, vg, bc(lnv_g, 1, TT), ALU.mult))
                    nc.vector.tensor_tensor(vg, vg, bc(lnv_b, 1, TT), ALU.add).then_inc(lnv_out, 1)
                if 0 <= w - X_TOP < 6:
                    top_keys((w - X_TOP) // 3, (w - X_TOP) % 3)
                if w == X_SP:
                    for a in range(TT):
                        dve.wait_ge(sp_done, a + 1)
                        for g in range(4):
                            cols = slice(g * P, (g + 1) * P)
                            last = nc.vector.scalar_tensor_tensor(out=ug[:, a, cols], in0=ps[:, (TB, O_B)[a], cols], scalar=bsT[:, g:g + 1], in1=ug[:, a, cols], op0=ALU.add, op1=ALU.mult)
                        last.then_inc(sp_out, 1)
                if w in (X_YB, X_YB + 1):
                    r = w - X_YB
                    dve.wait_ge(yb_hi, r + 1)
                    nc.vector.tensor_tensor(br_lo[:, 1, 2 * r:2 * r + 2, :], ps[:, TB, :].rearrange("p (c t) -> p c t", c=2),
                                            br_hi[:, 1, 2 * r:2 * r + 2, :].bitcast(F32), ALU.subtract).then_inc(yb_lo, 1)
            for w in range(W_PB, W_OUT):
                dve.wait_ge(unit_done, G2 + w + 1 + SPLIT_CREDIT)
                j = (w - W_PB) % 2
                c0 = 4 * j + (8 if w < W_PA else 0)
                for r in range(2):
                    g = gT[:, c0 + 2 * r:c0 + 2 * r + 2, :]
                    y = ps[:, PROJ_BANKS[j][r], :].rearrange("p (c t) -> p c t", c=2)
                    last = nc.vector.scalar_tensor_tensor(out=g, in0=g, scalar=1.0, in1=y, op0=ALU.add, op1=ALU.mult)
                last.then_inc(proj_b if w < W_PA else bank_d, 1)
                if w < W_PA:
                    split2(G2 + w + 2)
                else:
                    dve.wait_ge(bank_d, j + 1)
                    m, other = gT[:, 4 * j:4 * j + 4, :], gT[:, 8 + 4 * j:8 + 4 * j + 4, :]
                    nc.vector.tensor_tensor(m, m, other, ALU.add).then_inc(proj_a, 1)
                    split2(G2 + w + 2)
                    dve.wait_ge(pm_hi, j + 1)
                    nc.vector.scalar_tensor_tensor(out=xT_lo[:, 4 * j:4 * j + 4, :], in0=m, scalar=0.5, in1=xT_hi[:, 4 * j:4 * j + 4, :].bitcast(F32), op0=ALU.mult, op1=ALU.subtract).then_inc(pm_lo, 1)
            for w in range(W_OUT, W_OUT + 3):
                split2(G2 + w + 2, W_COLS.get(w + 2, UCOLS))
            add_product(G2 + W_OUT + 3)
            rms_rows(1, hn, lnb[:, 1, :])
            make_xT2(1)
            dve.wait_ge(h2_hid, 1)
            nc.vector.tensor_tensor(h2_lo, hn, h2_hi.bitcast(F32), ALU.subtract).then_inc(h2_lod, 1)

            def lo_e(j, r=None, i=None):
                if j >= ROUND_UNITS:
                    return
                plus, u = moe_counts(r, i), E0 + j
                for half, ready, number, done in ((slice(0, 1024), hi_half, j + 1, lo_half), (slice(1024, UCOLS), hi_done, u + 1, split_done)):
                    dve.wait_ge(ready, plus(number, ROUND_UNITS, 12))
                    nc.vector.tensor_tensor(w_lo[:, u % SPLIT, half], raw[:, u % RAW, half], w_hi[:, u % SPLIT, half].bitcast(F32), ALU.subtract).then_inc(done, 1)

            dve.wait_ge(rt_back, 1)
            nc.vector.tensor_tensor(lg, ps[:, 5, 0:72].rearrange("p (a c) -> p a c", a=TT), bc(rb[:], 1, TT), ALU.add).then_inc(rt_log, 1)
            dve.wait_ge(rt_log, 1)
            col = [st[:, :, 0, i] for i in range(6)]

            def over(x, n):
                return bc(x, 2, n)

            def first_of(out_, x, top, n, tmp):
                then(nc.vector.tensor_tensor(tmp, x, over(top, n), ALU.is_equal))
                then(nc.vector.tensor_tensor(tmp, tmp, bc(wdesc[:, 0:n], 1, TT), ALU.mult))
                then(nc.vector.tensor_reduce(col[5], tmp, AX.X, ALU.max))
                then(nc.vector.tensor_tensor(out_, tmp, over(col[5], n), ALU.is_equal))

            gl, ge = lg[:, :, 0:4], rt[:, 0, :, 0:4]
            then(nc.vector.tensor_reduce(col[0], gl, AX.X, ALU.max))
            nc.vector.tensor_tensor(ge, gl, over(col[0], 4), ALU.subtract).then_inc(rt_in, 1)
            dve.wait_ge(rt_exp, 1)
            then(nc.vector.tensor_reduce(col[1], ge, AX.X, ALU.add))
            then(nc.vector.reciprocal(col[1], col[1]))
            then(nc.vector.tensor_tensor(ge, ge, over(col[1], 4), ALU.mult))
            then(nc.vector.tensor_reduce(col[1], ge, AX.X, ALU.max))
            oh = rt[:, 1, :, 0:4]
            first_of(oh, ge, col[1], 4, rt[:, 3, :, 0:4])
            prod = rt[:, 4]
            el = lg[:, :, 4:36]
            for a in range(TT):
                last = nc.vector.tensor_tensor(prod[:, a].rearrange("p (g e) -> p g e", g=4), el[:, a].rearrange("p (g e) -> p g e", g=4), bc(oh[:, a], 2, 8), ALU.mult)
            then(last)
            es = rt[:, 2, :, 0:8]
            then(nc.vector.tensor_reduce(es, prod.rearrange("p a (g e) -> p a e g", g=4), AX.X, ALU.add))
            then(nc.vector.tensor_reduce(col[0], es, AX.X, ALU.max))
            nc.vector.tensor_tensor(es, es, over(col[0], 8), ALU.subtract).then_inc(rt_in, 1)
            dve.wait_ge(rt_exp, 2)
            then(nc.vector.tensor_reduce(col[0], es, AX.X, ALU.add))
            then(nc.vector.reciprocal(col[0], col[0]))
            then(nc.vector.tensor_tensor(es, es, over(col[0], 8), ALU.mult))
            then(nc.vector.tensor_reduce(col[2], es, AX.X, ALU.max))
            o1, o2 = rt[:, 3, :, 8:16], rt[:, 3, :, 16:24]
            first_of(o1, es, col[2], 8, rt[:, 3, :, 0:8])
            then(nc.vector.scalar_tensor_tensor(out=es, in0=o1, scalar=-2.0, in1=es, op0=ALU.mult, op1=ALU.add))
            then(nc.vector.tensor_reduce(col[3], es, AX.X, ALU.max))
            first_of(o2, es, col[3], 8, rt[:, 3, :, 0:8])
            both = rt[:, 2, :, 8:16]
            then(nc.vector.tensor_tensor(both, o1, o2, ALU.add))
            for a in range(TT):
                last = nc.vector.tensor_tensor(member[:, a].rearrange("p (g e) -> p g e", g=4), bc(oh[:, a], 2, 8), bc(both[:, a], 1, 4), ALU.mult)
            then(last)
            then(nc.vector.tensor_scalar(later, mask[:], 0.0, None, ALU.is_lt))
            nc.vector.memset(nw[:, 2, 6:7], 0.0).then_inc(comb_ready, 1)
            then(nc.vector.tensor_tensor(col[4], col[2], col[3], ALU.add))
            then(nc.vector.reciprocal(col[4], col[4]))
            then(nc.vector.tensor_tensor(col[4], col[4], col[1], ALU.mult))
            then(nc.vector.tensor_tensor(o1, o1, over(col[2], 8), ALU.mult))
            then(nc.vector.tensor_tensor(o2, o2, over(col[3], 8), ALU.mult))
            then(nc.vector.tensor_tensor(o1, o1, o2, ALU.add))
            then(nc.vector.tensor_tensor(o1, o1, over(col[4], 8), ALU.mult))
            for a in range(TT):
                last = nc.vector.tensor_tensor(comb[:, a].rearrange("p (g e) -> p g e", g=4), bc(oh[:, a], 2, 8), bc(o1[:, a], 1, 4), ALU.mult)
            last.then_inc(comb_ready, 1)

            dve.wait_ge(pos_done, 1)
            then(nc.vector.scalar_tensor_tensor(out=pos, in0=ps[:, 7, 0:64].rearrange("p (a e) -> p a e", a=TT), scalar=1e4, in1=member, op0=ALU.add, op1=ALU.mult))
            then(nc.vector.tensor_reduce(most, ps[:, 7, 64:96], AX.X, ALU.max))
            nc.vector.tensor_scalar(pos, pos, -1e4, None, ALU.add).then_inc(pos_ready, 1)
            nc.vector.tensor_scalar(more[:], most[0:1], float(CAP), None, ALU.is_gt).then_inc(more_ready, 1)
            dve.wait_ge(slots_in, 48)
            dve.wait_ge(pos_ready, 1)

            def moe_round(r):
                def pick_tokens(p, i=None):
                    plus = moe_counts(r, i)
                    if p >= 2:
                        dve.wait_ge(gathered, plus(4 * (p - 1), 4 * PAIRS, 8))
                    at = pos[:, :, 2 * p:2 * p + 2] if i is None else pos[:, :, bass.ds(i * 4 + 2 * p, 2)]
                    ids = slot_ids.unsqueeze(1).unsqueeze(1).broadcast_to([P, TT, 2, CAP])
                    nc.vector.tensor_tensor(picks[:, :, p % 2], ids, bc(at, 3, CAP), ALU.is_equal).then_inc(picked, 1)

                def place_slots(p, i=None):
                    plus, q = moe_counts(r, i), p % 2
                    dve.wait_ge(rows_in[q], plus(32 * (p // 2 + 1), 16 * PAIRS, 32))
                    if p >= 2:
                        dve.wait_ge(scattered[1], plus(p - 1, PAIRS, 2))
                    nc.vector.tensor_scalar(place[q], slot_rows[:, q, 0, :].rearrange("p (a t) -> p a t", a=TT), slot_id, None, ALU.is_equal)
                    nc.vector.scalar_tensor_tensor(out=placed[:, q, :], in0=slot_rows[:, q, 0, :], scalar=slot_id, in1=slot_rows[:, q, 1, :], op0=ALU.is_equal, op1=ALU.mult, accum_out=w_slot[:, q:q + 1]).then_inc(put_ready, 1)

                def y_low(d, h, i=None):
                    dve.wait_ge(y_hid[h], moe_counts(r, i)(d + 1, PAIRS, 2))
                    nc.vector.tensor_tensor(y_lo, ps[:, Y_BANKS[h], :], y_hi.bitcast(F32), ALU.subtract).then_inc(y_lod[h], 1)

                def step(p, i=None):
                    plus, j, q = moe_counts(r, i), first_unit(p), p % 2
                    if 1 <= p < PAIRS - 1:
                        pick_tokens(p + 1, i)
                    lo_e(j + 2, r, i)
                    place_slots(p, i)
                    lo_e(j + 3, r, i)
                    dve.wait_ge(th_done, plus(p + 1, PAIRS, 2))
                    nc.vector.scalar_tensor_tensor(out=eg[:, q, :], in0=eg[:, q, :], scalar=1.0, in1=ps[:, 6, 0:T], op0=ALU.add, op1=ALU.mult).then_inc(g_out, 1)
                    lo_e(j + 4, r, i)
                    dve.wait_ge(put_ready, plus(p + 1, PAIRS, 2))
                    dve.wait_ge(unit_done, plus(E0 + j + 4 + SPLIT_CREDIT, ROUND_UNITS, 12))
                    dve.wait_ge(g_out, plus(p + 1, PAIRS, 2))
                    nc.vector.scalar_tensor_tensor(out=he[:, q, :], in0=eg[:, q, :], scalar=w_slot[:, q:q + 1], in1=ps[:, 5, 0:T], op0=ALU.mult, op1=ALU.mult).then_inc(he_ready, 1)
                    lo_e(j + 5, r, i)
                    if p >= 1:
                        y_low(p - 1, 0, i)
                        lo_e(j + 6, r, i)
                    dve.wait_ge(heT_hid, plus(p + 1, PAIRS, 2))
                    nc.vector.tensor_tensor(heT_lo[:, :, 0:3:2, :], ps[:, 6, 0:2 * P].rearrange("p (c e s) -> p c e s", c=2, e=2), heT_hi[:, :, 0:3:2, :].bitcast(F32), ALU.subtract).then_inc(heT_lod, 1)
                    if p >= 1:
                        y_low(p - 1, 1, i)
                        lo_e(j + 7, r, i)

                if r is not None:
                    nc.vector.tensor_scalar(slot_ids, slot_ids, float(CAP), None, ALU.add).then_inc(shifted, 1)
                    nc.vector.tensor_scalar(slot_id, slot_id, float(CAP), None, ALU.add).then_inc(shifted, 1)
                    dve.wait_ge(shifted, r * 2 + 2)
                pick_tokens(0)
                pick_tokens(1)
                lo_e(0, r)
                lo_e(1, r)
                moe_steps(dve, step)
                y_low(PAIRS - 1, 0)
                y_low(PAIRS - 1, 1)
                plus = moe_counts(r, None)
                for h in range(2):
                    dve.wait_ge(scattered[h], plus(PAIRS, PAIRS, 2))
                    for a in range(TT):
                        cols = slice(h * BANK, (h + 1) * BANK)
                        last = nc.vector.tensor_tensor(x_nat[:, a, cols], x_nat[:, a, cols], ps[:, ACC + 2 * a + h, :], ALU.add)
                last.then_inc(summed, 1)
                dve.wait_ge(summed, plus(1, 1, 0))

            moe_round(None)
            with dve.If(dve.value_load(more[0:1, 0:1]) > 0):
                with dve.Fori(0, ROUNDS - 1) as r:
                    moe_round(r)
            nc.vector.memset(nw[:, 2, 7:8], 0.0).then_inc(x_out, 1)
            rms_rows(2, x_nat, lnb[:, 0, :])

        @block.tensor
        def _(pe):
            def mm3(out_, left, right, start, stop):
                nc.tensor.matmul(out_, left[1], right[0], start=start, stop=False)
                nc.tensor.matmul(out_, left[0], right[1], start=False, stop=False)
                return nc.tensor.matmul(out_, left[0], right[0], start=False, stop=stop)

            def weights(u, k, n):
                return unit3(w_hi, u % SPLIT, k, n), unit3(w_lo, u % SPLIT, k, n)

            def transposed(u, bank, xT, ready=None, between=None):
                w = weights(u, KC, 256)
                for c in range(2):
                    if between is not None and c == 1:
                        between()
                    for k in range(KC):
                        if ready is not None and c == 0 and k % 2 == 0:
                            pe.wait_ge(xT_lod, ready + (k // 2 + 1))
                        cols = slice(c * P, (c + 1) * P)
                        last = mm3(ps[:, bank, c * T:(c + 1) * T], [x[:, k, cols] for x in w], [x[:, k, :] for x in xT], k == 0, k == KC - 1)
                last.then_inc(unit_done, 1)

            def natural(u, bank, xT, between=None):
                w = weights(u, KC, 256)
                for a in range(TT):
                    if between is not None and a == 1:
                        between()
                    for k in range(KC):
                        last = mm3(ps[:, bank, a * 256:(a + 1) * 256], [x[:, k, a * P:(a + 1) * P] for x in xT], [x[:, k, :] for x in w], k == 0, k == KC - 1)
                last.then_inc(unit_done, 1)

            def rows_unit(u, left, start, stop, ready=None):
                w = weights(u, 2, D)
                for a in range(TT):
                    for k in range(2):
                        for h in range(2):
                            last = mm3(ps[:, ACC + 2 * a + h, :], [x[:, k, a * P:(a + 1) * P] for x in left],
                                       [x[:, k, h * BANK:(h + 1) * BANK] for x in w], start and k == 0, stop and k == 1)
                    if stop and a == 0:
                        last.then_inc(tile_done, 1)
                last.then_inc(unit_done, 1)

            pe.sem_inc(unit_done, SPLIT_CREDIT)
            pe.wait_ge(const_in, CONSTS)
            for i in range(LAYERS):
                nc.tensor.transpose(ps[:, 7, i * 256:i * 256 + C_CW], row_v[:, i, :], ident[0:C_CW, 0:C_CW])
                last = nc.tensor.transpose(ps[:, 7, i * 256 + C_CW:i * 256 + C_ALL], row_cw[:, i, :], ident[0:CONV_W * CC, 0:CONV_W * CC])
            last.then_inc(rows_T, 1)
            nc.tensor.matmul(ps[0:N_HEADS, 6, :], relb, t5, start=True, stop=True).then_inc(t5_mm, 1)
            pe.wait_ge(setup_p, 2)
            pe.wait_ge(x_in, 16)
            pe.wait_ge(prm_ready, 1)
            pe.sem_inc(x_out, 1)

            xT = (xT_hi, xT_lo)
            with pe.Fori(0, LAYERS) as l:
                base = l * UNITS

                def ready(u):
                    pe.wait_ge(split_done, base + u + 1 + RAW_CREDIT)

                def make_xT(k):
                    for a in range(TT):
                        if k == 1:
                            pe.wait_ge(x_out, l * 2 * TT + a + 1 + 1)
                        elif a == 0:
                            pe.wait_ge(x_out, l * 2 * TT + 1)
                        for c in range(KC):
                            last = nc.tensor.transpose(ps[:, ACC + c // 2, (c % 2) * T + a * P:(c % 2) * T + (a + 1) * P], x_nat[:, a, c * P:(c + 1) * P], ident[:])
                            if a == TT - 1 and c % 2 == 1:
                                last.then_inc(xT_done, 1)

                def scores(s):
                    pe.wait_ge(qk_copied, l * 8 + (4 if s < 8 else 8))
                    if s >= 1:
                        pe.wait_ge(exp_done, l * TASKS + s)
                    kind, c, a = 2 * (s // 8), (s % 8) // 2, s % 2
                    nk = P * (a + 1)
                    for i in range(2):
                        part = slice(i * HD, (i + 1) * HD)
                        last = nc.tensor.matmul(ps[:, i, 0:nk], qkT[part, kind, c, a * P:(a + 1) * P], qkT[part, kind + 1, c, 0:nk], start=True, stop=True)
                    last.then_inc(score_done, 1)

                def prob_transposes(s):
                    pe.wait_ge(prob_done, l * TASKS + s + 1)
                    if s >= 1:
                        pe.wait_ge(probT_copied, l * TASKS + s)
                    for i in range(1 if s < 8 else 2):
                        for b in range(s % 2 + 1):
                            last = nc.tensor.transpose(ps[:, PT_B, (2 * i + b) * P:(2 * i + b + 1) * P], E[:, s % 2, i, b * P:(b + 1) * P], ident[:])
                    last.then_inc(probT_done, 1)

                def values(s):
                    a, h = s % 2, (s % 8) // 2
                    pe.wait_ge(probT_copied, l * TASKS + s + 1)
                    pe.wait_ge(evac_a, l * EV_A + evac_before((U_V[1] if s < 8 else U_V[3]) + 1)[0])
                    if 1 <= s < 9:
                        pe.wait_ge(pv_copied, l * TASKS + s)
                    elif s >= 9:
                        pe.wait_ge(moba_lo, l * 8 + s - 8)
                    cols = slice(0, P)
                    for i in range(1 if s < 8 else 2):
                        for b in range(a + 1):
                            p = pT[:, (2 * i + b) * P:(2 * i + b + 1) * P]
                            if s < 8:
                                last = nc.tensor.matmul(ps[:, O_B, cols], p, vv[:, 0, b, h * P:(h + 1) * P], start=b == 0, stop=b == a)
                            else:
                                last = nc.tensor.matmul(ps[i * HD:(i + 1) * HD, O_B, cols], vv[:, 1, b, (2 * h + i) * HD:(2 * h + i + 1) * HD], p, start=b == 0, stop=b == a)
                    last.then_inc(pv_done, 1)

                make_xT(0)
                for u in range(U_BR):
                    ready(u)
                    if u >= 3:
                        v = u - 3
                        if v in U_QK:
                            pe.wait_ge(rotated, l * 8 + U_QK.index(v) + 1)
                        else:
                            pe.wait_ge(evac_a, l * EV_A + evac_before(v + 1)[0])
                    if u in U_QK or u in U_V:
                        natural(u, UB + u % 3, xT)
                    else:
                        transposed(u, UB + u % 3, xT, l * 8 if u == 0 else None)
                    if u - 2 in U_QK:
                        n = U_QK.index(u - 2)
                        pe.wait_ge(roped, l * 8 + n + 1)
                        if n >= 1:
                            pe.wait_ge(qk_copied, l * 8 + n)
                        for c in range(2):
                            for a in range(TT):
                                last = nc.tensor.transpose(ps[:, TB, c * T + a * P:c * T + (a + 1) * P], rope[:, n % 2, a * 256 + c * P:a * 256 + (c + 1) * P], ident[:])
                        last.then_inc(qk_T, 1)
                    if 0 <= u - 10 < TASKS:
                        scores(u - 10)
                    if 0 <= u - 12 < TASKS:
                        prob_transposes(u - 12)
                    if 0 <= u - 13 < TASKS:
                        values(u - 13)
                    if u == 19:
                        pe.wait_ge(conv_link, (l + 1) * CONV_W * CC)
                        pe.wait_ge(qk_copied, l * 8 + 8)
                        for c in range(CC):
                            last = nc.tensor.matmul(ps[:, TB, 0:T], ones[:], cv[:, c, :], start=c == 0, stop=c == CC - 1)
                        last.then_inc(csum_done, 1)
                    if u == 20:
                        pe.wait_ge(c_sq, l + 1)
                        for c in range(CC):
                            last = nc.tensor.matmul(ps[:, TB, T:2 * T], ones[:], hpad[:, c, PAD:], start=c == 0, stop=c == CC - 1)
                        last.then_inc(csum_done, 1)
                    if u in (24, 25):
                        r = u - 24
                        pe.wait_ge(o_normed, l + 1)
                        if r == 0:
                            pe.wait_ge(c_norm, l + 1)
                        else:
                            pe.wait_ge(oT_lod, l * 2 + 1)
                        for c in range(2):
                            for a in range(TT):
                                last = nc.tensor.transpose(ps[:, TB, c * T + a * P:c * T + (a + 1) * P], o_nat[:, a, 2 * r + c, :], ident[:])
                        last.then_inc(oT_done, 1)
                values(TASKS - 1)

                for c in range(KC):
                    u = U_BR + c
                    ready(u)
                    w = weights(u, 12, P)
                    b0 = 4 + 2 * (c % 2)
                    if c == 0:
                        pe.wait_ge(evac_a, l * EV_A + EV_A_IN)
                        pe.wait_ge(oT_lod, l * 2 + 2)
                    if c >= 2:
                        pe.wait_ge(evac_d, l * KC + c - 1)
                    for b in range(3):
                        if c == 0:
                            pe.wait_ge(*((c_lo, l + 1), (oT_lod, l * 2 + 2), (moba_lo, l * 8 + 8))[b])
                        o = ps[:, b0 + b // 2, (b % 2) * T:(b % 2 + 1) * T]
                        for k in range(CC):
                            last = mm3(o, [x[:, b * CC + k, :] for x in w], [x[:, b, k, :] for x in (br_hi, br_lo)], k == 0, k == CC - 1)
                    last.then_inc(unit_done, 1)
                for k in range(4):
                    ready(U_WO + k)
                    pe.wait_ge(m_lo, l * KC + 2 * k + 2)
                    rows_unit(U_WO + k, [x[:, 2 * k:2 * k + 2, :] for x in xT], k == 0, k == 3)
                make_xT(1)

                def ff2(j, u, i=0, jj=None, start=False, stop=False):
                    pe.wait_ge(split_done, base + i * 4 + (u + 1 + RAW_CREDIT))
                    pe.wait_ge(ff_lo, l * FFJ + jj + 1)
                    rows_unit(u, (h_hi[:, j], h_lo[:, j]), start, stop)

                for j in range(2):
                    ready(U_FF + j)
                    transposed(U_FF + j, 4 + j, xT, l * 8 + 4 if j == 0 else None)
                ff2(0, U_FF + 2, 0, 0, start=True)
                with pe.Fori(0, FFJ // 2 - 1) as i:
                    for q in range(2):
                        u = U_FF + 3 + 2 * q
                        pe.wait_ge(split_done, base + i * 4 + (u + 1 + RAW_CREDIT))
                        pe.wait_ge(evac_a, l * EV_A + i * 2 + (EV_A_IN + q + 1))
                        transposed(u, 4 + q, xT)
                        ff2(1 - q, u + 1, i, i * 2 + (1 + q))
                ff2(1, UNITS - 1, 0, FFJ - 1, stop=True)

            def ready2(u, i=None):
                pe.wait_ge(split_done, u + 1 + RAW_CREDIT if i is None else i * 12 + (u + 1 + RAW_CREDIT))

            def make_xT2(k):
                for a in range(TT):
                    pe.wait_ge(normed, k * TT + a + 1)
                    for c in range(KC):
                        last = nc.tensor.transpose(ps[:, ACC + c // 2, (c % 2) * T + a * P:(c % 2) * T + (a + 1) * P], hn[:, a, c * P:(c + 1) * P], ident[:])
                        if a == TT - 1 and c % 2 == 1:
                            last.then_inc(xT_done, 1)

            def bank_free(w):
                if w >= 3:
                    pe.wait_ge(ev2, w - 2)

            make_xT2(0)
            def small(w, half):
                n = 2 * (w - X_IX) + half
                if 0 <= n < 8:
                    a, p = n // 4, n % 4
                    nk = P * (a + 1)
                    pe.wait_ge(kvT_c, 1)
                    pe.wait_ge(wsT_c, 1)
                    if n >= 2:
                        pe.wait_ge(ix_rel, n - 1)
                    for i in range(2):
                        part = slice(i * HD, (i + 1) * HD)
                        last = nc.tensor.matmul(ps[:, 2 * (n % 2) + i, 0:nk], qiT[part, p, a * P:(a + 1) * P], kiT[part, 0:nk], start=True, stop=True)
                    last.then_inc(ix_done, 1)
                n = 2 * (w - X_QL) + half
                if 0 <= n < 4:
                    pe.wait_ge(ev2, W_Q + 2)
                    pe.wait_ge(ix_rel, 8)
                    if n >= 1:
                        pe.wait_ge(ql_c, n)
                    for i in range(2):
                        part = slice(i * HD, (i + 1) * HD)
                        last = nc.tensor.matmul(ps[:, O_B + i, 0:T], w_ukT[part, n, :], q2T[part, n, :], start=True, stop=True)
                    last.then_inc(ql_done, 1)
                for kind, s in latent_steps(w, half):
                    latent_pe(pe, kind, s)
                s = latent_task(w, half)
                if s is not None:
                    a, p = s // 4, s % 4
                    nk = P * (a + 1)
                    if s < 2:
                        pe.wait_ge(ix_rel, 8)
                    else:
                        pe.wait_ge(s2_max, s - 1)
                    for i in range(2):
                        last = nc.tensor.matmul(ps[:, s % 2, i * T:i * T + nk], q_latT[:, 2 * p + i, a * P:(a + 1) * P], ckvT[:, 0:nk], start=True, stop=True)
                    last.then_inc(s2_done, 1)

            for w in range(W_PB):
                u = G2 + w
                ready2(u)
                bank_free(w)
                if w == W_K:
                    k_w = weights(u, KC, K_COLS)
                    for a in range(TT):
                        for k in range(KC):
                            last = mm3(ps[:, UB + w % 3, a * 256:a * 256 + K_COLS], [x[:, k, a * P:(a + 1) * P] for x in xT], [x[:, k, :] for x in k_w], k == 0, k == KC - 1)
                    last.then_inc(unit_done, 1)
                elif W_V <= w < W_GA:
                    natural(u, UB + w % 3, xT, lambda: small(w, 0))
                else:
                    transposed(u, UB + w % 3, xT, LAYERS * 8 if w == 0 else None, lambda: small(w, 0))
                small(w, 1)
                if w == 0:
                    pe.wait_ge(late3_in, 32)
                    for c in range(4):
                        last = nc.tensor.transpose(ps[:, TB, c * P:(c + 1) * P], w_uk[:, c * P:(c + 1) * P], ident[:])
                    last.then_inc(ukT_done, 1)
                    pe.wait_ge(ws_masked, 1)
                    for g in range(4):
                        last = nc.tensor.transpose(ps[:, O_B, g * P:(g + 1) * P], ws_nat[:, g, :], ident[:])
                    last.then_inc(wsT_done, 1)
                if w == W_K + 1:
                    pe.wait_ge(kv_normed, 1)
                    pe.wait_ge(ukT_c, 1)
                    for a in range(TT):
                        nc.tensor.transpose(ps[:, TB, a * P:(a + 1) * P], ckv[:, a, :], ident[:])
                        last = nc.tensor.transpose(ps[:, TB, T + a * P:T + (a + 1) * P], ki2[:, a].rearrange("p i d -> p (i d)"), ident[:])
                    last.then_inc(kvT_done, 1)
                if w == X_SP:
                    pe.wait_ge(lnv_out, 1)
                    pe.wait_ge(ql_c, 4)
                    for a in range(TT):
                        for g in range(4):
                            cols = slice(g * P, (g + 1) * P)
                            last = nc.tensor.matmul(ps[:, (TB, O_B)[a], cols], wsT[:, g, :], vg[:, a, cols], start=True, stop=True)
                        last.then_inc(sp_done, 1)
                if w in (X_YB, X_YB + 1):
                    r = w - X_YB
                    pe.wait_ge(sp_out, TT)
                    if r == 1:
                        pe.wait_ge(yb_lo, 1)
                    for c in range(2):
                        for a in range(TT):
                            last = nc.tensor.transpose(ps[:, TB, c * T + a * P:c * T + (a + 1) * P], ug[:, a, (2 * r + c) * P:(2 * r + c + 1) * P], ident[:])
                    last.then_inc(ybT_done, 1)
            for w in range(W_PB, W_OUT):
                u = G2 + w
                ready2(u)
                j = (w - W_PB) % 2
                if w < W_PA:
                    pe.wait_ge(ev2, W_PB)
                    pe.wait_ge(yb_lo, 2)
                    pe.wait_ge(a2_lo, 8)
                else:
                    pe.wait_ge(proj_b, j + 1)
                w_u = weights(u, CC, 512)
                b = 1 if w < W_PA else 0
                for c in range(4):
                    for k in range(CC):
                        last = mm3(ps[:, PROJ_BANKS[j][c // 2], (c % 2) * T:(c % 2 + 1) * T], [x[:, k, c * P:(c + 1) * P] for x in w_u],
                                   [x[:, b, k, :] for x in (br_hi, br_lo)], k == 0, k == CC - 1)
                last.then_inc(unit_done, 1)
            for k in range(4):
                u = G2 + W_OUT + k
                ready2(u)
                pe.wait_ge(pm_lo, k // 2 + 1)
                rows_unit(u, [x[:, 2 * k:2 * k + 2, :] for x in xT], k == 0, k == 3)
            make_xT2(1)
            u = G2 + W_R
            ready2(u)
            pe.wait_ge(xT_lod, LAYERS * 8 + 8)
            r_w = weights(u, KC, 36)
            for k in range(KC):
                last = mm3(ps[0:36, 7, 0:T], [x[:, k, :] for x in r_w], [x[:, k, :] for x in xT], k == 0, k == KC - 1)
            last.then_inc(unit_done, 1)
            pe.wait_ge(rt_copied, 1)
            for a in range(TT):
                last = nc.tensor.transpose(ps[:, 5, a * 36:(a + 1) * 36], rtT[:, a * P:(a + 1) * P], ident[0:36, 0:36])
            last.then_inc(rt_back, 1)

            pe.wait_ge(comb_ready, 1)
            for a in range(TT):
                for b in range(a + 1):
                    nc.tensor.matmul(ps[:, 7, a * 32:(a + 1) * 32], later if a == b else ones[:], member[:, b, :], start=b == 0, stop=b == a)
            for a in range(TT):
                last = nc.tensor.matmul(ps[:, 7, 64:96], ones[:], member[:, a, :], start=a == 0, stop=a == TT - 1)
            last.then_inc(pos_done, 1)
            pe.wait_ge(pos_ready, 1)
            for k, x in enumerate((pos, comb)):
                for a in range(TT):
                    last = nc.tensor.transpose(ps[0:32, 6, k * T + a * P:k * T + (a + 1) * P], x[:, a, :], ident[:])
            last.then_inc(rowsT_done, 1)
            pe.wait_ge(h2_lod, 1)
            pe.wait_ge(zeroed, 1)

            def moe_round(r):
                def halves(j, i, body):
                    plus, u = moe_counts(r, i), E0 + j
                    pe.wait_ge(lo_half, plus(j + 1, ROUND_UNITS, 12))
                    body(0, u)
                    pe.wait_ge(split_done, plus(u + 1 + RAW_CREDIT, ROUND_UNITS, 12))
                    body(1, u).then_inc(unit_done, 1)

                def gather(p, g, i=None):
                    plus, q = moe_counts(r, i), p % 2
                    if g == 0:
                        pe.wait_ge(picked, plus(p + 1, PAIRS, 2))
                    bank = (4, 5)[g % 2] if p == 0 else 4
                    if p == 0 and g >= 2:
                        pe.wait_ge(gath_c, plus(g - 1, 4 * PAIRS, 8))
                    elif p >= 1:
                        pe.wait_ge(gath_c, plus(4 * p + g, 4 * PAIRS, 8))
                    for m in range(4):
                        c, x = 2 * g + m // 2, (h2_hi, h2_lo)[m % 2]
                        for a in range(TT):
                            last = nc.tensor.matmul(ps[:, bank, m * P:(m + 1) * P], x[:, a, c * P:(c + 1) * P], picks[:, a, q], start=a == 0, stop=a == TT - 1)
                    last.then_inc(gathered, 1)

                def inner(p, kind, e, i):
                    plus = moe_counts(r, i)
                    slots = slice(e * CAP, e * CAP + P)

                    def body(half, u):
                        w = weights(u, KC, 256)
                        for k in range(4 * half, 4 * half + 4):
                            if kind == 0 and e == 0 and k % 2 == 0:
                                pe.wait_ge(gath_c, plus(4 * p + k // 2 + 1, 4 * PAIRS, 8))
                            last = mm3(ps[:, 6 - kind, 0:256], [x[:, k, slots] for x in (xg_hi, xg_lo)], [x[:, k, :] for x in w], e == 0 and k == 0, e == 1 and k == KC - 1)
                        return last

                    halves(first_unit(p) + 2 * kind + e, i, body)

                def outer(d, h, i=None):
                    def body(e, u):
                        w = weights(u, 4, BANK)
                        for c in range(2):
                            last = mm3(ps[:, Y_BANKS[h], :], [x[:, c, e:e + 2, :] for x in (heT_hi, heT_lo)], [x[:, 2 * e + c, :] for x in w], e == 0 and c == 0, e == 1 and c == 1)
                        return last

                    halves(down_unit(d, h), i, body)

                def scatter(d, h, i=None):
                    pe.wait_ge(y_lod[h], moe_counts(r, i)(d + 1, PAIRS, 2))
                    for a in range(TT):
                        for k, y in enumerate((y_lo, y_hi)):
                            last = nc.tensor.matmul(ps[:, ACC + 2 * a + h, :], place[d % 2][:, a, :], y, start=d == 0 and k == 0, stop=d == PAIRS - 1 and k == 1)
                    last.then_inc(scattered[h], 1)

                def step(p, i=None):
                    plus, q = moe_counts(r, i), p % 2
                    if p >= 1:
                        pe.wait_ge(heT_lod, plus(p, PAIRS, 2))
                    inner(p, 0, 0, i)
                    if p >= 2:
                        scatter(p - 2, 1, i)
                    inner(p, 0, 1, i)
                    if p >= 2:
                        pe.wait_ge(y_lod[1], plus(p - 1, PAIRS, 2))
                    inner(p, 1, 0, i)
                    inner(p, 1, 1, i)
                    if p < PAIRS - 1:
                        gather(p + 1, 0, i)
                    if p >= 2:
                        pe.wait_ge(y_lod[0], plus(p - 1, PAIRS, 2))
                    if p >= 1:
                        outer(p - 1, 0, i)
                    if p < PAIRS - 1:
                        gather(p + 1, 1, i)
                    pe.wait_ge(he_ready, plus(p + 1, PAIRS, 2))
                    if p >= 1:
                        outer(p - 1, 1, i)
                    if p < PAIRS - 1:
                        gather(p + 1, 2, i)
                    for c in range(2):
                        last = nc.tensor.transpose(ps[:, 6, c * P:(c + 1) * P], he[:, q, c * P:(c + 1) * P], ident[:])
                    last.then_inc(heT_done, 1)
                    if p >= 1:
                        scatter(p - 1, 0, i)
                    if p < PAIRS - 1:
                        gather(p + 1, 3, i)

                if r is not None:
                    pe.wait_ge(summed, r + 1)
                for g in range(4):
                    gather(0, g)
                pe.wait_ge(rowsT_c, 1)
                moe_steps(pe, step)
                scatter(PAIRS - 2, 1)
                plus = moe_counts(r, None)
                pe.wait_ge(heT_lod, plus(PAIRS, PAIRS, 2))
                outer(PAIRS - 1, 0)
                outer(PAIRS - 1, 1)
                scatter(PAIRS - 1, 0)
                scatter(PAIRS - 1, 1)

            moe_round(None)
            pe.wait_ge(more_ready, 1)
            with pe.If(pe.value_load(more[0:1, 0:1]) > 0):
                with pe.Fori(0, ROUNDS - 1) as r:
                    moe_round(r)


_OUT = ((1, T, D), "float32")


def constants():
    inv = np.float32(10000.0) ** (-np.arange(0, HD, 2, dtype=np.float32) / np.float32(HD))
    ang = np.arange(T, dtype=np.float32)[:, None] * inv[None, :].astype(np.float32)
    ang = np.concatenate([ang, ang], axis=-1)
    cos, sin = np.cos(ang), np.sin(ang)
    sin = np.concatenate([-sin[:, :HD // 2], sin[:, HD // 2:]], axis=-1)
    scale = np.float32(HD ** -0.5)
    lam = np.array([0.8 - 0.6 * math.exp(-0.3 * i) for i in range(LAYERS)])
    n = 255 - np.arange(512)
    nf = np.maximum(n, 1).astype(np.float32)
    large = 16 + (np.log(nf / np.float32(16)) / np.float32(np.log(128 / 16)) * np.float32(16)).astype(np.int32)
    bucket = np.where(n < 16, n, np.minimum(large, 31))
    t5 = (np.arange(32)[:, None] == bucket[None, :]) & (n >= 0)[None, :]
    keep = np.arange(P)[None, :] <= np.arange(P)[:, None]
    return {
        "c_ident": np.eye(P, dtype=np.float32),
        "c_mask": np.where(keep, 0.0, NEG).astype(np.float32),
        "c_rot": np.stack([cos * scale, sin * scale, cos, sin]).astype(np.float32),
        "c_slots": np.arange(CAP, dtype=np.float32),
        "c_t5": t5.astype(np.float32),
        "c_lam": np.stack([lam, 1.0 - lam]).astype(np.float32),
    }


def kernel(**inputs):
    import concourse.bacc as bacc
    from concourse.bass_utils import run_bass_kernel_spmd

    nc = bacc.Bacc("TRN2", target_bir_lowering=False, num_devices=1)
    arrays = {"in_" + n: np.ascontiguousarray(a) for n, a in {**inputs, **constants()}.items()}
    aps = {n[3:]: nc.dram_tensor(n, a.shape, mybir.dt.from_np(a.dtype), kind="ExternalInput").ap() for n, a in arrays.items()}
    out = nc.dram_tensor("out_0", _OUT[0], F32, kind="ExternalOutput").ap()
    build(nc, aps, out)
    return run_bass_kernel_spmd(nc, [arrays], core_ids=[0]).results[0]["out_0"]
```
